# Optimizing a Trainium2 kernel written in Bass

```python
import math
import jax, jax.numpy as jnp
from jax import lax
import numpy as np

D_MODEL = 1024
BATCH = 1
SEQ = 512
DEPTH = 2

GRID_W = 64
EPS = 1e-6
ROPE_THETA = 10000.0
BLOCK = 128
A_HEADS = 4
A_DK = 128
A_DV = 128
A_CONV = 5
A_CHUNK = 64
A_CONV_CH = 2 * A_HEADS * A_DK + A_HEADS * A_DV
HD = 64
B_HEADS = 4
B_KV = 2
WINDOW = 128
C_HEADS = 4
C_KV = 2
PROJ_SIZES = (A_CONV_CH, A_HEADS * A_DV, 2 * A_HEADS, 2 * A_HEADS,
              B_HEADS * HD, B_KV * HD, B_KV * HD,
              C_HEADS * HD, C_KV * HD, C_KV * HD)
PROJ_DIM = 3088
MIX_WIDTH = A_HEADS * A_DV + B_HEADS * HD + C_HEADS * HD
N_EXPERTS = 16
CAP_FACTOR = 2
D_EXPERT = 1024

kernel_name = "hybrid_parallel_heads_ec_moe_encoder"

def rmsnorm(x, g):
    xf = x.astype(jnp.float32)
    y = xf * lax.rsqrt(jnp.mean(xf * xf, axis=-1, keepdims=True) + EPS)
    return (y * g.astype(jnp.float32)).astype(x.dtype)

def l2norm(x):
    xf = x.astype(jnp.float32)
    return xf * lax.rsqrt(jnp.sum(xf * xf, axis=-1, keepdims=True) + EPS)

def rope_tables(pos, dim):
    inv = ROPE_THETA ** (-jnp.arange(0, dim, 2, dtype=jnp.float32) / dim)
    ang = pos.astype(jnp.float32)[:, None] * inv[None, :]
    ang = jnp.concatenate([ang, ang], axis=-1)
    return jnp.cos(ang), jnp.sin(ang)

def apply_rope(x, cos, sin):
    xf = x.astype(jnp.float32)
    half = xf.shape[-1] // 2
    rot = jnp.concatenate([-xf[..., half:], xf[..., :half]], axis=-1)
    return (xf * cos[None, :, None, :] + rot * sin[None, :, None, :]).astype(x.dtype)

def apply_axial_rope(x, row_cs, col_cs):
    h = x.shape[-1] // 2
    return jnp.concatenate([apply_rope(x[..., :h], *row_cs),
                            apply_rope(x[..., h:], *col_cs)], axis=-1)

def short_conv(x, w):
    k = w.shape[0]
    return lax.conv_general_dilated(
        x, w[:, None, :].astype(x.dtype), window_strides=(1,),
        padding=[(k // 2, k // 2)], dimension_numbers=('NWC', 'WIO', 'NWC'),
        feature_group_count=x.shape[-1])

def delta_rule_chunked(q, k, v, g, beta):
    B, S, H, dk = q.shape
    dv = v.shape[-1]
    n = S // A_CHUNK

    def chunks(t):
        return t.reshape(B, n, A_CHUNK, H, -1).transpose(1, 0, 3, 2, 4)

    q, k, v = chunks(q), chunks(k), chunks(v)
    g = g.reshape(B, n, A_CHUNK, H).transpose(1, 0, 3, 2)
    beta = beta.reshape(B, n, A_CHUNK, H).transpose(1, 0, 3, 2)
    gc = jnp.cumsum(g, axis=-1)
    tril = jnp.tril(jnp.ones((A_CHUNK, A_CHUNK), bool))
    strict = jnp.tril(jnp.ones((A_CHUNK, A_CHUNK), bool), -1)
    decay = jnp.exp(jnp.where(tril, gc[..., :, None] - gc[..., None, :], -jnp.inf))
    k_beta = k * beta[..., None]
    v_beta = v * beta[..., None]
    lower = jnp.where(strict, jnp.einsum('nbhid,nbhjd->nbhij', k_beta, k) * decay, 0.0)
    eye = jnp.eye(A_CHUNK, dtype=jnp.float32)
    t_mat = lax.linalg.triangular_solve(eye + lower, jnp.broadcast_to(eye, lower.shape),
                                        left_side=True, lower=True, unit_diagonal=True)
    u = jnp.einsum('nbhij,nbhjd->nbhid', t_mat, v_beta)
    w = jnp.einsum('nbhij,nbhjd->nbhid', t_mat, k_beta * jnp.exp(gc)[..., None])
    a_intra = jnp.einsum('nbhid,nbhjd->nbhij', q, k) * decay

    def step(state, inp):
        q_i, k_i, u_i, w_i, a_i, gc_i = inp
        v_new = u_i - jnp.einsum('bhcd,bhde->bhce', w_i, state)
        o = (jnp.einsum('bhcd,bhde->bhce', q_i * jnp.exp(gc_i)[..., None], state)
             + jnp.einsum('bhij,bhje->bhie', a_i, v_new))
        g_last = gc_i[..., -1]
        k_dec = k_i * jnp.exp(g_last[..., None] - gc_i)[..., None]
        state = state * jnp.exp(g_last)[..., None, None] + jnp.einsum('bhcd,bhce->bhde', k_dec, v_new)
        return state, o

    init = jnp.zeros((B, H, dk, dv), jnp.float32)
    _, o = lax.scan(step, init, (q, k, u, w, a_intra, gc))
    return o.transpose(1, 0, 3, 2, 4).reshape(B, S, H, dv)

def gated_deltanet(qkv, z, b, a, conv_w, a_log, dt_bias, norm_g):
    B, S, _ = qkv.shape
    qkv = jax.nn.silu(short_conv(qkv, conv_w))
    q, k, v = jnp.split(qkv, [A_HEADS * A_DK, 2 * A_HEADS * A_DK], axis=-1)
    q = l2norm(q.reshape(B, S, A_HEADS, A_DK)) * (A_DK ** -0.5)
    k = l2norm(k.reshape(B, S, A_HEADS, A_DK))
    v = v.reshape(B, S, A_HEADS, A_DV).astype(jnp.float32)
    beta = jax.nn.sigmoid(b.astype(jnp.float32)).reshape(B, S, 2, A_HEADS)
    g = (-jnp.exp(a_log.astype(jnp.float32))[None, None]
         * jax.nn.softplus(a.astype(jnp.float32).reshape(B, S, 2, A_HEADS)
                           + dt_bias.astype(jnp.float32)[None, None]))
    o_fwd = delta_rule_chunked(q, k, v, g[:, :, 0], beta[:, :, 0])
    fl = lambda t: jnp.flip(t, axis=1)
    o_bwd = fl(delta_rule_chunked(fl(q), fl(k), fl(v), fl(g[:, :, 1]), fl(beta[:, :, 1])))
    o = rmsnorm(o_fwd + o_bwd, norm_g) * jax.nn.silu(z.astype(jnp.float32).reshape(B, S, A_HEADS, A_DV))
    return o.reshape(B, S, A_HEADS * A_DV).astype(qkv.dtype)

def window_attention(q, k, v, sink):
    B, S, hq, d = q.shape
    hkv = k.shape[2]
    grp = hq // hkv
    nb = S // BLOCK
    qb = q.reshape(B, nb, BLOCK, hkv, grp, d)
    pad = ((0, 0), (BLOCK, BLOCK), (0, 0), (0, 0))
    kp = jnp.pad(k, pad).reshape(B, nb + 2, BLOCK, hkv, d)
    vp = jnp.pad(v, pad).reshape(B, nb + 2, BLOCK, hkv, d)
    kn = jnp.concatenate([kp[:, :-2], kp[:, 1:-1], kp[:, 2:]], axis=2)
    vn = jnp.concatenate([vp[:, :-2], vp[:, 1:-1], vp[:, 2:]], axis=2)
    s = jnp.einsum('bnqhgd,bnkhd->bnhgqk', qb, kn).astype(jnp.float32) * (d ** -0.5)
    blk = jnp.arange(nb)[:, None]
    qpos = blk * BLOCK + jnp.arange(BLOCK)[None, :]
    kpos = (blk - 1) * BLOCK + jnp.arange(3 * BLOCK)[None, :]
    valid = ((jnp.abs(qpos[:, :, None] - kpos[:, None, :]) <= WINDOW)
             & (kpos >= 0)[:, None, :] & (kpos < S)[:, None, :])
    s = jnp.where(valid[None, :, None, None], s, -jnp.inf)
    sink_b = sink.astype(jnp.float32).reshape(hkv, grp)[None, None, :, :, None, None]
    m = jnp.maximum(jnp.max(s, axis=-1, keepdims=True), sink_b)
    p = jnp.exp(s - m)
    p = p / (jnp.sum(p, axis=-1, keepdims=True) + jnp.exp(sink_b - m))
    o = jnp.einsum('bnhgqk,bnkhd->bnqhgd', p.astype(v.dtype), vn)
    return o.reshape(B, S, hq * d)

def dense_attention(q, k, v):
    B, S, hq, d = q.shape
    hkv = k.shape[2]
    grp = hq // hkv
    nb = S // BLOCK
    qb = q.reshape(B, nb, BLOCK, hkv, grp, d).transpose(1, 0, 2, 3, 4, 5)

    def one_block(q_blk):
        s = jnp.einsum('bqhgd,bkhd->bhgqk', q_blk, k).astype(jnp.float32) * (d ** -0.5)
        p = jax.nn.softmax(s, axis=-1)
        return jnp.einsum('bhgqk,bkhd->bqhgd', p.astype(v.dtype), v)

    o = lax.map(one_block, qb)
    return o.transpose(1, 0, 2, 3, 4, 5).reshape(B, S, hq * d)

def expert_choice_ffn(h, w_router, w_gate, w_up, w_down):
    B, S, D = h.shape
    cap = CAP_FACTOR * S // N_EXPERTS
    aff = jax.nn.softmax(jnp.einsum('bsd,de->bse', h, w_router).astype(jnp.float32), axis=-1)
    gate, idx = lax.top_k(jnp.swapaxes(aff, 1, 2), cap)
    bidx = jnp.arange(B)[:, None, None]
    xs = h[bidx, idx]
    hid = (jax.nn.silu(jnp.einsum('becd,edf->becf', xs, w_gate))
           * jnp.einsum('becd,edf->becf', xs, w_up))
    y = jnp.einsum('becf,efd->becd', hid, w_down) * gate[..., None].astype(h.dtype)
    return jnp.zeros_like(h).at[bidx, idx].add(y)

def setup_inputs(seed: int = 0) -> dict:
    key = jax.random.key(seed)
    ks = jax.random.split(key, 20)
    f32 = jnp.float32

    def nrm(k, shape, scale):
        return jax.random.normal(k, shape, f32) * scale

    x = nrm(ks[0], (BATCH, SEQ, D_MODEL), 1.0)
    norm1_g = 1.0 + nrm(ks[1], (DEPTH, D_MODEL), 0.02)
    w_in = nrm(ks[2], (DEPTH, D_MODEL, PROJ_DIM), D_MODEL ** -0.5)
    conv_w = nrm(ks[3], (DEPTH, A_CONV, A_CONV_CH), A_CONV ** -0.5)
    a_log = jnp.log(jax.random.uniform(ks[4], (DEPTH, 2, A_HEADS), f32, 1.0, 16.0))
    dt = jnp.exp(jax.random.uniform(ks[5], (DEPTH, 2, A_HEADS), f32, math.log(1e-3), math.log(1e-1)))
    dt_bias = dt + jnp.log(-jnp.expm1(-dt))
    a_norm_g = 1.0 + nrm(ks[6], (DEPTH, A_DV), 0.02)
    b_qnorm_g = 1.0 + nrm(ks[7], (DEPTH, HD), 0.02)
    b_knorm_g = 1.0 + nrm(ks[8], (DEPTH, HD), 0.02)
    b_sink = nrm(ks[9], (DEPTH, B_HEADS), 0.5)
    c_qnorm_g = 1.0 + nrm(ks[10], (DEPTH, HD), 0.02)
    c_knorm_g = 1.0 + nrm(ks[11], (DEPTH, HD), 0.02)
    w_out = nrm(ks[12], (DEPTH, MIX_WIDTH, D_MODEL), MIX_WIDTH ** -0.5)
    norm2_g = 1.0 + nrm(ks[13], (DEPTH, D_MODEL), 0.02)
    w_router = nrm(ks[14], (DEPTH, D_MODEL, N_EXPERTS), D_MODEL ** -0.5)
    w_gate = nrm(ks[15], (DEPTH, N_EXPERTS, D_MODEL, D_EXPERT), D_MODEL ** -0.5)
    w_up = nrm(ks[16], (DEPTH, N_EXPERTS, D_MODEL, D_EXPERT), D_MODEL ** -0.5)
    w_down = nrm(ks[17], (DEPTH, N_EXPERTS, D_EXPERT, D_MODEL), D_EXPERT ** -0.5)
    return {"x": x, "norm1_g": norm1_g, "w_in": w_in, "conv_w": conv_w,
            "a_log": a_log, "dt_bias": dt_bias, "a_norm_g": a_norm_g,
            "b_qnorm_g": b_qnorm_g, "b_knorm_g": b_knorm_g, "b_sink": b_sink,
            "c_qnorm_g": c_qnorm_g, "c_knorm_g": c_knorm_g, "w_out": w_out,
            "norm2_g": norm2_g, "w_router": w_router, "w_gate": w_gate,
            "w_up": w_up, "w_down": w_down}

def reference(x, norm1_g, w_in, conv_w, a_log, dt_bias, a_norm_g, b_qnorm_g, b_knorm_g,
              b_sink, c_qnorm_g, c_knorm_g, w_out, norm2_g, w_router, w_gate, w_up, w_down):
    B, S, _ = x.shape
    n_rows = S // GRID_W
    pos = jnp.arange(S)
    row_ids = jnp.repeat(jnp.arange(n_rows), GRID_W)
    col_ids = jnp.tile(jnp.arange(GRID_W), n_rows)
    rope_1d = rope_tables(pos, HD)
    rope_row = rope_tables(row_ids, HD // 2)
    rope_col = rope_tables(col_ids, HD // 2)
    split_idx = [int(i) for i in np.cumsum(PROJ_SIZES)[:-1]]

    for l in range(DEPTH):
        h = rmsnorm(x, norm1_g[l])
        proj = jnp.einsum('bsd,dp->bsp', h, w_in[l])
        qkv_a, z_a, b_a, a_a, q_b, k_b, v_b, q_c, k_c, v_c = jnp.split(proj, split_idx, axis=-1)

        out_a = gated_deltanet(qkv_a, z_a, b_a, a_a, conv_w[l], a_log[l], dt_bias[l], a_norm_g[l])

        qb = apply_rope(rmsnorm(q_b.reshape(B, S, B_HEADS, HD), b_qnorm_g[l]), *rope_1d)
        kb = apply_rope(rmsnorm(k_b.reshape(B, S, B_KV, HD), b_knorm_g[l]), *rope_1d)
        out_b = window_attention(qb, kb, v_b.reshape(B, S, B_KV, HD), b_sink[l])

        qc = apply_axial_rope(rmsnorm(q_c.reshape(B, S, C_HEADS, HD), c_qnorm_g[l]), rope_row, rope_col)
        kc = apply_axial_rope(rmsnorm(k_c.reshape(B, S, C_KV, HD), c_knorm_g[l]), rope_row, rope_col)
        out_c = dense_attention(qc, kc, v_c.reshape(B, S, C_KV, HD))

        mixed = jnp.concatenate([out_a, out_b, out_c], axis=-1)
        x = x + jnp.einsum('bsm,md->bsd', mixed, w_out[l])
        x = x + expert_choice_ffn(rmsnorm(x, norm2_g[l]), w_router[l], w_gate[l], w_up[l], w_down[l])
    return x


_drawn_inputs = setup_inputs


def setup_inputs(seed=0):
    import zlib

    import numpy as np

    out = dict(_drawn_inputs(seed))
    spreads = {}
    factors = {'a_norm_g': 3.273,
     'b_qnorm_g': 8.0,
     'b_knorm_g': 8.0,
     'b_sink': 8.0,
     'c_qnorm_g': 8.0,
     'c_knorm_g': 8.0}
    for name, (base, spread) in spreads.items():
        noise = np.random.default_rng([zlib.crc32(name.encode()), seed]).standard_normal(out[name].shape)
        drawn = base * np.exp(spread * noise) if base else spread * noise
        out[name] = __import__('jax').numpy.asarray(drawn.astype(out[name].dtype))
    for name, factor in factors.items():
        out[name] = (out[name] * factor).astype(out[name].dtype)
    return out
```

```python
from contextlib import ExitStack

import numpy as np

import concourse.bass as bass
from concourse import mybir

ALU = mybir.AluOpType
ACT = mybir.ActivationFunctionType
F32 = mybir.dt.float32
F32R = mybir.dt.float32r
U32 = mybir.dt.uint32
AX = mybir.AxisListType.X

P = 128
EPS = 1e-6

LAYERS = 2
SEQ = 512
D = 1024
TT = SEQ // P
KD = D // P
HA = 4
NQKV = 3 * HA
PROJ = 3088
REST = PROJ - NQKV * P
HD = 64
HB = 4
NSLOT = 12
NE = 16
CAP = 2 * SEQ // NE
DE = 1024
Z0, BA0, AT0 = 0, 512, 528
VOFF = 384

GROUPS = 7
RW = REST // 4
PIECE = 2048
RAW_A = 3
SPLIT = 3
N_IN = 2 * GROUPS
N_OUT = 4
SCALE = HD ** -0.5
RAW_M = 6
PAIRS = NE // 2
PER = 12
TURN = 2 * PER
GATE, UP, DOWN = range(3)
STREAM = [(GATE, 0), (UP, 0), (GATE, 1), (DOWN, 0), (UP, 1), (DOWN, 1)]
BY_POOL = (3, 9, 15, 21)
LOADS_A = (N_IN + N_OUT) // RAW_A

CONST_COLS = dict(ident=P, cum=2 * P, level=7 * P, window=3 * P, cos=2 * TT * HD, sin=2 * TT * HD,
                  iota=SEQ, tokid=TT)


def constants():
    p = np.arange(P)
    c = {"ident": np.eye(P)}
    c["cum"] = np.stack([p[:, None] <= p[None, :], p[:, None] >= p[None, :]], 1).reshape(P, -1)
    c["level"] = np.stack([(p[:, None] >> (l + 1) == p[None, :] >> (l + 1))
                           & (p[:, None] >> l != p[None, :] >> l) for l in range(7)], 1).reshape(P, -1)
    w = np.zeros((P, 3, P))
    w[:, 0] = np.where(p[None, :] >= p[:, None], 0.0, -1e30)
    w[:, 2] = np.where(p[None, :] <= p[:, None], 0.0, -1e30)
    c["window"] = w.reshape(P, -1)
    f = np.float32

    def table(pos, dim):
        inv = f(10000.0) ** (-np.arange(0, dim, 2, dtype=f) / f(dim))
        ang = pos.astype(f)[:, None] * inv[None, :]
        sign = np.concatenate([-np.ones(dim // 2), np.ones(dim // 2)])
        ang = np.concatenate([ang, ang], -1)
        return np.cos(ang), np.sin(ang) * sign
    pos = np.arange(SEQ)
    one, row, col = table(pos, HD), table(pos // 64, HD // 2), table(pos % 64, HD // 2)
    for n, key in enumerate(("cos", "sin")):
        t = np.stack([one[n], np.concatenate([row[n], col[n]], -1)], 1)
        c[key] = t.reshape(TT, P, 2, HD).transpose(1, 2, 0, 3).reshape(P, -1)
    c["iota"] = np.broadcast_to(np.arange(SEQ), (P, SEQ))
    c["tokid"] = p[:, None] + P * np.arange(TT)[None, :]
    return np.concatenate([c[k].astype(f) for k in CONST_COLS], 1)


def const_at(name):
    at = 0
    for k, n in CONST_COLS.items():
        if k == name:
            return at, n
        at += n


ROW_COLS = dict(a_log=8, dt_bias=8, a_norm=P, gains=4 * HD, sink=HB)
ROWS = sum(ROW_COLS.values())
COLS = KD + NQKV * 5


def bc(ap, axis, shape):
    return ap.unsqueeze(axis).to_broadcast(shape)


def bass_hybrid_encoder(nc, x, rows, cols, norm2, w_in, w_out, w_router, w_gate, w_up, w_down, consts, out):
    ctx = ExitStack()
    with ctx:
        def sem(name):
            return ctx.enter_context(nc.semaphore(name))

        def sb(name, shape, dt=F32, at=None):
            return (at or ctx).enter_context(nc.sbuf_tensor(name, shape, dt))

        X = sb("X", [P, TT, D])
        ident = sb("ident", [P, P])
        ones = sb("ones", [P, P])
        row = sb("row", [P, ROWS])
        col = sb("col", [P, COLS])
        raw = [sb(f"raw{i}", [P, PIECE]) for i in range(RAW_A)]
        one = ExitStack()
        delta = [{n: sb(f"{n}{d}", [P, HA, P], at=one)
                  for n in ("DM", "NT", "NM", "T", "TTr", "XS", "AT", "WT", "QG", "KD", "KG", "VN")}
                 for d in range(2)]
        one.close()
        whi = [sb(f"whi{i}", [P, PIECE], F32R) for i in range(SPLIT)]
        wlo = [sb(f"wlo{i}", [P, PIECE], F32R) for i in range(SPLIT)]
        mixer = ExitStack()
        one = ExitStack()
        QT, KT = (sb(n, [P, HA, SEQ], at=one) for n in ("QT", "KT"))
        KN, VN_ = (sb(n, [P, TT, HA, P], at=one) for n in ("KN", "VA"))
        one.close()
        MH, ML = (sb(n, [P, KD, SEQ], F32R, at=mixer) for n in ("MH", "ML"))
        one = ExitStack()
        HH, HL = (sb(n, [P, KD, SEQ], F32R, at=one) for n in ("HH", "HL"))
        one.close()
        AQ = sb("AQ", [P, 6, SEQ], at=mixer)
        AW = sb("AW", [P, 3, 768], at=mixer)
        O = sb("O", [P, TT, HA, P], at=mixer)
        junk = sb("junk", [P, 2 * KD * SEQ - 6 * SEQ - 3 * 768 - TT * HA * P], at=mixer)[:, 0:512]
        one = ExitStack()
        XN = sb("XN", [P, TT, D], at=one)
        one.close()
        PR = sb("PR", [P, TT, REST], at=mixer)
        one = ExitStack()
        XP = sb("XP", [P, 2, SEQ + 4], at=one)
        VD = sb("VD", [P, HA, SEQ], at=one)
        one.close()
        OB = sb("OB", [P, TT, 2 * HB * HD], at=mixer)
        S = sb("S", [P, 2, HA, P], at=mixer)
        sb("conv_rest", [P, 8], at=mixer)
        cum = sb("cum", [P, 2, P], at=mixer)
        level = sb("level", [P, 7, P], at=mixer)
        window = sb("window", [P, 3 * P], at=mixer)
        cosT = sb("cosT", [P, 2, TT, HD], at=mixer)
        sinT = sb("sinT", [P, 2, TT, HD], at=mixer)
        GN = sb("GN", [P, NSLOT, HD], at=mixer)
        st = sb("st", [P, 640], at=mixer)
        mixer.close()
        raw += [sb(f"raw{i}", [P, PIECE]) for i in range(RAW_A, RAW_M)]
        EH, EL = (sb(n, [P, TT, D], F32R) for n in ("EH", "EL"))
        idx_rows = sb("idx_rows", [P, (NE + 2) * CAP])
        sel = sb("sel", [P, TT, 2 * CAP], F32R)
        XE = sb("XE", [P, KD, 2, P], F32R)
        selT = sb("selT", [P, SEQ])
        norm2_row = sb("norm2_row", [P, D])
        one = ExitStack()
        HT = sb("HT", [P, KD, SEQ], at=one)
        one.close()
        GU = sb("GU", [P, 2, DE])
        YT = sb("YT", [CAP, D])
        YE = sb("YE", [P, D])
        one = ExitStack()
        hw = sb("hw", [P, 2, D], at=one)
        one.close()
        SG = sb("SG", [P, DE // P, CAP])
        HM = sb("HM", [P, DE // P, CAP])
        HP = sb("HP", [P, DE // P, P], F32R)
        iota = sb("iota", [P, SEQ])
        tokid = sb("tokid", [P, TT])
        router = sb("router", [P, KD, NE])
        fold = sb("fold", [P, CAP])
        aff = sb("aff", [P, TT, NE])
        work = sb("work", [NE, SEQ])
        best = sb("best", [NE, CAP])
        best_at = sb("best_at", [NE, CAP], U32)
        twice = sb("twice", [NE, 2, 2, CAP])
        spread = sb("spread", [NE, NE, CAP])
        slot_tok = sb("slot_tok", [P, PAIRS])
        slot_gate = sb("slot_gate", [P, NE])
        gate_now = sb("gate_now", [P, 2])
        st2 = sb("st2", [P, 32])
        ps = ctx.enter_context(nc.psum_tensor("ps", [P, 8, 512], F32))

        used = [0]

        def small(*shape):
            n = int(np.prod(shape))
            v = st[:, used[0]:used[0] + n]
            used[0] += n
            if len(shape) == 2:
                return v.rearrange("p (a b) -> p a b", b=shape[1])
            if len(shape) == 3:
                return v.rearrange("p (a b c) -> p a b c", b=shape[1], c=shape[2])
            return v
        ss1, rs1 = small(TT), small(TT)
        ssA, rsA = small(2, TT, HA), small(2, TT, HA)
        zb, tb, eb, lb = (small(TT, 8) for _ in range(4))
        beta, gdec = small(TT, 8), small(TT, 8)
        gcc, gll = small(2, TT, HA), small(2, TT, HA)
        egc, egl, kdc = small(2, TT, HA), small(2, TT, HA), small(2, TT, HA)
        ea = small(8)
        ssR, rsR = small(TT, NSLOT), small(TT, NSLOT)
        ssO, rsO = small(TT, HA), small(TT, HA)
        nsink = small(HB)
        rmax, nmx = small(2), small(2, HB)
        psumS, rinv, esk = small(2, HB), small(2, HB), small(2, HB)

        a_log, dt_b = row[:, 0:8], row[:, 8:16]
        a_norm = row[:, 16:16 + P]
        gains = row[:, 16 + P:16 + P + 4 * HD].rearrange("p (a b) -> p a b", b=HD)
        sink = row[:, 16 + P + 4 * HD:ROWS]
        g1 = col[:, 0:KD]
        cw = col[:, KD:COLS].rearrange("p (c j) -> p c j", j=5)

        s_init, ones_set, s_out = sem("s_init"), sem("ones_set"), sem("s_out")
        raw_full = [sem(f"raw_full{i}") for i in range(RAW_M)]
        par_in, const_in = sem("par_in"), sem("const_in")
        hi_done, lo_done, passes = sem("hi_done"), sem("lo_done"), sem("passes")
        x_sq, x_var, x_std, x_rstd, x_normed = (sem(n) for n in ("x_sq", "x_var", "x_std", "x_rstd", "x_normed"))
        xT_done, hT_hi, hT_lo = sem("xT_done"), sem("hT_hi"), sem("hT_lo")
        pad_set, proj_evac, tap0, conv_done, silu_done = (sem(n) for n in ("pad_set", "proj_evac", "tap0", "conv_done", "silu_done"))
        conv_step = sem("conv_step")
        tok_T, tok_evac, tok_sq, tok_ss = (sem(n) for n in ("tok_T", "tok_evac", "tok_sq", "tok_ss"))
        a_chain, v_chain, p_chain = sem("a_chain"), sem("v_chain"), sem("p_chain")
        qk_var, qk_std, qk_normed, back_T, back_evac = (sem(n) for n in ("qk_var", "qk_std", "qk_normed", "back_T", "back_evac"))
        gate_z, gate_e, gate_w, gate_ln, g_ready = (sem(n) for n in ("gate_z", "gate_e", "gate_w", "gate_ln", "g_ready"))
        cum_done, cum_evac, cum_diff, cum_exp = (sem(n) for n in ("cum_done", "cum_evac", "cum_diff", "cum_exp"))
        gu_ready, row_done, diff_done, dm_exp, eg_exp, masked, nt_base = (sem(n) for n in ("gu_ready", "row_done", "diff_done", "dm_exp", "eg_exp", "masked", "nt_base"))
        gram_done, at_done, nt_done, qg_done, kgd_done = (sem(n) for n in ("gram_done", "at_done", "nt_done", "qg_done", "kgd_done"))
        nm_done, t0_done, t0_T, t0_evac = (sem(n) for n in ("nm_done", "t0_done", "t0_T", "t0_evac"))
        x_done, x_evac, y_done, t_new = (sem(n) for n in ("x_done", "x_evac", "y_done", "t_new"))
        w_done, w_evac, v_done, vn_done, o_done, o_evac = (sem(n) for n in ("w_done", "w_evac", "v_done", "vn_done", "o_done", "o_evac"))
        s_done, s_dec, s_new, s_zero = (sem(n) for n in ("s_done", "s_dec", "s_new", "s_zero"))
        r_sq, r_ss, r_std, r_normed, rope_done, aq_T, aq_evac, gain_set = (sem(n) for n in ("r_sq", "r_ss", "r_std", "r_normed", "rope_done", "aq_T", "aq_evac", "gain_set"))
        score_done, win_done, max_done, prob_done, pT_done, pT_evac, pv_done, ob_evac = (sem(n) for n in ("score_done", "win_done", "max_done", "prob_done", "pT_done", "pT_evac", "pv_done", "ob_evac"))
        sink_in, sink_exp = sem("sink_in"), sem("sink_exp")
        oa_sq, oa_var, oa_std, z_exp, oa_done = (sem(n) for n in ("oa_sq", "oa_var", "oa_std", "z_exp", "oa_done"))
        mix_T, mix_hi, mix_lo, x_added = (sem(n) for n in ("mix_T", "mix_hi", "mix_lo", "x_added"))
        e_in, fold_set, e_sq, e_var, e_std, h_done, e_hi, e_lo, hT2_done, hT2_evac = (sem(n) for n in (
            "e_in", "fold_set", "e_sq", "e_var", "e_std", "h_done", "e_hi", "e_lo", "hT2_done", "hT2_evac"))
        logit_done, logit_max, logit_exp, aff_done, affT_done, chosen, chosen_T, spread_done, rows_done, top_ready = (sem(n) for n in (
            "logit_done", "logit_max", "logit_exp", "aff_done", "affT_done", "chosen", "chosen_T", "spread_done", "rows_done", "top_ready"))
        m_hi, m_lo, m_lo_pool, m_pass = (sem(n) for n in ("m_hi", "m_lo", "m_lo_pool", "m_pass"))
        sel_done, selT_done, gathered, xe_evac = (sem(n) for n in ("sel_done", "selT_done", "gathered", "xe_evac"))
        gu_evac, folded, sg_done, hm_done, hp_hi, hp_lo = (sem(n) for n in ("gu_evac", "folded", "sg_done", "hm_done", "hp_hi", "hp_lo"))
        yt_done, ye_done, zeroed, scattered = (sem(n) for n in ("yt_done", "ye_done", "zeroed", "scattered"))
        slot_free = sem("slot_free")

        def piece_view(t, n):
            if n >= N_IN:
                return t[:, :].rearrange("p (k c) -> p k c", k=2)
            w = 512 if n < 2 * 3 else RW
            return t[:, 0:4 * w].rearrange("p (k c) -> p k c", k=4)

        def piece_dram(L, n):
            if n >= N_IN:
                m = n - N_IN
                return w_out[bass.ds(L, 1), m * 2 * P:(m + 1) * 2 * P, :].rearrange("l (k p) c -> p (l k) c", p=P)
            g, half = divmod(n, 2)
            c0, w = (g * 512, 512) if g < 3 else (NQKV * P + (g - 3) * RW, RW)
            return w_in[bass.ds(L, 1), half * 4 * P:(half + 1) * 4 * P, c0:c0 + w].rearrange("l (k p) c -> p (l k) c", p=P)

        UNITS = [(s, qt, h) for s in range(2) for qt in range(TT) for h in range(HB)]

        def key_tiles(s, qt):
            return range(max(0, qt - 1), min(TT, qt + 2)) if s == 0 else range(TT)

        def tile_of(d, t):
            return t if d == 0 else TT - 1 - t

        def win(u):
            return delta[u % 2]["DM"][:, :, :].rearrange("p a b -> p (a b)")

        def prob(u):
            return delta[u % 2]["NT"][:, :, :].rearrange("p a b -> p (a b)")

        def probT(u):
            return delta[u % 2]["NM"][:, :, :].rearrange("p a b -> p (a b)")

        def rounds(eng, n):
            eng.wait_ge(raw_full[n % RAW_A], 16 * (n // RAW_A + 1))
            if n >= SPLIT:
                m = n - SPLIT
                eng.wait_ge(passes, 4 * (m + 1) if m < N_IN else 4 * N_IN + 8 * (m - N_IN + 1))
            nc.scalar.activation(piece_view(whi[n % SPLIT], n), piece_view(raw[n % RAW_A], n), ACT.Copy).then_inc(hi_done, 1)

        def rests(eng, n):
            eng.wait_ge(hi_done, n + 1)
            nc.vector.tensor_tensor(piece_view(wlo[n % SPLIT], n), piece_view(raw[n % RAW_A], n),
                                    piece_view(whi[n % SPLIT], n), ALU.subtract).then_inc(lo_done, 1)

        def expert_dram(L, g, q):
            (m, e), j = STREAM[q // 4], q % 4
            w = (w_gate, w_up, w_down)[m]
            return w[bass.ds(L, 1), bass.ds(g * 2 + e, 1), j * 2 * P:(j + 1) * 2 * P, :].rearrange("l e (k p) c -> p (l e k) c", p=P)

        def two(t):
            return t[:, :].rearrange("p (k c) -> p k c", k=2)

        def by_pool(q):
            return q in BY_POOL

        def dve_split(q):
            return sum(not by_pool(p) for p in range(q + 1))
        DVE_TURN, POOL_TURN = dve_split(TURN - 1), TURN - dve_split(TURN - 1)

        def wait_split(eng, g, q):
            if by_pool(q):
                eng.wait_ge(m_lo_pool, g * POOL_TURN + (q + 1 - dve_split(q)))
            else:
                eng.wait_ge(m_lo, g * DVE_TURN + dve_split(q))

        def expert_rounds(eng, g, q):
            slot = q % RAW_M
            eng.wait_ge(raw_full[slot], (g * (TURN // RAW_M) + (q // RAW_M + 1 + (LOADS_A if slot < RAW_A else 0))) * 16)
            eng.wait_ge(m_pass, g * TURN + (q + 1))
            nc.scalar.activation(whi[q % SPLIT][:, :], raw[slot][:, :], ACT.Copy).then_inc(m_hi, 1)

        def expert_rests(eng, g, q):
            eng.wait_ge(m_hi, g * TURN + (q + 1))
            o, a, b = wlo[q % SPLIT][:, :], raw[q % RAW_M][:, :], whi[q % SPLIT][:, :]
            if by_pool(q):
                nc.gpsimd.tensor_tensor(o, a, b, ALU.subtract).then_inc(m_lo_pool, 1)
            else:
                nc.vector.tensor_tensor(o, a, b, ALU.subtract).then_inc(m_lo, 1)

        with nc.Block() as block:
            @block.sync
            def _(sp):
                sp.dma_start(X[:, :, :], x.rearrange("o (t p) d -> p (o t) d", p=P)).then_inc(s_init, 16)
                a, n = const_at("ident")
                sp.dma_start(ident[:, :], consts[:, a:a + n]).then_inc(s_init, 16)
                sp.wait_ge(s_init, 32)
                sp.wait_ge(ones_set, 1)

            @block.gpsimd
            def _(pool):
                nc.gpsimd.memset(ones[:, :], 1.0).then_inc(ones_set, 1)

        with nc.Fori(0, LAYERS) as L:
            with nc.Block() as block:
                @block.sync
                def _(sp):
                    for n in range(2):
                        sp.dma_start(piece_view(raw[n], n), piece_dram(L, n)).then_inc(raw_full[n % RAW_A], 16)
                    sp.dma_start(row[:, :], rows[bass.ds(L, 1), :].to_broadcast([P, ROWS])).then_inc(par_in, 16)
                    sp.dma_start(col[:, :], cols[bass.ds(L, 1), :, :].rearrange("l p c -> p (l c)")).then_inc(par_in, 16)
                    for name, dst in (("cum", cum[:, :, :]), ("level", level[:, :, :]), ("window", window[:, :]),
                                      ("cos", cosT[:, :, :, :]), ("sin", sinT[:, :, :, :])):
                        a, n = const_at(name)
                        src = consts[:, a:a + n]
                        if name in ("cum", "level"):
                            src = src.rearrange("p (a b) -> p a b", b=P)
                        elif name != "window":
                            src = src.rearrange("p (a b c) -> p a b c", b=TT, c=HD)
                        sp.dma_start(dst, src).then_inc(const_in, 16)
                    for n in range(2, N_IN + N_OUT):
                        if n >= RAW_A:
                            sp.wait_ge(lo_done, n - RAW_A + 1)
                        sp.dma_start(piece_view(raw[n % RAW_A], n), piece_dram(L, n)).then_inc(raw_full[n % RAW_A], 16)

                    for i in range(RAW_A):
                        sp.wait_ge(lo_done, N_IN + N_OUT - RAW_A + i + 1)
                        sp.dma_start(two(raw[i]), expert_dram(L, 0, i)).then_inc(raw_full[i], 16)
                    sp.wait_ge(x_added, 8)
                    sp.dma_start(norm2_row[:, :], norm2[bass.ds(L, 1), :].to_broadcast([P, D])).then_inc(e_in, 16)
                    sp.dma_start(router[:, :, :], w_router[bass.ds(L, 1), :, :].rearrange("l (k p) e -> p (l k) e", p=P)).then_inc(e_in, 16)
                    for name, dst in (("iota", iota[:, :]), ("tokid", tokid[:, :])):
                        a, n = const_at(name)
                        sp.dma_start(dst, consts[:, a:a + n]).then_inc(e_in, 16)
                    for i in range(RAW_A, RAW_M):
                        sp.dma_start(two(raw[i]), expert_dram(L, 0, i)).then_inc(raw_full[i], 16)

                    def refill(g, q):
                        n = q + RAW_M
                        src = expert_dram(L, g + n // TURN, n % TURN)
                        wait_split(sp, g, q)
                        sp.sem_inc(slot_free, 1)
                        sp.dma_start(two(raw[q % RAW_M]), src).then_inc(raw_full[q % RAW_M], 16)
                    with sp.Fori(0, PAIRS - 1) as g:
                        for q in range(TURN):
                            refill(g, q)
                    for q in range(TURN - RAW_M):
                        refill(PAIRS - 1, q)

                @block.tensor
                def _(pe):
                    mm = nc.tensor.matmul
                    pe.wait_ge(x_normed, TT)
                    for k in range(KD):
                        for t in range(TT):
                            last = nc.tensor.transpose(ps[:, k, t * P:(t + 1) * P], XN[:, t, k * P:(k + 1) * P], ident[:, :])
                        last.then_inc(xT_done, 1)
                    for g in range(GROUPS):
                        for half in range(2):
                            n = 2 * g + half
                            pe.wait_ge(lo_done, n + 1)
                            if g == 0:
                                pe.wait_ge(hT_lo, 4 * (half + 1))
                            if g == 1:
                                pe.wait_ge(hT_lo, KD)
                            hi, lo = piece_view(whi[n % SPLIT], n), piece_view(wlo[n % SPLIT], n)
                            for t in range(4):
                                if g >= 2 and half == 0:
                                    pe.wait_ge(proj_evac, 4 * (g - 2) + t + 1)
                                b = 4 * (g % 2) + t
                                for kk in range(4):
                                    k = 4 * half + kk
                                    for j, (w, h) in enumerate(((hi, HH), (lo, HH), (hi, HL))):
                                        flags = dict(start=half == 0 and kk == 0 and j == 0, stop=half == 1 and kk == 3 and j == 2)
                                        if g < 3:
                                            last = mm(ps[:, b, :], w[:, kk, t * P:(t + 1) * P], h[:, k, :], **flags)
                                        else:
                                            last = mm(ps[:, b, 0:RW], h[:, k, t * P:(t + 1) * P], w[:, kk, :], **flags)
                                last.then_inc(passes, 1)
                    pe.wait_ge(silu_done, NQKV)
                    for i, (c, t) in enumerate((c, t) for c in range(3) for t in range(TT)):
                        if i == 0:
                            pe.wait_ge(proj_evac, 4 * GROUPS)
                        if i >= 8:
                            pe.wait_ge(tok_sq, i - 7)
                        for h in range(HA):
                            src = (QT, KT, VD)[c][:, h, t * P:(t + 1) * P]
                            last = nc.tensor.transpose(ps[:, i % 8, h * P:(h + 1) * P], src, ident[:, :])
                        last.then_inc(tok_T, 1)
                    for i, (c, h) in enumerate((c, h) for c in range(2) for h in range(HA)):
                        if h == 0:
                            pe.wait_ge(qk_normed, 4 * (c + 1))
                        if i < 4:
                            pe.wait_ge(tok_sq, 8)
                            pe.wait_ge(tok_evac, 9 + i)
                        for t in range(TT):
                            src = (O, KN)[c][:, t, h, :]
                            last = nc.tensor.transpose(ps[:, i, t * P:(t + 1) * P], src, ident[:, :])
                        last.then_inc(back_T, 1)
                    pe.wait_ge(g_ready, 1)
                    pe.wait_ge(const_in, 5 * 16)
                    pe.wait_ge(back_evac, 1)
                    for d in range(2):
                        g = gdec[:, :, d * HA:(d + 1) * HA]
                        mm(ps[:, 0, d * 16:(d + 1) * 16], cum[:, d, :], g, start=True, stop=True)
                        last = mm(ps[:, 0, 32 + d * 16:48 + d * 16], ones[:, :], g, start=True, stop=True)
                    last.then_inc(cum_done, 1)
                    pe.wait_ge(back_evac, 8)
                    pe.wait_ge(cum_evac, 1)
                    for t in range(TT):
                        for d in range(2):
                            i = 2 * t + d
                            B, b0 = delta[d], 4 * d
                            tl = tile_of(d, t)
                            tok = slice(tl * P, (tl + 1) * P)
                            pe.wait_ge(gu_ready, i + 1)
                            if t > 0:
                                pe.wait_ge(w_evac, i - 1)
                                pe.wait_ge(vn_done, i - 1)
                                pe.wait_ge(o_evac, i - 1)
                            mm(ps[:, b0, :], ones[:, :], B["NM"][:, :, :].rearrange("p a b -> p (a b)"), start=True, stop=True).then_inc(row_done, 1)
                            for h in range(HA):
                                mm(ps[:, b0 + 1, h * P:(h + 1) * P], KT[:, h, tok], QT[:, h, tok], start=True, stop=True)
                            for h in range(HA):
                                last = mm(ps[:, b0 + 2, h * P:(h + 1) * P], KT[:, h, tok], KT[:, h, tok], start=True, stop=True)
                            last.then_inc(gram_done, 1)
                        for d in range(2):
                            i = 2 * t + d
                            B, b0 = delta[d], 4 * d
                            pe.wait_ge(t0_done, i + 1)
                            if t > 0:
                                pe.wait_ge(s_new, i - 1)
                            for h in range(HA):
                                last = nc.tensor.transpose(ps[:, b0 + 3, h * P:(h + 1) * P], B["TTr"][:, h, :], ident[:, :])
                            last.then_inc(t0_T, 1)
                        for l in range(1, 7):
                            for d in range(2):
                                i = 2 * t + d
                                c = (6 * t + l - 1) * 2 + d
                                B, b0 = delta[d], 4 * d
                                pe.wait_ge(nm_done, (7 * t + l) * 2 + d + 1)
                                if l == 1:
                                    pe.wait_ge(t0_evac, i + 1)
                                    pe.wait_ge(diff_done, i + 1)
                                    pe.wait_ge(nt_done, i + 1)
                                else:
                                    pe.wait_ge(t_new, 2 * (c - 1))
                                for h in range(HA):
                                    last = mm(ps[:, b0, h * P:(h + 1) * P], B["NM"][:, h, :], B["T"][:, h, :], start=True, stop=True)
                                last.then_inc(x_done, 1)
                            for d in range(2):
                                c = (6 * t + l - 1) * 2 + d
                                B, b0 = delta[d], 4 * d
                                pe.wait_ge(x_evac, c + 1)
                                if l < 6:
                                    for h in range(HA):
                                        mm(ps[:, b0 + 1, h * P:(h + 1) * P], B["TTr"][:, h, :], B["XS"][:, h, :], start=True, stop=True)
                                for h in range(HA):
                                    last = mm(ps[:, b0 + 2, h * P:(h + 1) * P], B["XS"][:, h, :], B["TTr"][:, h, :], start=True, stop=True)
                                last.then_inc(y_done, 1)
                        for d in range(2):
                            i = 2 * t + d
                            B, b0 = delta[d], 4 * d
                            tl = tile_of(d, t)
                            pe.wait_ge(t_new, 2 * ((6 * t + 5) * 2 + d + 1))
                            pe.wait_ge(kgd_done, 2 * (i + 1))
                            for h in range(HA):
                                last = mm(ps[:, b0, h * P:(h + 1) * P], B["KG"][:, h, :], B["TTr"][:, h, :], start=True, stop=True)
                            last.then_inc(w_done, 1)
                        for d in range(2):
                            i = 2 * t + d
                            B, b0 = delta[d], 4 * d
                            tl = tile_of(d, t)
                            pe.wait_ge(w_evac, i + 1)
                            if t == 0:
                                pe.wait_ge(s_zero, 1)
                            else:
                                pe.wait_ge(s_new, i - 1)
                            pe.wait_ge(t0_evac, i + 1)
                            for h in range(HA):
                                mm(ps[:, b0 + 1, h * P:(h + 1) * P], B["TTr"][:, h, :], VN_[:, tl, h, :], start=True, stop=False)
                                last = mm(ps[:, b0 + 1, h * P:(h + 1) * P], B["WT"][:, h, :], S[:, d, h, :], start=False, stop=True)
                            last.then_inc(v_done, 1)
                        for d in range(2):
                            i = 2 * t + d
                            B, b0 = delta[d], 4 * d
                            pe.wait_ge(vn_done, i + 1)
                            pe.wait_ge(qg_done, i + 1)
                            for h in range(HA):
                                mm(ps[:, b0 + 2, h * P:(h + 1) * P], B["QG"][:, h, :], S[:, d, h, :], start=True, stop=False)
                                last = mm(ps[:, b0 + 2, h * P:(h + 1) * P], B["AT"][:, h, :], B["VN"][:, h, :], start=False, stop=True)
                            last.then_inc(o_done, 1)
                            if t < TT - 1:
                                for h in range(HA):
                                    last = mm(ps[:, b0 + 3, h * P:(h + 1) * P], B["KD"][:, h, :], B["VN"][:, h, :], start=True, stop=True)
                                last.then_inc(s_done, 1)
                    for t in range(TT):
                        pe.wait_ge(rope_done, t + 1)
                        if t == 0:
                            pe.wait_ge(o_evac, 8)
                            pe.wait_ge(t0_evac, 8)
                        if t >= 2:
                            pe.wait_ge(aq_evac, 2 * (t - 1))
                        for half in range(2):
                            for j in range(3):
                                c = (3 * half + j) * P
                                last = nc.tensor.transpose(ps[:, 4 + 2 * (t % 2) + half, j * P:(j + 1) * P], AW[:, 0, c:c + P], ident[:, :])
                            last.then_inc(aq_T, 1)

                    def scores(u):
                        s, qt, h = UNITS[u]
                        kts = key_tiles(s, qt)
                        if u >= 2:
                            if s == 0 or UNITS[u - 2][0] == 0:
                                pe.wait_ge(win_done, min(u - 1, 16))
                            if UNITS[u - 2][0] == 1:
                                pe.wait_ge(prob_done, u - 1)
                        base = HD * (h // 2)
                        mm(ps[:, u % 2, 0:P * len(kts)], AQ[base:base + HD, 3 * s + h % 2, qt * P:(qt + 1) * P],
                           AQ[base:base + HD, 3 * s + 2, kts[0] * P:(kts[-1] + 1) * P], start=True, stop=True).then_inc(score_done, 1)

                    def transposed(u):
                        s, qt, h = UNITS[u]
                        pe.wait_ge(prob_done, u + 1)
                        if u >= 2:
                            pe.wait_ge(pT_evac, u - 1)
                        for j in range(len(key_tiles(s, qt))):
                            last = nc.tensor.transpose(ps[:, 2 + u % 2, j * P:(j + 1) * P], prob(u)[:, j * P:(j + 1) * P], ident[:, :])
                        last.then_inc(pT_done, 1)

                    def weighted(u):
                        s, qt, h = UNITS[u]
                        kts = key_tiles(s, qt)
                        pe.wait_ge(pT_evac, u + 1)
                        if u >= 8 and h == 0:
                            pe.wait_ge(ob_evac, u // 4 - 1)
                        for j, kt in enumerate(kts):
                            v = BA0 + 16 + s * 512 + VOFF + (h // 2) * HD
                            last = mm(ps[:, 4 + (u // 4) % 2, h * HD:(h + 1) * HD], probT(u)[:, j * P:(j + 1) * P],
                                      PR[:, kt, v:v + HD], start=j == 0, stop=j == len(kts) - 1)
                        last.then_inc(pv_done, 1)
                    pe.wait_ge(aq_evac, 2 * TT)
                    scores(0)
                    for u in range(len(UNITS)):
                        if u + 1 < len(UNITS):
                            scores(u + 1)
                        transposed(u)
                        if u:
                            weighted(u - 1)
                    weighted(len(UNITS) - 1)
                    for k in range(KD):
                        if k == 0:
                            pe.wait_ge(ob_evac, 2 * TT)
                            pe.wait_ge(oa_done, 1)
                        for t in range(TT):
                            src = O[:, t, k, :] if k < HA else OB[:, t, (k - HA) * P:(k - HA + 1) * P]
                            last = nc.tensor.transpose(ps[:, k, t * P:(t + 1) * P], src, ident[:, :])
                        last.then_inc(mix_T, 1)
                    pe.wait_ge(mix_lo, KD)
                    for m in range(N_OUT):
                        n = N_IN + m
                        pe.wait_ge(lo_done, n + 1)
                        hi, lo = piece_view(whi[n % SPLIT], n), piece_view(wlo[n % SPLIT], n)
                        for b in range(8):
                            t, half = divmod(b, 2)
                            for kk in range(2):
                                for j, (w, h) in enumerate(((hi, MH), (lo, MH), (hi, ML))):
                                    last = mm(ps[:, b, :], h[:, 2 * m + kk, t * P:(t + 1) * P], w[:, kk, half * 512:(half + 1) * 512],
                                              start=m == 0 and kk == 0 and j == 0, stop=m == N_OUT - 1 and kk == 1 and j == 2)
                            last.then_inc(passes, 1)

                    for t in range(TT):
                        pe.wait_ge(h_done, t + 1)
                        pe.wait_ge(x_added, 8)
                        if t >= 2:
                            pe.wait_ge(hT2_evac, 2 * (t - 1))
                        for half in range(2):
                            for j in range(4):
                                k = 4 * half + j
                                last = nc.tensor.transpose(ps[:, 2 * (t % 2) + half, j * P:(j + 1) * P], hw[:, t % 2, k * P:(k + 1) * P], ident[:, :])
                            last.then_inc(hT2_done, 1)
                    pe.wait_ge(e_in, 64)
                    pe.wait_ge(hT2_evac, 2 * TT)
                    for t in range(TT):
                        for k in range(KD):
                            last = mm(ps[:, 4, t * NE:(t + 1) * NE], HT[:, k, t * P:(t + 1) * P], router[:, k, :], start=k == 0, stop=k == KD - 1)
                    last.then_inc(logit_done, 1)
                    pe.wait_ge(aff_done, 1)
                    for t in range(TT):
                        last = nc.tensor.transpose(ps[0:NE, 5, t * P:(t + 1) * P], aff[:, t, :], ident[:, :])
                    last.then_inc(affT_done, 1)
                    pe.wait_ge(chosen, 1)
                    for j in range(2):
                        last = nc.tensor.transpose(ps[:, 6, j * NE:(j + 1) * NE], twice[:, j, :, :].rearrange("p a b -> p (a b)"), ident[0:NE, 0:NE])
                    last.then_inc(chosen_T, 1)
                    pe.wait_ge(spread_done, 1)
                    for j in range(2):
                        last = mm(ps[:, j, :], ones[0:NE, :], spread[:, 8 * j:8 * j + 8, :].rearrange("p a b -> p (a b)"), start=True, stop=True)
                    last.then_inc(rows_done, 1)
                    pe.wait_ge(fold_set, 1)
                    pe.wait_ge(top_ready, 1)
                    pe.sem_inc(m_pass, SPLIT)
                    pe.wait_ge(selT_done, 1)
                    pe.wait_ge(ye_done, 1)
                    for half in range(2):
                        mm(ps[:, 6 + half, :], selT[:, 0:P], YE[:, 0:512], start=True, stop=True).then_inc(zeroed, 1)

                    def gather(part):
                        for k in range(4 * part, 4 * part + 4):
                            for z, h in enumerate((EH, EL)):
                                at = 128 * (2 * (k % 2) + z)
                                copies = 2 if at < 384 else 1
                                o = ps[:, k // 2, at:at + copies * P].rearrange("p (c s) -> p c s", c=copies)
                                for t in range(TT):
                                    last = mm(o, h[:, t, k * P:(k + 1) * P], bc(sel[:, t, :], 1, [P, copies, P]), start=t == 0, stop=t == TT - 1)
                        last.then_inc(gathered, 1)
                    def scatter(ns):
                        for n in ns:
                            t, half = divmod(n, 2)
                            mm(ps[:, 4 + n % 4, :], selT[:, t * P:(t + 1) * P], YE[:, half * 512:(half + 1) * 512], start=True, stop=True).then_inc(scattered, 1)
                    pe.wait_ge(sel_done, 1)
                    gather(0)
                    gather(1)
                    with pe.Fori(0, PAIRS) as g:
                        def times(block, js, bank, lhs):
                            for j in js:
                                q = 4 * block + j
                                wait_split(pe, g, q)
                                for kk in range(2):
                                    k = 2 * j + kk
                                    for half in range(2):
                                        for z, w in enumerate((whi, wlo)):
                                            last = mm(ps[:, bank + half, :], lhs(k), two(w[q % SPLIT])[:, kk, half * 512:(half + 1) * 512],
                                                      start=k == 0 and z == 0, stop=k == KD - 1 and z == 1)
                                last.then_inc(m_pass, 1)

                        def folds(j):
                            for f in range(DE // P):
                                last = mm(ps[:, 4 + j, f * CAP:(f + 1) * CAP], GU[:, j, f * P:(f + 1) * P], fold[:, :], start=True, stop=True)
                            last.then_inc(folded, 1)

                        def a(k):
                            return XE[:, k, 0, :]

                        def b(k):
                            return XE[:, k, 1, :]

                        def hidden(k):
                            return HP[:, k, :]
                        pe.wait_ge(xe_evac, g * 2 + 2)
                        times(0, range(3), 0, a)
                        pe.wait_ge(ye_done, g * 2 + 2)
                        pe.wait_ge(selT_done, g + 1)
                        scatter(range(4))
                        times(0, range(3, 4), 0, a)
                        times(1, range(3), 2, a)
                        pe.wait_ge(x_added, g * 8 + 12)
                        scatter(range(4, 8))
                        times(1, range(3, 4), 2, a)
                        pe.wait_ge(gu_evac, g * 4 + 1)
                        times(2, range(2), 0, b)
                        pe.wait_ge(gu_evac, g * 4 + 2)
                        pe.wait_ge(x_added, g * 8 + 16)
                        folds(0)
                        folds(1)
                        times(2, range(2, 4), 0, b)
                        pe.wait_ge(hp_lo, g * 2 + 1)
                        times(3, range(4), 6, hidden)
                        pe.wait_ge(gu_evac, g * 4 + 3)
                        folds(0)
                        times(4, range(4), 2, b)
                        pe.wait_ge(gu_evac, g * 4 + 4)
                        folds(1)
                        pe.wait_ge(sel_done, g + 2)
                        gather(0)
                        pe.wait_ge(hp_lo, g * 2 + 2)
                        pe.wait_ge(ye_done, g * 2 + 3)
                        times(5, range(1), 6, hidden)
                        gather(1)
                        times(5, range(1, 4), 6, hidden)
                    pe.wait_ge(ye_done, PAIRS * 2 + 2)
                    pe.wait_ge(selT_done, PAIRS + 1)
                    scatter(range(4))
                    pe.wait_ge(x_added, PAIRS * 8 + 12)
                    scatter(range(4, 8))

                @block.scalar
                def _(act):
                    A = nc.scalar.activation

                    for t in range(TT):
                        A(XN[:, t, :], X[:, t, :], ACT.Square, accum_out=ss1[:, t:t + 1]).then_inc(x_sq, 1)
                    rounds(act, 0)
                    rounds(act, 1)
                    act.wait_ge(x_var, 1)
                    A(rs1[:, :], ss1[:, :], ACT.Sqrt).then_inc(x_std, 1)
                    act.wait_ge(par_in, 32)
                    for k in range(KD):
                        act.wait_ge(xT_done, k + 1)
                        A(HH[:, k, :], ps[:, k, :], ACT.Copy, scale=g1[:, k:k + 1]).then_inc(hT_hi, 1)

                    def silu(ct):
                        dst = (QT, KT, VD)[ct // 4][:, ct % 4, :]
                        act.wait_ge(conv_done, ct + 1)
                        A(dst, dst, ACT.Silu).then_inc(silu_done, 1)
                    act.wait_ge(pad_set, 1)
                    for g in range(GROUPS):
                        for n in (2 * g + 2, 2 * g + 3):
                            if n < N_IN:
                                rounds(act, n)
                        for t in range(4):
                            act.wait_ge(passes, 8 * g + 4 + t + 1)
                            b = 4 * (g % 2) + t
                            if g < 3:
                                ct = 4 * g + t
                                if ct >= 2:
                                    act.wait_ge(conv_done, ct - 1)
                                A(XP[:, ct % 2, 2:SEQ + 2], ps[:, b, :], ACT.Copy).then_inc(proj_evac, 1)
                                act.wait_ge(proj_evac, ct + 1)
                                A((QT, KT, VD)[g][:, t, :], XP[:, ct % 2, 0:SEQ], ACT.Copy, scale=cw[:, ct, 0:1]).then_inc(tap0, 1)
                                if ct >= 1:
                                    silu(ct - 1)
                            else:
                                if g == 3 and t == 0:
                                    silu(NQKV - 1)
                                A(PR[:, t, (g - 3) * RW:(g - 2) * RW], ps[:, b, 0:RW], ACT.Copy).then_inc(proj_evac, 1)
                    for i in range(12):
                        c, t = divmod(i, TT)
                        act.wait_ge(tok_T, i + 1)
                        dst = (O, KN, VN_)[c][:, t, :, :]
                        A(dst, ps[:, i % 8, :].rearrange("p (a b) -> p a b", b=P), ACT.Copy).then_inc(tok_evac, 1)
                        if c < 2:
                            if i >= 1:
                                act.wait_ge(tok_ss, i)
                            A(junk, ps[:, i % 8, :], ACT.Square).then_inc(tok_sq, 1)
                    act.wait_ge(qk_var, 1)
                    A(rsA[:, :, :, :], ssA[:, :, :, :], ACT.Sqrt).then_inc(qk_std, 1)
                    act.wait_ge(gate_z, 1)
                    A(eb[:, :, :], tb[:, :, :], ACT.Exp, scale=-1.0).then_inc(gate_e, 1)
                    A(beta[:, :, :], PR[:, :, BA0:BA0 + 8], ACT.Exp, scale=-1.0).then_inc(gate_e, 1)
                    A(ea[:, :], a_log, ACT.Exp).then_inc(gate_e, 1)
                    act.wait_ge(gate_w, 1)
                    A(lb[:, :, :], tb[:, :, :], ACT.Ln).then_inc(gate_ln, 1)
                    for i in range(8):
                        c, h = divmod(i, HA)
                        act.wait_ge(back_T, i + 1)
                        A((QT, KT)[c][:, h, :], ps[:, i, :], ACT.Copy).then_inc(back_evac, 1)
                    act.wait_ge(cum_diff, 1)
                    A(egc[:, :, :, :], gcc[:, :, :, :], ACT.Exp)
                    A(egl[:, :, :, :], gll[:, :, :, :], ACT.Exp)
                    A(kdc[:, :, :, :], kdc[:, :, :, :], ACT.Exp).then_inc(cum_exp, 1)
                    for t in range(TT):
                        for d in range(2):
                            i = 2 * t + d
                            B, b0 = delta[d], 4 * d
                            act.wait_ge(row_done, i + 1)
                            if t > 0:
                                act.wait_ge(o_done, i - 1)
                            A(B["QG"][:, :, :], ps[:, b0, :].rearrange("p (a b) -> p a b", b=P), ACT.Exp).then_inc(eg_exp, 1)
                            act.wait_ge(diff_done, i + 1)
                            A(B["DM"][:, :, :], B["DM"][:, :, :], ACT.Exp).then_inc(dm_exp, 1)
                        for d in range(2):
                            i = 2 * t + d
                            B, b0 = delta[d], 4 * d
                            act.wait_ge(t0_T, i + 1)
                            A(B["T"][:, :, :], ps[:, b0 + 3, :].rearrange("p (a b) -> p a b", b=P), ACT.Copy).then_inc(t0_evac, 1)
                        for l in range(1, 7):
                            for d in range(2):
                                c = (6 * t + l - 1) * 2 + d
                                B, b0 = delta[d], 4 * d
                                act.wait_ge(x_done, c + 1)
                                if c >= 2:
                                    act.wait_ge(y_done, c - 1)
                                A(B["XS"][:, :, :], ps[:, b0, :].rearrange("p (a b) -> p a b", b=P), ACT.Copy).then_inc(x_evac, 1)
                        for d in range(2):
                            i = 2 * t + d
                            B, b0 = delta[d], 4 * d
                            act.wait_ge(w_done, i + 1)
                            if t > 0:
                                act.wait_ge(v_done, i - 1)
                            A(B["WT"][:, :, :], ps[:, b0, :].rearrange("p (a b) -> p a b", b=P), ACT.Copy, scale=-1.0).then_inc(w_evac, 1)
                    act.wait_ge(oa_var, 1)
                    A(rsO[:, :, :], ssO[:, :, :], ACT.Sqrt).then_inc(oa_std, 1)
                    A(rsR[:, :, :], ssR[:, :, :], ACT.Sqrt).then_inc(r_std, 1)
                    A(PR[:, :, Z0:Z0 + 512], PR[:, :, Z0:Z0 + 512], ACT.Silu).then_inc(z_exp, 1)
                    for i in range(2 * TT):
                        t, half = divmod(i, 2)
                        act.wait_ge(aq_T, i + 1)
                        A(AQ[:, 3 * half:3 * half + 3, t * P:(t + 1) * P],
                          ps[:, 4 + 2 * (t % 2) + half, 0:3 * P].rearrange("p (a b) -> p a b", b=P), ACT.Copy).then_inc(aq_evac, 1)
                    act.wait_ge(aq_evac, 2 * TT)
                    for u, (s, qt, h) in enumerate(UNITS):
                        n = P * len(key_tiles(s, qt))
                        act.wait_ge(max_done, u + 1)
                        if u >= 2:
                            act.wait_ge(pT_done, u - 1)
                        if u >= 8 and h == 0:
                            act.wait_ge(ob_evac, u // 4 - 1)
                        src = win(u)[:, 0:n] if s == 0 else ps[:, u % 2, 0:n]
                        A(prob(u)[:, 0:n], src, ACT.Exp, scale=SCALE, bias=nmx[:, (u // 4) % 2, h:h + 1],
                          accum_out=psumS[:, (u // 4) % 2, h:h + 1]).then_inc(prob_done, 1)
                        if s == 0 and h == HB - 1:
                            act.wait_ge(sink_in, qt + 1)
                            A(esk[:, (u // 4) % 2, :], esk[:, (u // 4) % 2, :], ACT.Exp).then_inc(sink_exp, 1)
                        act.wait_ge(pT_done, u + 1)
                        if u >= 2:
                            act.wait_ge(pv_done, u - 1)
                        A(probT(u)[:, 0:n], ps[:, 2 + u % 2, 0:n], ACT.Copy).then_inc(pT_evac, 1)
                    act.wait_ge(pv_done, len(UNITS))
                    for m in range(SPLIT):
                        rounds(act, N_IN + m)
                    for k in range(KD):
                        act.wait_ge(mix_T, k + 1)
                        A(MH[:, k, :], ps[:, k, :], ACT.Copy).then_inc(mix_hi, 1)
                    rounds(act, N_IN + 3)


                    act.wait_ge(x_added, 8)
                    for t in range(TT):
                        A(GU[:, 0, :], X[:, t, :], ACT.Square, accum_out=st2[:, t:t + 1]).then_inc(e_sq, 1)
                        act.wait_ge(e_sq, t + 1)
                    act.wait_ge(e_var, 1)
                    A(st2[:, 4:8], st2[:, 0:4], ACT.Sqrt).then_inc(e_std, 1)
                    for t in range(TT):
                        act.wait_ge(h_done, t + 1)
                        A(EH[:, t, :], hw[:, t % 2, :], ACT.Copy).then_inc(e_hi, 1)
                        for half in range(2):
                            act.wait_ge(hT2_done, 2 * t + half + 1)
                            A(HT[:, 4 * half:4 * half + 4, t * P:(t + 1) * P],
                              ps[:, 2 * (t % 2) + half, :].rearrange("p (a b) -> p a b", b=P), ACT.Copy).then_inc(hT2_evac, 1)
                    act.wait_ge(logit_max, 1)
                    A(aff[:, :, :], aff[:, :, :], ACT.Exp).then_inc(logit_exp, 1)

                    def tokens_in(i, part):
                        act.wait_ge(gathered, i * 2 + (part + 1))
                        for e in range(2):
                            last = A(XE[:, 4 * part:4 * part + 4, e, :].rearrange("p k (z c) -> p k z c", z=2),
                                     ps[:, 2 * part:2 * part + 2, :].rearrange("p b (k z e c) -> p (b k) z e c", k=2, z=2, e=2)[:, :, :, e, :], ACT.Copy)
                        last.then_inc(xe_evac, 1)
                    tokens_in(0, 0)
                    tokens_in(0, 1)
                    act.wait_ge(zeroed, 2)
                    with act.Fori(0, PAIRS) as g:
                        def rows_out(j, block):
                            act.wait_ge(m_pass, g * TURN + (SPLIT + 4 * block + 4))
                            A(GU[:, j, :], ps[:, 2 * j:2 * j + 2, :].rearrange("p a b -> p (a b)"), ACT.Copy).then_inc(gu_evac, 1)

                        def gate(n):
                            act.wait_ge(folded, g * 4 + (2 * n + 1))
                            A(SG[:, :, :], ps[:, 4, :].rearrange("p (a b) -> p a b", b=CAP), ACT.Silu).then_inc(sg_done, 1)

                        def hidden_hi(n):
                            act.wait_ge(hm_done, g * 2 + (n + 1))
                            A(HP[:, :, 0:CAP], HM[:, :, :], ACT.Copy).then_inc(hp_hi, 1)

                        def low_share(n, passed):
                            act.wait_ge(m_pass, g * TURN + (SPLIT + passed))
                            A(YT[:, :], ps[CAP:P, 6:8, :].rearrange("p a b -> p (a b)"), ACT.Copy, scale=gate_now[CAP:P, n:n + 1]).then_inc(yt_done, 1)
                        after = {1: [lambda: low_share(1, 0)], 5: [lambda: rows_out(0, 0)], 9: [lambda: rows_out(1, 1)], 11: [lambda: gate(0)],
                                 12: [lambda: hidden_hi(0)], 13: [lambda: rows_out(0, 2)], 17: [lambda: low_share(0, 16)],
                                 21: [lambda: rows_out(1, 4)], 22: [lambda: gate(1), lambda: hidden_hi(1), lambda: tokens_in(g + 1, 0)],
                                 23: [lambda: tokens_in(g + 1, 1)]}
                        for q in range(TURN):
                            expert_rounds(act, g, q)
                            for work_ in after.get(q, ()):
                                work_()
                    act.wait_ge(m_pass, PAIRS * TURN + SPLIT)
                    A(YT[:, :], ps[CAP:P, 6:8, :].rearrange("p a b -> p (a b)"), ACT.Copy, scale=gate_now[CAP:P, 1:2]).then_inc(yt_done, 1)

                @block.vector
                def _(dve):
                    V = nc.vector
                    chained = [0]

                    def step(ins):
                        chained[0] += 1
                        ins.then_inc(v_chain, 1)
                        dve.wait_ge(v_chain, chained[0])
                    dve.wait_ge(x_sq, TT)
                    V.tensor_scalar(ss1[:, :], ss1[:, :], 1.0 / D, EPS, ALU.mult, ALU.add).then_inc(x_var, 1)
                    dve.wait_ge(x_std, 1)
                    step(V.reciprocal(rs1[:, :], rs1[:, :]))
                    for t in range(TT):
                        V.tensor_scalar(XN[:, t, :], X[:, t, :], rs1[:, t:t + 1], None, ALU.mult).then_inc(x_normed, 1)
                    rests(dve, 0)
                    rests(dve, 1)
                    for k in range(KD):
                        dve.wait_ge(hT_hi, k + 1)
                        V.scalar_tensor_tensor(HL[:, k, :], ps[:, k, :], g1[:, k:k + 1], HH[:, k, :],
                                               ALU.mult, ALU.subtract).then_inc(hT_lo, 1)
                    steps = 0
                    for g in range(GROUPS):
                        for n in (2 * g + 2, 2 * g + 3):
                            if n < N_IN:
                                rests(dve, n)
                        if g < 3:
                            for t in range(4):
                                ct = 4 * g + t
                                y = (QT, KT, VD)[g][:, t, :]
                                dve.wait_ge(tap0, ct + 1)
                                for j in range(1, 5):
                                    ins = V.scalar_tensor_tensor(y, XP[:, ct % 2, j:j + SEQ], cw[:, ct, j:j + 1], y, ALU.mult, ALU.add)
                                    if j < 4:
                                        steps += 1
                                        ins.then_inc(conv_step, 1)
                                        dve.wait_ge(conv_step, steps)
                                    else:
                                        ins.then_inc(conv_done, 1)
                    for i in range(8):
                        c, t = divmod(i, TT)
                        dve.wait_ge(tok_sq, i + 1)
                        V.reduce_sum(ssA[:, c, t, :], junk.rearrange("p (a b) -> p a b", b=P), axis=AX).then_inc(tok_ss, 1)
                    dve.wait_ge(tok_ss, 8)
                    V.tensor_scalar(ssA[:, :, :, :], ssA[:, :, :, :], EPS, None, ALU.add).then_inc(qk_var, 1)
                    dve.wait_ge(qk_std, 1)
                    step(V.reciprocal(rsA[:, :, :, :], rsA[:, :, :, :]))
                    step(V.tensor_scalar(rsA[:, 0, :, :], rsA[:, 0, :, :], float(P) ** -0.5, None, ALU.mult))
                    dve.wait_ge(tok_evac, 8)
                    for i in range(8):
                        c, t = divmod(i, TT)
                        dst = (O, KN)[c][:, t, :, :]
                        V.tensor_tensor(dst, dst, bc(rsA[:, c, t, :], 2, [P, HA, P]), ALU.mult).then_inc(qk_normed, 1)
                    dve.wait_ge(proj_evac, 4 * GROUPS)
                    dve.wait_ge(par_in, 32)
                    step(V.tensor_tensor(zb[:, :, :], PR[:, :, BA0 + 8:BA0 + 16], bc(dt_b, 1, [P, TT, 8]), ALU.add))
                    V.scalar_tensor_tensor(tb[:, :, :], zb[:, :, :], -1.0, zb[:, :, :], ALU.mult, ALU.max).then_inc(gate_z, 1)
                    dve.wait_ge(gate_e, 3)
                    step(V.tensor_scalar(beta[:, :, :], beta[:, :, :], 1.0, None, ALU.add))
                    V.reciprocal(beta[:, :, :], beta[:, :, :])
                    V.tensor_scalar(tb[:, :, :], eb[:, :, :], 1.0, None, ALU.add).then_inc(gate_w, 1)
                    dve.wait_ge(gate_w, 1)
                    step(V.scalar_tensor_tensor(eb[:, :, :], tb[:, :, :], -1.0, eb[:, :, :], ALU.add, ALU.subtract))
                    dve.wait_ge(gate_ln, 1)
                    step(V.reciprocal(tb[:, :, :], tb[:, :, :]))
                    step(V.tensor_tensor(eb[:, :, :], eb[:, :, :], tb[:, :, :], ALU.mult))
                    step(V.tensor_tensor(lb[:, :, :], lb[:, :, :], eb[:, :, :], ALU.subtract))
                    step(V.scalar_tensor_tensor(zb[:, :, :], zb[:, :, :], 0.0, lb[:, :, :], ALU.max, ALU.add))
                    V.scalar_tensor_tensor(gdec[:, :, :], zb[:, :, :], -1.0, bc(ea[:, :], 1, [P, TT, 8]), ALU.mult, ALU.mult).then_inc(g_ready, 1)
                    dve.wait_ge(cum_done, 1)
                    four = dict(b=TT, c=HA)
                    V.tensor_copy(gcc[:, :, :, :], ps[:, 0, 0:32].rearrange("p (a b c) -> p a b c", **four))
                    V.tensor_copy(gll[:, :, :, :], ps[:, 0, 32:64].rearrange("p (a b c) -> p a b c", **four)).then_inc(cum_evac, 1)
                    dve.wait_ge(cum_evac, 1)
                    V.tensor_tensor(kdc[:, :, :, :], gll[:, :, :, :], gcc[:, :, :, :], ALU.subtract).then_inc(cum_diff, 1)
                    for t in range(TT):
                        for d in range(2):
                            i = 2 * t + d
                            B, b0 = delta[d], 4 * d
                            dve.wait_ge(eg_exp, i + 1)
                            if t > 0:
                                dve.wait_ge(nt_base, i - 1)
                            for h in range(HA):
                                last = V.tensor_scalar(B["DM"][:, h, :], ps[:, b0, h * P:(h + 1) * P],
                                                       gcc[:, d, tile_of(d, t), h:h + 1], 0.0, ALU.subtract, ALU.min)
                            last.then_inc(diff_done, 1)
                        for d in range(2):
                            i = 2 * t + d
                            B, b0 = delta[d], 4 * d
                            tl = tile_of(d, t)
                            tok = slice(tl * P, (tl + 1) * P)
                            dve.wait_ge(gram_done, i + 1)
                            dve.wait_ge(masked, i + 1)
                            if t > 0:
                                dve.wait_ge(o_done, i - 1)
                            V.tensor_tensor(B["AT"][:, :, :], ps[:, b0 + 1, :].rearrange("p (a b) -> p a b", b=P), B["DM"][:, :, :], ALU.mult).then_inc(at_done, 1)
                            dve.wait_ge(nt_base, i + 1)
                            V.tensor_tensor(B["NT"][:, :, :], ps[:, b0 + 2, :].rearrange("p (a b) -> p a b", b=P), B["NT"][:, :, :], ALU.mult).then_inc(nt_done, 1)
                            dve.wait_ge(eg_exp, i + 1)
                            dve.wait_ge(back_evac, 4)
                            V.tensor_tensor(B["QG"][:, :, :], B["QG"][:, :, :], QT[:, :, tok], ALU.mult).then_inc(qg_done, 1)
                        for d in range(2):
                            i = 2 * t + d
                            B, b0 = delta[d], 4 * d
                            dve.wait_ge(nm_done, 14 * t + d + 1)
                            if t > 0:
                                dve.wait_ge(v_done, i - 1)
                            V.tensor_tensor(B["TTr"][:, :, :], bc(ident[:, :], 1, [P, HA, P]), B["NM"][:, :, :], ALU.subtract).then_inc(t0_done, 1)
                        for l in range(1, 7):
                            for d in range(2):
                                i = 2 * t + d
                                c = (6 * t + l - 1) * 2 + d
                                B, b0 = delta[d], 4 * d
                                dve.wait_ge(y_done, c + 1)
                                if l == 1:
                                    dve.wait_ge(t0_evac, i + 1)
                                if l < 6:
                                    V.tensor_tensor(B["T"][:, :, :], B["T"][:, :, :], ps[:, b0 + 1, :].rearrange("p (a b) -> p a b", b=P), ALU.subtract).then_inc(t_new, 1)
                                V.tensor_tensor(B["TTr"][:, :, :], B["TTr"][:, :, :], ps[:, b0 + 2, :].rearrange("p (a b) -> p a b", b=P), ALU.subtract).then_inc(t_new, 1 if l < 6 else 2)
                        for d in range(2):
                            i = 2 * t + d
                            B, b0 = delta[d], 4 * d
                            tl = tile_of(d, t)
                            dve.wait_ge(v_done, i + 1)
                            if t > 0:
                                dve.wait_ge(s_done, i - 1)
                            V.tensor_tensor(B["VN"][:, :, :], ps[:, b0 + 1, :].rearrange("p (a b) -> p a b", b=P),
                                            bc(beta[:, tl, d * HA:(d + 1) * HA], 2, [P, HA, P]), ALU.mult).then_inc(vn_done, 1)
                        for d in range(2):
                            i = 2 * t + d
                            B, b0 = delta[d], 4 * d
                            tl = tile_of(d, t)
                            dve.wait_ge(o_done, i + 1)
                            o = ps[:, b0 + 2, :].rearrange("p (a b) -> p a b", b=P)
                            if t < TT // 2:
                                if i == 0:
                                    dve.wait_ge(back_T, 4)
                                V.tensor_copy(O[:, tl, :, :], o).then_inc(o_evac, 1)
                            else:
                                dve.wait_ge(o_evac, 4)
                                V.tensor_tensor(O[:, tl, :, :], O[:, tl, :, :], o, ALU.add).then_inc(o_evac, 1)
                            if t < TT - 1:
                                dve.wait_ge(s_done, i + 1)
                                dve.wait_ge(s_dec, i + 1)
                                V.tensor_tensor(S[:, d, :, :], S[:, d, :, :], ps[:, b0 + 3, :].rearrange("p (a b) -> p a b", b=P), ALU.add).then_inc(s_new, 1)
                    dve.wait_ge(o_evac, 8)
                    sq = AW[:, :, :].rearrange("p a b -> p (a b)")[:, 0:TT * 512]
                    flatO = O[:, :, :, :].rearrange("p t h c -> p (t h c)")
                    step(V.tensor_tensor(sq, flatO, flatO, ALU.mult))
                    step(V.reduce_sum(ssO[:, :, :].rearrange("p a b -> p (a b)"), sq.rearrange("p (a b) -> p a b", b=P), axis=AX))
                    step(V.tensor_scalar(ssO[:, :, :], ssO[:, :, :], 1.0 / P, EPS, ALU.mult, ALU.add))

                    def qk(t):
                        return PR[:, t, AT0:AT0 + 1024].rearrange("p (s c) -> p s c", s=2)[:, :, 0:VOFF].rearrange("p s (a b) -> p s a b", b=HD)
                    for t in range(TT):
                        w = AW[:, t % 3, :]
                        step(V.tensor_tensor(w.rearrange("p (s a b) -> p s a b", s=2, b=HD), qk(t), qk(t), ALU.mult))
                        step(V.reduce_sum(ssR[:, t, :], w.rearrange("p (a b) -> p a b", b=HD), axis=AX))
                    V.tensor_scalar(ssR[:, :, :], ssR[:, :, :], 1.0 / HD, EPS, ALU.mult, ALU.add).then_inc(oa_var, 1)
                    dve.wait_ge(r_std, 1)
                    step(V.reciprocal(rsR[:, :, :], rsR[:, :, :]))
                    for t in range(TT):
                        r = rsR[:, t, :].rearrange("p (s a) -> p s a", s=2)
                        step(V.tensor_tensor(qk(t), qk(t), bc(r, 3, [P, 2, 6, HD]), ALU.mult))
                        if t == 0:
                            dve.wait_ge(gain_set, 1)
                        V.tensor_tensor(qk(t), qk(t), GN[:, :, :].rearrange("p (s a) b -> p s a b", s=2), ALU.mult).then_inc(r_normed, 1)
                    step(V.reciprocal(rsO[:, :, :], rsO[:, :, :]))
                    O3 = O[:, :, :, :].rearrange("p t h c -> p (t h) c")
                    step(V.tensor_tensor(O3, O3, bc(rsO[:, :, :].rearrange("p a b -> p (a b)"), 2, [P, TT * HA, P]), ALU.mult))
                    step(V.tensor_tensor(O3, O3, bc(a_norm, 1, [P, TT * HA, P]), ALU.mult))
                    dve.wait_ge(z_exp, 1)
                    V.tensor_tensor(O[:, :, :, :].rearrange("p t h c -> p t (h c)"), O[:, :, :, :].rearrange("p t h c -> p t (h c)"),
                                    PR[:, :, Z0:Z0 + 512], ALU.mult).then_inc(oa_done, 1)
                    step(V.tensor_scalar(nsink[:, :], sink, -1.0, None, ALU.mult))

                    def finish(G):
                        s, qt = divmod(G, TT)
                        r = G % 2
                        dve.wait_ge(pv_done, 4 * G + 4)
                        if s == 0:
                            dve.wait_ge(sink_exp, qt + 1)
                            step(V.tensor_tensor(rinv[:, r, :], psumS[:, r, :], esk[:, r, :], ALU.add))
                            step(V.reciprocal(rinv[:, r, :], rinv[:, r, :]))
                        else:
                            step(V.reciprocal(rinv[:, r, :], psumS[:, r, :]))
                        V.tensor_tensor(OB[:, qt, s * 256:(s + 1) * 256].rearrange("p (a b) -> p a b", b=HD),
                                        ps[:, 4 + G % 2, 0:256].rearrange("p (a b) -> p a b", b=HD),
                                        bc(rinv[:, r, :], 2, [P, HB, HD]), ALU.mult).then_inc(ob_evac, 1)
                    for u, (s, qt, h) in enumerate(UNITS):
                        kts = key_tiles(s, qt)
                        n = P * len(kts)
                        r = (u // 4) % 2
                        dve.wait_ge(score_done, u + 1)
                        if u >= 2:
                            dve.wait_ge(prob_done, u - 1)
                        src = ps[:, u % 2, 0:n]
                        if s == 0:
                            off = (kts[0] - qt + 1) * P
                            V.tensor_tensor(win(u)[:, 0:n], src, window[:, off:off + n], ALU.add).then_inc(win_done, 1)
                            dve.wait_ge(win_done, u + 1)
                            src = win(u)[:, 0:n]
                        step(V.reduce_max(rmax[:, u % 2:u % 2 + 1], src, axis=AX))
                        V.tensor_scalar(nmx[:, r, h:h + 1], rmax[:, u % 2:u % 2 + 1], -SCALE, nsink[:, h:h + 1] if s == 0 else None,
                                        ALU.mult, *((ALU.min,) if s == 0 else ())).then_inc(max_done, 1)
                        if s == 0 and h == HB - 1:
                            dve.wait_ge(max_done, u + 1)
                            V.tensor_tensor(esk[:, r, :], nmx[:, r, :], sink, ALU.add).then_inc(sink_in, 1)
                        if u % 4 == 1 and u > 4:
                            finish(u // 4 - 1)
                    finish(2 * TT - 1)
                    for m in range(SPLIT):
                        rests(dve, N_IN + m)
                    for k in range(KD):
                        dve.wait_ge(mix_hi, k + 1)
                        V.tensor_tensor(ML[:, k, :], ps[:, k, :], MH[:, k, :], ALU.subtract).then_inc(mix_lo, 1)
                    rests(dve, N_IN + 3)
                    for b in range(8):
                        t, half = divmod(b, 2)
                        dve.wait_ge(passes, 4 * N_IN + 8 * (N_OUT - 1) + b + 1)
                        xs = X[:, t, half * 512:(half + 1) * 512]
                        V.tensor_tensor(xs, xs, ps[:, b, :], ALU.add).then_inc(x_added, 1)

                    dve.wait_ge(e_sq, TT)
                    V.tensor_scalar(st2[:, 0:4], st2[:, 0:4], 1.0 / D, EPS, ALU.mult, ALU.add).then_inc(e_var, 1)
                    dve.wait_ge(e_in, 64)
                    dve.wait_ge(e_std, 1)
                    step(V.reciprocal(st2[:, 4:8], st2[:, 4:8]))
                    for t in range(TT):
                        if t >= 2:
                            dve.wait_ge(hT2_done, 2 * (t - 1))
                            dve.wait_ge(e_hi, t - 1)
                        V.scalar_tensor_tensor(hw[:, t % 2, :], X[:, t, :], st2[:, 4 + t:5 + t], norm2_row[:, :], ALU.mult, ALU.mult).then_inc(h_done, 1)
                        dve.wait_ge(e_hi, t + 1)
                        V.tensor_tensor(EL[:, t, :], hw[:, t % 2, :], EH[:, t, :], ALU.subtract).then_inc(e_lo, 1)
                    dve.wait_ge(logit_done, 1)
                    lg = ps[:, 4, 0:TT * NE].rearrange("p (a b) -> p a b", b=NE)
                    step(V.reduce_max(st2[:, 8:12], lg, axis=AX))
                    V.tensor_tensor(aff[:, :, :], lg, bc(st2[:, 8:12], 2, [P, TT, NE]), ALU.subtract).then_inc(logit_max, 1)
                    dve.wait_ge(logit_exp, 1)
                    step(V.reduce_sum(st2[:, 12:16], aff[:, :, :], axis=AX))
                    step(V.reciprocal(st2[:, 12:16], st2[:, 12:16]))
                    V.tensor_tensor(aff[:, :, :], aff[:, :, :], bc(st2[:, 12:16], 2, [P, TT, NE]), ALU.mult).then_inc(aff_done, 1)
                    dve.wait_ge(affT_done, 1)
                    step(V.tensor_copy(work[:, :], ps[0:NE, 5, :]))
                    for r in range(CAP // 8):
                        b = slice(8 * r, 8 * r + 8)
                        step(V.max(best[:, b], work[:, :]))
                        step(V.max_index(best_at[:, b], best[:, b], work[:, :]))
                        if r < CAP // 8 - 1:
                            step(V.match_replace(work[:, :], best[:, b], work[:, :], -1.0))
                    step(V.tensor_copy(twice[:, 0, 0, :], best_at[:, :]))
                    V.tensor_copy(twice[:, 0, 1, :], twice[:, 0, 0, :])
                    V.tensor_copy(twice[:, 1, :, :], bc(best[:, :], 1, [NE, 2, CAP])).then_inc(chosen, 1)
                    V.tensor_tensor(spread[:, :, :], bc(twice[:, 0, 0, :], 1, [NE, NE, CAP]), bc(ident[0:NE, 0:NE], 2, [NE, NE, CAP]), ALU.mult).then_inc(spread_done, 1)
                    dve.wait_ge(chosen_T, 1)
                    pair = ps[:, 6, 0:NE].rearrange("p (g e) -> p g e", e=2)
                    V.tensor_copy(slot_tok[0:CAP, :], pair[0:CAP, :, 0])
                    V.tensor_copy(slot_tok[CAP:P, :], pair[CAP:P, :, 1])
                    V.tensor_copy(slot_gate[:, :], ps[:, 6, NE:2 * NE])
                    dve.wait_ge(rows_done, 1)
                    V.tensor_copy(idx_rows[:, NE * CAP:], ps[:, 0, 0:2 * CAP])
                    V.tensor_copy(idx_rows[:, 0:NE * CAP], ps[:, 0:2, :].rearrange("p a b -> p (a b)")).then_inc(top_ready, 1)
                    dve.wait_ge(top_ready, 1)

                    def choose(columns):
                        for t in range(TT):
                            last = V.tensor_scalar(sel[:, t, :], idx_rows[:, columns], tokid[:, t:t + 1], None, ALU.is_equal)
                        last.then_inc(sel_done, 1)
                    choose(slice(0, 2 * CAP))
                    V.tensor_copy(gate_now[:, :], slot_gate[:, 0:2])
                    V.tensor_scalar(selT[:, :], iota[:, :], -1.0, None, ALU.is_equal).then_inc(selT_done, 1)
                    for half in range(2):
                        last = V.tensor_scalar(YE[:, half * 512:(half + 1) * 512], iota[:, :], -1.0, None, ALU.is_equal)
                    last.then_inc(ye_done, 1)

                    def to_tokens(g, ns):
                        for n in ns:
                            t, half = divmod(n, 2)
                            dve.wait_ge(scattered, g * 8 + (n + 1))
                            xs = X[:, t, half * 512:(half + 1) * 512]
                            V.tensor_tensor(xs, xs, ps[:, 4 + n % 4, :], ALU.add).then_inc(x_added, 1)
                    with dve.Fori(0, PAIRS) as g:
                        def hidden(n):
                            dve.wait_ge(sg_done, g * 2 + (n + 1))
                            dve.wait_ge(folded, g * 4 + (2 * n + 2))
                            V.tensor_tensor(HM[:, :, :], SG[:, :, :], ps[:, 5, :].rearrange("p (a b) -> p a b", b=CAP), ALU.mult).then_inc(hm_done, 1)

                        def hidden_lo(n):
                            dve.wait_ge(hp_hi, g * 2 + (n + 1))
                            V.tensor_tensor(HP[:, :, CAP:P], HM[:, :, :], HP[:, :, 0:CAP], ALU.subtract).then_inc(hp_lo, 1)

                        def output(n):
                            dve.wait_ge(yt_done, g * 2 + (2 - n))
                            V.scalar_tensor_tensor(YE[n * CAP:(n + 1) * CAP, :], ps[0:CAP, 6:8, :].rearrange("p a b -> p (a b)"),
                                                   gate_now[0:CAP, n:n + 1], YT[:, :], ALU.mult, ALU.add).then_inc(ye_done, 1)

                        def next_choice():
                            dve.wait_ge(gathered, g * 2 + 2)
                            choose(bass.ds(g * P + P, P))

                        def tokens_of_slots():
                            V.tensor_scalar(selT[:, :], iota[:, :], slot_tok[:, bass.ds(g, 1)], None, ALU.is_equal).then_inc(selT_done, 1)
                        def last_pair():
                            output(1)
                            dve.wait_ge(ye_done, g * 2 + 2)
                            V.tensor_copy(gate_now[:, :], slot_gate[:, bass.ds(g * 2, 2)])
                        after = {1: [last_pair], 4: [lambda: to_tokens(g, (0, 1))], 5: [lambda: to_tokens(g, (2, 3))],
                                 8: [lambda: to_tokens(g, (4, 5))], 9: [lambda: to_tokens(g, (6, 7)), tokens_of_slots], 11: [lambda: hidden(0)], 12: [lambda: hidden_lo(0)], 14: [next_choice],
                                 17: [lambda: output(0)], 22: [lambda: hidden(1), lambda: hidden_lo(1)]}
                        for q in range(TURN):
                            if not by_pool(q):
                                expert_rests(dve, g, q)
                            for work_ in after.get(q, ()):
                                work_()
                    dve.wait_ge(yt_done, PAIRS * 2 + 1)
                    V.scalar_tensor_tensor(YE[CAP:P, :], ps[0:CAP, 6:8, :].rearrange("p a b -> p (a b)"),
                                           gate_now[0:CAP, 1:2], YT[:, :], ALU.mult, ALU.add).then_inc(ye_done, 1)
                    to_tokens(PAIRS, range(8))

                @block.gpsimd
                def _(pool):
                    G = nc.gpsimd
                    chained = [0]

                    def step(ins):
                        chained[0] += 1
                        ins.then_inc(p_chain, 1)
                        pool.wait_ge(p_chain, chained[0])
                    G.memset(XP[:, :, 0:2], 0.0)
                    G.memset(XP[:, :, SEQ + 2:SEQ + 4], 0.0).then_inc(pad_set, 1)
                    pool.wait_ge(par_in, 32)
                    at = 0
                    for j, heads in enumerate((4, 2, 4, 2)):
                        last = G.tensor_copy(GN[:, at:at + heads, :], bc(gains[:, j, :], 1, [P, heads, HD]))
                        at += heads
                    last.then_inc(gain_set, 1)
                    pool.wait_ge(tok_T, 12)
                    G.memset(S[:, :, :, :], 0.0).then_inc(s_zero, 1)
                    pool.wait_ge(s_zero, 1)
                    pool.wait_ge(const_in, 5 * 16)
                    pool.wait_ge(g_ready, 1)
                    pool.wait_ge(proj_evac, 4 * GROUPS)
                    for t in range(TT):
                        for d in range(2):
                            i = 2 * t + d
                            B = delta[d]
                            if t > 0:
                                pool.wait_ge(x_done, 12 * t + d - 1)
                            G.tensor_tensor(B["NM"][:, :, :], bc(cum[:, d, :], 1, [P, HA, P]),
                                            bc(gdec[:, tile_of(d, t), d * HA:(d + 1) * HA], 2, [P, HA, P]), ALU.mult).then_inc(gu_ready, 1)
                        for d in range(2):
                            i = 2 * t + d
                            tl = tile_of(d, t)
                            B = delta[d]
                            pool.wait_ge(dm_exp, i + 1)
                            G.tensor_tensor(B["DM"][:, :, :], B["DM"][:, :, :], bc(cum[:, d, :], 1, [P, HA, P]), ALU.mult).then_inc(masked, 1)
                            pool.wait_ge(masked, i + 1)
                            G.tensor_tensor(B["NT"][:, :, :], B["DM"][:, :, :], bc(beta[:, tl, d * HA:(d + 1) * HA], 2, [P, HA, P]), ALU.mult).then_inc(nt_base, 1)
                        for l in range(7):
                            for d in range(2):
                                i = 2 * t + d
                                B = delta[d]
                                if l == 0:
                                    pool.wait_ge(nt_done, i + 1)
                                    pool.wait_ge(row_done, i + 1)
                                elif l == 1:
                                    pool.wait_ge(t0_done, i + 1)
                                else:
                                    pool.wait_ge(x_done, (6 * t + l - 2) * 2 + d + 1)
                                G.tensor_tensor(B["NM"][:, :, :], B["NT"][:, :, :], bc(level[:, l, :], 1, [P, HA, P]), ALU.mult).then_inc(nm_done, 1)
                            if l == 1:
                                for d in range(2):
                                    i = 2 * t + d
                                    tl = tile_of(d, t)
                                    B = delta[d]
                                    pool.wait_ge(cum_exp, 1)
                                    pool.wait_ge(qk_normed, 8)
                                    if t > 0:
                                        pool.wait_ge(w_done, i - 1)
                                        pool.wait_ge(s_done, i - 1)
                                    G.tensor_tensor(B["KG"][:, :, :], KN[:, tl, :, :], bc(egc[:, d, tl, :], 2, [P, HA, P]), ALU.mult).then_inc(kgd_done, 1)
                                    G.tensor_tensor(B["KD"][:, :, :], KN[:, tl, :, :], bc(kdc[:, d, tl, :], 2, [P, HA, P]), ALU.mult).then_inc(kgd_done, 1)
                        if t < TT - 1:
                            for d in range(2):
                                i = 2 * t + d
                                pool.wait_ge(o_done, i + 1)
                                if t > 0:
                                    pool.wait_ge(s_new, i - 1)
                                G.tensor_tensor(S[:, d, :, :], S[:, d, :, :], bc(egl[:, d, tile_of(d, t), :], 2, [P, HA, P]), ALU.mult).then_inc(s_dec, 1)
                    for t in range(TT):
                        pool.wait_ge(r_normed, t + 1)
                        if t > 0:
                            pool.wait_ge(rope_done, t)
                        q = PR[:, t, AT0:AT0 + 1024].rearrange("p (s c) -> p s c", s=2)
                        for s in range(2):
                            src = q[:, s, 0:VOFF].rearrange("p (a b) -> p a b", b=HD)
                            c_ = AW[:, 1, s * VOFF:(s + 1) * VOFF].rearrange("p (a b) -> p a b", b=HD)
                            r_ = AW[:, 2, s * VOFF:(s + 1) * VOFF]
                            G.tensor_tensor(c_, src, bc(cosT[:, s, t, :], 1, [P, 6, HD]), ALU.mult)
                            w = HD // 2 if s == 0 else HD // 4
                            m = HD // (2 * w)
                            srcv = q[:, s, 0:VOFF].rearrange("p (a m z w) -> p a m z w", m=m, z=2, w=w)
                            dstv = r_.rearrange("p (a m z w) -> p a m z w", m=m, z=2, w=w)
                            sinv = sinT[:, s, t, :].rearrange("p (m z w) -> p m z w", z=2, w=w)
                            for z in range(2):
                                a, b, c = dstv[:, :, :, z, :], srcv[:, :, :, 1 - z, :], sinv[:, :, z, :]
                                last = G.tensor_tensor(a, b, bc(c, 1, [P, 6, m, w]), ALU.mult)
                        step(last)
                        if t > 0:
                            pool.wait_ge(aq_T, 2 * t)
                        for s in range(2):
                            c_ = AW[:, 1, s * VOFF:(s + 1) * VOFF].rearrange("p (a b) -> p a b", b=HD)
                            r_ = AW[:, 2, s * VOFF:(s + 1) * VOFF].rearrange("p (a b) -> p a b", b=HD)
                            o_ = AW[:, 0, s * VOFF:(s + 1) * VOFF].rearrange("p (a b) -> p a b", b=HD)
                            G.tensor_tensor(o_[:, 0:4, :].rearrange("p (j i) b -> p i j b", j=2),
                                            c_[:, 0:4, :].rearrange("p (i j) b -> p i j b", i=2),
                                            r_[:, 0:4, :].rearrange("p (i j) b -> p i j b", i=2), ALU.add)
                            last = G.tensor_tensor(o_[:, 4:6, :], c_[:, 4:6, :], r_[:, 4:6, :], ALU.add)
                        last.then_inc(rope_done, 1)
                    pool.wait_ge(x_added, 8)
                    G.tensor_tensor(fold[:, :], ident[:, 0:CAP], ident[:, CAP:P], ALU.add).then_inc(fold_set, 1)
                    with pool.Fori(0, PAIRS) as g:
                        for q in range(TURN):
                            if by_pool(q):
                                expert_rests(pool, g, q)
            nc.all_engine_barrier(sems_to_clear=range(raw_full[0].num, slot_free.num + 1))
        with nc.Block() as block:
            @block.sync
            def _(sp):
                sp.dma_start(out.rearrange("o (t p) d -> p (o t) d", p=P), X[:, :, :]).then_inc(s_out, 16)
                sp.wait_ge(s_out, 16)


_INS = ["x", "rows", "cols", "norm2", "w_in", "w_out", "w_router", "w_gate", "w_up", "w_down", "consts"]
_OUTS = [((1, SEQ, D), "float32")]


def kernel(**inputs):
    import numpy as _np
    import concourse.bacc as _bacc
    from concourse import mybir as _mybir
    from concourse.bass_utils import run_bass_kernel_spmd as _run

    i = {k: _np.asarray(v) for k, v in inputs.items()}
    laid = {k: i[k] for k in ("x", "w_in", "w_out", "w_router", "w_gate", "w_up", "w_down")}
    laid["rows"] = _np.concatenate([i["a_log"].reshape(LAYERS, -1), i["dt_bias"].reshape(LAYERS, -1), i["a_norm_g"],
                                    i["b_qnorm_g"], i["b_knorm_g"], i["c_qnorm_g"], i["c_knorm_g"], i["b_sink"]], 1)
    laid["cols"] = _np.concatenate([i["norm1_g"].reshape(LAYERS, KD, P).transpose(0, 2, 1),
                                    i["conv_w"].reshape(LAYERS, 5, NQKV, P).transpose(0, 3, 2, 1).reshape(LAYERS, P, -1)], 2)
    laid["norm2"] = i["norm2_g"]
    laid["consts"] = constants()
    nc = _bacc.Bacc("TRN2", target_bir_lowering=False, num_devices=1)
    arrays, args = {}, []
    for name in _INS:
        a = _np.ascontiguousarray(laid[name])
        arrays[f"in_{name}_dram"] = a
        args.append(nc.dram_tensor(f"in_{name}_dram", a.shape, _mybir.dt.from_np(a.dtype), kind="ExternalInput").ap())
    for n, (shape, dtype) in enumerate(_OUTS):
        args.append(nc.dram_tensor(f"out_{n}_dram", shape, _mybir.dt.from_np(_np.dtype(dtype)), kind="ExternalOutput").ap())
    bass_hybrid_encoder(nc, *args)
    r = _run(nc, [arrays], core_ids=[0])
    return r.results[0]["out_0_dram"]
```

```python
from contextlib import ExitStack

import numpy as np

import concourse.bass as bass
from concourse import mybir

ALU = mybir.AluOpType
ACT = mybir.ActivationFunctionType
F32 = mybir.dt.float32
F32R = mybir.dt.float32r
U32 = mybir.dt.uint32
AX = mybir.AxisListType.X

P = 128
EPS = 1e-6

LAYERS = 2
SEQ = 512
D = 1024
TT = SEQ // P
KD = D // P
HA = 4
NQKV = 3 * HA
PROJ = 3088
REST = PROJ - NQKV * P
HD = 64
HB = 4
NSLOT = 12
NE = 16
CAP = 2 * SEQ // NE
DE = 1024
Z0, BA0, AT0 = 0, 512, 528
VOFF = 384

GROUPS = 7
FIRST_QKV = 3
REST_OF = {0: 1, 1: 2, 2: 3, 6: 0}
RW = REST // 4
PIECE = 2048
RAW_A = 3
SPLIT = 3
N_IN = 2 * GROUPS
N_OUT = 4
SCALE = HD ** -0.5
RAW_M = 6
SPLIT_M = 4
PAIRS = NE // 2
PER = 12
TURN = 2 * PER
GATE, UP, DOWN = range(3)
STREAM = [(GATE, 0), (UP, 0), (GATE, 1), (DOWN, 0), (UP, 1), (DOWN, 1)]
BY_POOL = (3, 9, 15, 21)
LOADS_A = (N_IN + N_OUT) // RAW_A

CONST_COLS = dict(ident=P, cum=2 * P, level=7 * P, window=3 * P, cos=2 * TT * HD, sin=2 * TT * HD,
                  iota=SEQ, tokid=TT)


def constants():
    p = np.arange(P)
    c = {"ident": np.eye(P)}
    c["cum"] = np.stack([p[:, None] <= p[None, :], p[:, None] >= p[None, :]], 1).reshape(P, -1)
    c["level"] = np.stack([(p[:, None] >> (l + 1) == p[None, :] >> (l + 1))
                           & (p[:, None] >> l != p[None, :] >> l) for l in range(7)], 1).reshape(P, -1)
    w = np.zeros((P, 3, P))
    w[:, 0] = np.where(p[None, :] >= p[:, None], 0.0, -1e30)
    w[:, 2] = np.where(p[None, :] <= p[:, None], 0.0, -1e30)
    c["window"] = w.reshape(P, -1)
    f = np.float32

    def table(pos, dim):
        inv = f(10000.0) ** (-np.arange(0, dim, 2, dtype=f) / f(dim))
        ang = pos.astype(f)[:, None] * inv[None, :]
        sign = np.concatenate([-np.ones(dim // 2), np.ones(dim // 2)])
        ang = np.concatenate([ang, ang], -1)
        return np.cos(ang), np.sin(ang) * sign
    pos = np.arange(SEQ)
    one, row, col = table(pos, HD), table(pos // 64, HD // 2), table(pos % 64, HD // 2)
    for n, key in enumerate(("cos", "sin")):
        t = np.stack([one[n], np.concatenate([row[n], col[n]], -1)], 1)
        c[key] = t.reshape(TT, P, 2, HD).transpose(1, 2, 0, 3).reshape(P, -1)
    c["iota"] = np.broadcast_to(np.arange(SEQ), (P, SEQ))
    c["tokid"] = p[:, None] + P * np.arange(TT)[None, :]
    return np.concatenate([c[k].astype(f) for k in CONST_COLS], 1)


def const_at(name):
    at = 0
    for k, n in CONST_COLS.items():
        if k == name:
            return at, n
        at += n


ROW_COLS = dict(a_log=8, dt_bias=8, a_norm=P, gains=4 * HD, sink=HB)
ROWS = sum(ROW_COLS.values())
COLS = KD + NQKV * 5


def bc(ap, axis, shape):
    return ap.unsqueeze(axis).to_broadcast(shape)


def bass_hybrid_encoder(nc, x, rows, cols, norm2, w_in, w_out, w_router, w_gate, w_up, w_down, consts, out):
    ctx = ExitStack()
    with ctx:
        def sem(name):
            return ctx.enter_context(nc.semaphore(name))

        def sb(name, shape, dt=F32, at=None):
            return (at or ctx).enter_context(nc.sbuf_tensor(name, shape, dt))

        X = sb("X", [P, TT, D])
        ident = sb("ident", [P, P])
        ones = sb("ones", [P, P])
        row = sb("row", [P, ROWS])
        col = sb("col", [P, COLS])
        raw = [sb(f"raw{i}", [P, PIECE]) for i in range(RAW_A)]
        one = ExitStack()
        delta = [{n: sb(f"{n}{d}", [P, HA, P], at=one)
                  for n in ("DM", "NT", "NM", "T", "TTr", "XS", "AT", "WT", "QG", "KD", "KG", "VN")}
                 for d in range(2)]
        one.close()
        whi = [sb(f"whi{i}", [P, PIECE], F32R) for i in range(SPLIT)]
        wlo = [sb(f"wlo{i}", [P, PIECE], F32R) for i in range(SPLIT)]
        mixer = ExitStack()
        one = ExitStack()
        QT, KT = (sb(n, [P, HA, SEQ], at=one) for n in ("QT", "KT"))
        KN, VN_ = (sb(n, [P, TT, HA, P], at=one) for n in ("KN", "VA"))
        one.close()
        MH, ML = (sb(n, [P, KD, SEQ], F32R, at=mixer) for n in ("MH", "ML"))
        one = ExitStack()
        HH, HL = (sb(n, [P, KD, SEQ], F32R, at=one) for n in ("HH", "HL"))
        one.close()
        one = ExitStack()
        SQ = sb("SQ", [P, 2, HA * P], at=one)
        one.close()
        AQH, AQL = (sb(n, [P, 6, SEQ], F32R, at=mixer) for n in ("AQH", "AQL"))
        O = sb("O", [P, TT, HA, P], at=mixer)
        one = ExitStack()
        XN = sb("XN", [P, TT, D], at=one)
        one.close()
        PR = sb("PR", [P, TT, REST], at=mixer)
        one = ExitStack()
        XP = sb("XP", [P, 2, SEQ + 4], at=one)
        VD = sb("VD", [P, HA, SEQ], at=one)
        one.close()
        OB = sb("OB", [P, TT, 2 * HB * HD], at=mixer)
        S = sb("S", [P, 2, HA, P], at=mixer)
        sb("conv_rest", [P, 8], at=mixer)
        cum = sb("cum", [P, 2, P], at=mixer)
        level = sb("level", [P, 7, P], at=mixer)
        window = sb("window", [P, 3 * P], at=mixer)
        cosT = sb("cosT", [P, 2, TT, HD], at=mixer)
        sinT = sb("sinT", [P, 2, TT, HD], at=mixer)
        GN = sb("GN", [P, NSLOT, HD], at=mixer)
        st = sb("st", [P, 640], at=mixer)
        mixer.close()
        raw += [sb(f"raw{i}", [P, PIECE]) for i in range(RAW_A, RAW_M)]
        whi += [sb(f"whi{i}", [P, PIECE], F32R) for i in range(SPLIT, SPLIT_M)]
        wlo += [sb(f"wlo{i}", [P, PIECE], F32R) for i in range(SPLIT, SPLIT_M)]
        EH, EL = (sb(n, [P, TT, D], F32R) for n in ("EH", "EL"))
        idx_rows = sb("idx_rows", [P, (NE + 2) * CAP])
        sel = sb("sel", [P, TT, 2 * CAP], F32R)
        one = ExitStack()
        norm2_row = sb("norm2_row", [P, D], at=one)
        router = sb("router", [P, KD, NE], at=one)
        one.close()
        XE = sb("XE", [P, KD, 2, P], F32R)
        selT = sb("selT", [P, SEQ])
        one = ExitStack()
        HT = sb("HT", [P, KD, SEQ], at=one)
        one.close()
        one = ExitStack()
        aff = sb("aff", [P, TT, NE], at=one)
        work = sb("work", [NE, SEQ], at=one)
        best = sb("best", [NE, CAP], at=one)
        best_at = sb("best_at", [NE, CAP], U32, at=one)
        twice = sb("twice", [NE, 2, 2, CAP], at=one)
        spread = sb("spread", [NE, NE, CAP], at=one)
        one.close()
        GU = sb("GU", [P, 2, DE])
        YT = sb("YT", [CAP, D])
        YE = sb("YE", [P, D])
        one = ExitStack()
        hw = sb("hw", [P, 2, D], at=one)
        one.close()
        SG = sb("SG", [P, DE // P, CAP])
        HM = sb("HM", [P, DE // P, CAP])
        HP = sb("HP", [P, DE // P, P], F32R)
        iota = sb("iota", [P, SEQ])
        tokid = sb("tokid", [P, TT])
        fold = sb("fold", [P, CAP])
        slot_tok = sb("slot_tok", [P, PAIRS])
        slot_gate = sb("slot_gate", [P, NE])
        gate_now = sb("gate_now", [P, 2])
        st2 = sb("st2", [P, 32])
        ps = ctx.enter_context(nc.psum_tensor("ps", [P, 8, 512], F32))

        used = [0]

        def small(*shape):
            n = int(np.prod(shape))
            v = st[:, used[0]:used[0] + n]
            used[0] += n
            if len(shape) == 2:
                return v.rearrange("p (a b) -> p a b", b=shape[1])
            if len(shape) == 3:
                return v.rearrange("p (a b c) -> p a b c", b=shape[1], c=shape[2])
            return v
        ss1, rs1 = small(TT), small(TT)
        ssA, rsA = small(2, TT, HA), small(2, TT, HA)
        zb, tb, eb, lb = (small(TT, 8) for _ in range(4))
        beta, gdec = small(TT, 8), small(TT, 8)
        gcc, gll = small(2, TT, HA), small(2, TT, HA)
        egc, egl, kdc = small(2, TT, HA), small(2, TT, HA), small(2, TT, HA)
        ea = small(8)
        ssR, rsR = small(TT, NSLOT), small(TT, NSLOT)
        ssO, rsO = small(TT, HA), small(TT, HA)
        nsink = small(HB)
        rmax, nmx = small(3), small(2, HB)
        psumS, rinv, esk = small(2, HB), small(2, HB), small(2, HB)

        a_log, dt_b = row[:, 0:8], row[:, 8:16]
        a_norm = row[:, 16:16 + P]
        gains = row[:, 16 + P:16 + P + 4 * HD].rearrange("p (a b) -> p a b", b=HD)
        sink = row[:, 16 + P + 4 * HD:ROWS]
        g1 = col[:, 0:KD]
        cw = col[:, KD:COLS].rearrange("p (c j) -> p c j", j=5)

        s_init, ones_set, s_out = sem("s_init"), sem("ones_set"), sem("s_out")
        raw_full = [sem(f"raw_full{i}") for i in range(RAW_M)]
        par_in, const_in = sem("par_in"), sem("const_in")
        hi_done, lo_done, passes = sem("hi_done"), sem("lo_done"), sem("passes")
        x_sq, x_var, x_std, x_rstd, x_normed = (sem(n) for n in ("x_sq", "x_var", "x_std", "x_rstd", "x_normed"))
        xT_done, hT_hi, hT_lo = sem("xT_done"), sem("hT_hi"), sem("hT_lo")
        pad_set, proj_evac, tap0, conv_done, silu_done = (sem(n) for n in ("pad_set", "proj_evac", "tap0", "conv_done", "silu_done"))
        conv_step = sem("conv_step")
        tok_T, tok_evac, tok_sq, tok_ss = (sem(n) for n in ("tok_T", "tok_evac", "tok_sq", "tok_ss"))
        a_chain, v_chain, p_chain = sem("a_chain"), sem("v_chain"), sem("p_chain")
        qk_var, qk_std, qk_normed, back_T, back_evac = (sem(n) for n in ("qk_var", "qk_std", "qk_normed", "back_T", "back_evac"))
        gate_z, gate_e, gate_w, gate_ln, g_ready = (sem(n) for n in ("gate_z", "gate_e", "gate_w", "gate_ln", "g_ready"))
        cum_done, cum_evac, cum_diff, cum_exp = (sem(n) for n in ("cum_done", "cum_evac", "cum_diff", "cum_exp"))
        gu_ready, row_done, diff_done, dm_exp, eg_exp, masked, nt_base = (sem(n) for n in ("gu_ready", "row_done", "diff_done", "dm_exp", "eg_exp", "masked", "nt_base"))
        gram_done, at_done, nt_done, qg_done, kgd_done = (sem(n) for n in ("gram_done", "at_done", "nt_done", "qg_done", "kgd_done"))
        nm_done, t0_done, t0_T, t0_evac = (sem(n) for n in ("nm_done", "t0_done", "t0_T", "t0_evac"))
        x_done, x_evac, y_done, t_new = (sem(n) for n in ("x_done", "x_evac", "y_done", "t_new"))
        w_done, w_evac, v_done, vn_done, o_done, o_evac = (sem(n) for n in ("w_done", "w_evac", "v_done", "vn_done", "o_done", "o_evac"))
        s_done, s_dec, s_new, s_zero = (sem(n) for n in ("s_done", "s_dec", "s_new", "s_zero"))
        r_sq, r_ss, r_std, rope_done, aq_T, aq_evac, aq_lo, gain_set = (sem(n) for n in ("r_sq", "r_ss", "r_std", "rope_done", "aq_T", "aq_evac", "aq_lo", "gain_set"))
        score_done, win_done, max_done, prob_done, pT_done, pT_evac, pv_done, ob_evac = (sem(n) for n in ("score_done", "win_done", "max_done", "prob_done", "pT_done", "pT_evac", "pv_done", "ob_evac"))
        sink_in, sink_exp = sem("sink_in"), sem("sink_exp")
        oa_var, oa_std, z_silu, oa_done, r_var, r_scale = (sem(n) for n in ("oa_var", "oa_std", "z_silu", "oa_done", "r_var", "r_scale"))
        mix_T, mix_hi, mix_lo, x_added = (sem(n) for n in ("mix_T", "mix_hi", "mix_lo", "x_added"))
        e_in, fold_set, e_sq, e_var, e_std, h_done, e_hi, e_lo, hT2_done, hT2_evac = (sem(n) for n in (
            "e_in", "fold_set", "e_sq", "e_var", "e_std", "h_done", "e_hi", "e_lo", "hT2_done", "hT2_evac"))
        logit_done, logit_max, logit_exp, aff_done, affT_done, chosen, chosen_T, spread_done, rows_done, top_ready = (sem(n) for n in (
            "logit_done", "logit_max", "logit_exp", "aff_done", "affT_done", "chosen", "chosen_T", "spread_done", "rows_done", "top_ready"))
        m_hi, m_lo, m_lo_pool, m_pass = (sem(n) for n in ("m_hi", "m_lo", "m_lo_pool", "m_pass"))
        sel_done, selT_done, gathered, xe_evac = (sem(n) for n in ("sel_done", "selT_done", "gathered", "xe_evac"))
        gu_evac, folded, sg_done, hm_done, hp_hi, hp_lo = (sem(n) for n in ("gu_evac", "folded", "sg_done", "hm_done", "hp_hi", "hp_lo"))
        yt_done, ye_done, zeroed, scattered = (sem(n) for n in ("yt_done", "ye_done", "zeroed", "scattered"))
        slot_free = sem("slot_free")

        def piece_view(t, n):
            if n >= N_IN:
                return t[:, :].rearrange("p (k c) -> p k c", k=2)
            w = RW if n // 2 in REST_OF else 512
            return t[:, 0:4 * w].rearrange("p (k c) -> p k c", k=4)

        def piece_dram(L, n):
            if n >= N_IN:
                m = n - N_IN
                return w_out[bass.ds(L, 1), m * 2 * P:(m + 1) * 2 * P, :].rearrange("l (k p) c -> p (l k) c", p=P)
            g, half = divmod(n, 2)
            c0, w = (NQKV * P + REST_OF[g] * RW, RW) if g in REST_OF else ((g - FIRST_QKV) * 512, 512)
            return w_in[bass.ds(L, 1), half * 4 * P:(half + 1) * 4 * P, c0:c0 + w].rearrange("l (k p) c -> p (l k) c", p=P)

        def qk(t):
            return PR[:, t, AT0:AT0 + 1024].rearrange("p (s c) -> p s c", s=2)[:, :, 0:VOFF].rearrange("p s (a b) -> p s a b", b=HD)

        def squares(t):
            a = t % 2 * 2 * VOFF
            return VN_[:, :, :, :].rearrange("p a b c -> p (a b c)")[:, a:a + 2 * VOFF]

        def rotary(z, s):
            a = (2 * z + s) * VOFF
            return KN[:, :, :, :].rearrange("p a b c -> p (a b c)")[:, a:a + VOFF]

        UNITS = [(s, qt, h) for s in range(2) for qt in range(TT) for h in range(HB)]

        def key_tiles(s, qt):
            return range(max(0, qt - 1), min(TT, qt + 2)) if s == 0 else range(TT)

        def tile_of(d, t):
            return t if d == 0 else TT - 1 - t

        flight = [[delta[d][n] for n in names] for d, names in ((0, ("DM", "NT", "NM")), (1, ("DM", "NT", "NM")), (0, ("T", "XS", "WT")))]

        def win(u):
            return flight[u % 3][0][:, :, :].rearrange("p a b -> p (a b)")

        def prob(u):
            return flight[u % 3][1][:, :, :].rearrange("p a b -> p (a b)")

        def probT(u):
            return flight[u % 3][2][:, :, :].rearrange("p a b -> p (a b)")

        def rounds(eng, n):
            eng.wait_ge(raw_full[n % RAW_A], 16 * (n // RAW_A + 1))
            if n >= SPLIT:
                m = n - SPLIT
                eng.wait_ge(passes, 4 * (m + 1) if m < N_IN else 4 * N_IN + 8 * (m - N_IN + 1))
            nc.scalar.activation(piece_view(whi[n % SPLIT], n), piece_view(raw[n % RAW_A], n), ACT.Copy).then_inc(hi_done, 1)

        def rests(eng, n):
            eng.wait_ge(hi_done, n + 1)
            nc.vector.tensor_tensor(piece_view(wlo[n % SPLIT], n), piece_view(raw[n % RAW_A], n),
                                    piece_view(whi[n % SPLIT], n), ALU.subtract).then_inc(lo_done, 1)

        def expert_dram(L, g, q):
            (m, e), j = STREAM[q // 4], q % 4
            w = (w_gate, w_up, w_down)[m]
            return w[bass.ds(L, 1), bass.ds(g * 2 + e, 1), j * 2 * P:(j + 1) * 2 * P, :].rearrange("l e (k p) c -> p (l e k) c", p=P)

        def two(t):
            return t[:, :].rearrange("p (k c) -> p k c", k=2)

        def by_pool(q):
            return q in BY_POOL

        def dve_split(q):
            return sum(not by_pool(p) for p in range(q + 1))
        DVE_TURN, POOL_TURN = dve_split(TURN - 1), TURN - dve_split(TURN - 1)

        def wait_split(eng, g, q):
            if by_pool(q):
                eng.wait_ge(m_lo_pool, g * POOL_TURN + (q + 1 - dve_split(q)))
            else:
                eng.wait_ge(m_lo, g * DVE_TURN + dve_split(q))

        def expert_rounds(eng, g, q):
            slot = q % RAW_M
            eng.wait_ge(raw_full[slot], (g * (TURN // RAW_M) + (q // RAW_M + 1 + (LOADS_A if slot < RAW_A else 0))) * 16)
            eng.wait_ge(m_pass, g * TURN + (q + 1))
            nc.scalar.activation(whi[q % SPLIT_M][:, :], raw[slot][:, :], ACT.Copy).then_inc(m_hi, 1)

        def expert_rests(eng, g, q):
            eng.wait_ge(m_hi, g * TURN + (q + 1))
            o, a, b = wlo[q % SPLIT_M][:, :], raw[q % RAW_M][:, :], whi[q % SPLIT_M][:, :]
            if by_pool(q):
                nc.gpsimd.tensor_tensor(o, a, b, ALU.subtract).then_inc(m_lo_pool, 1)
            else:
                nc.vector.tensor_tensor(o, a, b, ALU.subtract).then_inc(m_lo, 1)

        with nc.Block() as block:
            @block.sync
            def _(sp):
                sp.dma_start(X[:, :, :], x.rearrange("o (t p) d -> p (o t) d", p=P)).then_inc(s_init, 16)
                a, n = const_at("ident")
                sp.dma_start(ident[:, :], consts[:, a:a + n]).then_inc(s_init, 16)
                sp.wait_ge(s_init, 32)
                sp.wait_ge(ones_set, 1)

            @block.gpsimd
            def _(pool):
                nc.gpsimd.memset(ones[:, :], 1.0).then_inc(ones_set, 1)

        with nc.Fori(0, LAYERS) as L:
            with nc.Block() as block:
                @block.sync
                def _(sp):
                    for n in range(2):
                        sp.dma_start(piece_view(raw[n], n), piece_dram(L, n)).then_inc(raw_full[n % RAW_A], 16)
                    sp.dma_start(row[:, :], rows[bass.ds(L, 1), :].to_broadcast([P, ROWS])).then_inc(par_in, 16)
                    sp.dma_start(col[:, :], cols[bass.ds(L, 1), :, :].rearrange("l p c -> p (l c)")).then_inc(par_in, 16)
                    for name, dst in (("cum", cum[:, :, :]), ("level", level[:, :, :]), ("window", window[:, :]),
                                      ("cos", cosT[:, :, :, :]), ("sin", sinT[:, :, :, :])):
                        a, n = const_at(name)
                        src = consts[:, a:a + n]
                        if name in ("cum", "level"):
                            src = src.rearrange("p (a b) -> p a b", b=P)
                        elif name != "window":
                            src = src.rearrange("p (a b c) -> p a b c", b=TT, c=HD)
                        sp.dma_start(dst, src).then_inc(const_in, 16)
                    for n in range(2, N_IN + N_OUT):
                        if n >= RAW_A:
                            sp.wait_ge(lo_done, n - RAW_A + 1)
                        sp.dma_start(piece_view(raw[n % RAW_A], n), piece_dram(L, n)).then_inc(raw_full[n % RAW_A], 16)

                    for i in range(RAW_A):
                        sp.wait_ge(lo_done, N_IN + N_OUT - RAW_A + i + 1)
                        sp.dma_start(two(raw[i]), expert_dram(L, 0, i)).then_inc(raw_full[i], 16)
                    sp.wait_ge(x_added, 8)
                    sp.dma_start(norm2_row[:, :], norm2[bass.ds(L, 1), :].to_broadcast([P, D])).then_inc(e_in, 16)
                    sp.dma_start(router[:, :, :], w_router[bass.ds(L, 1), :, :].rearrange("l (k p) e -> p (l k) e", p=P)).then_inc(e_in, 16)
                    for name, dst in (("iota", iota[:, :]), ("tokid", tokid[:, :])):
                        a, n = const_at(name)
                        sp.dma_start(dst, consts[:, a:a + n]).then_inc(e_in, 16)
                    for i in range(RAW_A, RAW_M):
                        sp.dma_start(two(raw[i]), expert_dram(L, 0, i)).then_inc(raw_full[i], 16)

                    def refill(g, q):
                        n = q + RAW_M
                        src = expert_dram(L, g + n // TURN, n % TURN)
                        wait_split(sp, g, q)
                        sp.sem_inc(slot_free, 1)
                        sp.dma_start(two(raw[q % RAW_M]), src).then_inc(raw_full[q % RAW_M], 16)
                    with sp.Fori(0, PAIRS - 1) as g:
                        for q in range(TURN):
                            refill(g, q)
                    for q in range(TURN - RAW_M):
                        refill(PAIRS - 1, q)

                @block.tensor
                def _(pe):
                    mm = nc.tensor.matmul
                    pe.wait_ge(x_normed, TT)
                    for k in range(KD):
                        for t in range(TT):
                            last = nc.tensor.transpose(ps[:, k, t * P:(t + 1) * P], XN[:, t, k * P:(k + 1) * P], ident[:, :])
                        last.then_inc(xT_done, 1)
                    for g in range(GROUPS):
                        for half in range(2):
                            n = 2 * g + half
                            pe.wait_ge(lo_done, n + 1)
                            if g == 0:
                                pe.wait_ge(hT_lo, 4 * (half + 1))
                            if g == 1:
                                pe.wait_ge(hT_lo, KD)
                            hi, lo = piece_view(whi[n % SPLIT], n), piece_view(wlo[n % SPLIT], n)
                            for t in range(4):
                                if g >= 2 and half == 0:
                                    pe.wait_ge(proj_evac, 4 * (g - 2) + t + 1)
                                b = 4 * (g % 2) + t
                                for kk in range(4):
                                    k = 4 * half + kk
                                    for j, (w, h) in enumerate(((hi, HH), (lo, HH), (hi, HL))):
                                        flags = dict(start=half == 0 and kk == 0 and j == 0, stop=half == 1 and kk == 3 and j == 2)
                                        if g not in REST_OF:
                                            last = mm(ps[:, b, :], w[:, kk, t * P:(t + 1) * P], h[:, k, :], **flags)
                                        else:
                                            last = mm(ps[:, b, 0:RW], h[:, k, t * P:(t + 1) * P], w[:, kk, :], **flags)
                                last.then_inc(passes, 1)
                    pe.wait_ge(g_ready, 1)
                    pe.wait_ge(const_in, 5 * 16)
                    pe.wait_ge(proj_evac, 4 * GROUPS)
                    for d in range(2):
                        g = gdec[:, :, d * HA:(d + 1) * HA]
                        mm(ps[:, 7, d * 16:(d + 1) * 16], cum[:, d, :], g, start=True, stop=True)
                        last = mm(ps[:, 7, 32 + d * 16:48 + d * 16], ones[:, :], g, start=True, stop=True)
                    last.then_inc(cum_done, 1)
                    pe.wait_ge(silu_done, NQKV)
                    for i, (c, t) in enumerate((c, t) for c in range(3) for t in range(TT)):
                        if i == 7:
                            pe.wait_ge(cum_evac, 1)
                        if i >= 8:
                            pe.wait_ge(tok_sq, i - 7)
                        for h in range(HA):
                            src = (QT, KT, VD)[c][:, h, t * P:(t + 1) * P]
                            last = nc.tensor.transpose(ps[:, i % 8, h * P:(h + 1) * P], src, ident[:, :])
                        last.then_inc(tok_T, 1)
                    for i, (c, h) in enumerate((c, h) for c in range(2) for h in range(HA)):
                        if h == 0:
                            pe.wait_ge(qk_normed, 4 * (c + 1))
                        if i < 4:
                            pe.wait_ge(tok_sq, 8)
                            pe.wait_ge(tok_evac, 9 + i)
                        for t in range(TT):
                            src = (O, KN)[c][:, t, h, :]
                            last = nc.tensor.transpose(ps[:, i, t * P:(t + 1) * P], src, ident[:, :])
                        last.then_inc(back_T, 1)
                    pe.wait_ge(back_evac, 8)
                    pe.wait_ge(cum_evac, 1)
                    for t in range(TT):
                        for d in range(2):
                            i = 2 * t + d
                            B, b0 = delta[d], 4 * d
                            tl = tile_of(d, t)
                            tok = slice(tl * P, (tl + 1) * P)
                            pe.wait_ge(gu_ready, i + 1)
                            if t > 0:
                                pe.wait_ge(w_evac, i - 1)
                                pe.wait_ge(vn_done, i - 1)
                                pe.wait_ge(o_evac, i - 1)
                            mm(ps[:, b0, :], ones[:, :], B["NM"][:, :, :].rearrange("p a b -> p (a b)"), start=True, stop=True).then_inc(row_done, 1)
                            for h in range(HA):
                                mm(ps[:, b0 + 1, h * P:(h + 1) * P], KT[:, h, tok], QT[:, h, tok], start=True, stop=True)
                            for h in range(HA):
                                last = mm(ps[:, b0 + 2, h * P:(h + 1) * P], KT[:, h, tok], KT[:, h, tok], start=True, stop=True)
                            last.then_inc(gram_done, 1)
                        for d in range(2):
                            i = 2 * t + d
                            B, b0 = delta[d], 4 * d
                            pe.wait_ge(t0_done, i + 1)
                            if t > 0:
                                pe.wait_ge(s_new, i - 1)
                            for h in range(HA):
                                last = nc.tensor.transpose(ps[:, b0 + 3, h * P:(h + 1) * P], B["TTr"][:, h, :], ident[:, :])
                            last.then_inc(t0_T, 1)
                        for l in range(1, 7):
                            for d in range(2):
                                i = 2 * t + d
                                c = (6 * t + l - 1) * 2 + d
                                B, b0 = delta[d], 4 * d
                                pe.wait_ge(nm_done, (7 * t + l) * 2 + d + 1)
                                if l == 1:
                                    pe.wait_ge(t0_evac, i + 1)
                                    pe.wait_ge(diff_done, i + 1)
                                    pe.wait_ge(nt_done, i + 1)
                                else:
                                    pe.wait_ge(t_new, 2 * (c - 1))
                                for h in range(HA):
                                    last = mm(ps[:, b0, h * P:(h + 1) * P], B["NM"][:, h, :], B["T"][:, h, :], start=True, stop=True)
                                last.then_inc(x_done, 1)
                            for d in range(2):
                                c = (6 * t + l - 1) * 2 + d
                                B, b0 = delta[d], 4 * d
                                pe.wait_ge(x_evac, c + 1)
                                if l < 6:
                                    for h in range(HA):
                                        mm(ps[:, b0 + 1, h * P:(h + 1) * P], B["TTr"][:, h, :], B["XS"][:, h, :], start=True, stop=True)
                                for h in range(HA):
                                    last = mm(ps[:, b0 + 2, h * P:(h + 1) * P], B["XS"][:, h, :], B["TTr"][:, h, :], start=True, stop=True)
                                last.then_inc(y_done, 1)
                        for d in range(2):
                            i = 2 * t + d
                            B, b0 = delta[d], 4 * d
                            tl = tile_of(d, t)
                            pe.wait_ge(t_new, 2 * ((6 * t + 5) * 2 + d + 1))
                            pe.wait_ge(kgd_done, 2 * (i + 1))
                            for h in range(HA):
                                last = mm(ps[:, b0, h * P:(h + 1) * P], B["KG"][:, h, :], B["TTr"][:, h, :], start=True, stop=True)
                            last.then_inc(w_done, 1)
                        for d in range(2):
                            i = 2 * t + d
                            B, b0 = delta[d], 4 * d
                            tl = tile_of(d, t)
                            pe.wait_ge(w_evac, i + 1)
                            if t == 0:
                                pe.wait_ge(s_zero, 1)
                            else:
                                pe.wait_ge(s_new, i - 1)
                            pe.wait_ge(t0_evac, i + 1)
                            for h in range(HA):
                                mm(ps[:, b0 + 1, h * P:(h + 1) * P], B["TTr"][:, h, :], VN_[:, tl, h, :], start=True, stop=False)
                                last = mm(ps[:, b0 + 1, h * P:(h + 1) * P], B["WT"][:, h, :], S[:, d, h, :], start=False, stop=True)
                            last.then_inc(v_done, 1)
                        for d in range(2):
                            i = 2 * t + d
                            B, b0 = delta[d], 4 * d
                            pe.wait_ge(vn_done, i + 1)
                            pe.wait_ge(qg_done, i + 1)
                            for h in range(HA):
                                mm(ps[:, b0 + 2, h * P:(h + 1) * P], B["QG"][:, h, :], S[:, d, h, :], start=True, stop=False)
                                last = mm(ps[:, b0 + 2, h * P:(h + 1) * P], B["AT"][:, h, :], B["VN"][:, h, :], start=False, stop=True)
                            last.then_inc(o_done, 1)
                            if t < TT - 1:
                                for h in range(HA):
                                    last = mm(ps[:, b0 + 3, h * P:(h + 1) * P], B["KD"][:, h, :], B["VN"][:, h, :], start=True, stop=True)
                                last.then_inc(s_done, 1)
                    for t in range(TT):
                        if t == 0:
                            pe.wait_ge(rope_done, TT)
                            pe.wait_ge(o_evac, 8)
                            pe.wait_ge(t0_evac, 8)
                        if t >= 2:
                            pe.wait_ge(aq_lo, 2 * (t - 1))
                        for half in range(2):
                            for j in range(3):
                                c = AT0 + half * 512 + j * P
                                last = nc.tensor.transpose(ps[:, 4 + 2 * (t % 2) + half, j * P:(j + 1) * P], PR[:, t, c:c + P], ident[:, :])
                            last.then_inc(aq_T, 1)

                    def scores(u):
                        s, qt, h = UNITS[u]
                        kts = key_tiles(s, qt)
                        if u >= 3:
                            if UNITS[u - 3][0] == 0:
                                pe.wait_ge(win_done, u - 2)
                            else:
                                pe.wait_ge(prob_done, u - 2)
                        base = HD * (h // 2)
                        for j, (a, b) in enumerate(((AQH, AQH), (AQL, AQH), (AQH, AQL))):
                            last = mm(ps[:, u % 3, 0:P * len(kts)], a[base:base + HD, 3 * s + h % 2, qt * P:(qt + 1) * P],
                                      b[base:base + HD, 3 * s + 2, kts[0] * P:(kts[-1] + 1) * P], start=j == 0, stop=j == 2)
                        last.then_inc(score_done, 1)

                    def transposed(u):
                        s, qt, h = UNITS[u]
                        pe.wait_ge(prob_done, u + 1)
                        if u >= 3:
                            pe.wait_ge(pT_evac, u - 2)
                        for j in range(len(key_tiles(s, qt))):
                            last = nc.tensor.transpose(ps[:, 3 + u % 3, j * P:(j + 1) * P], prob(u)[:, j * P:(j + 1) * P], ident[:, :])
                        last.then_inc(pT_done, 1)

                    def weighted(u):
                        s, qt, h = UNITS[u]
                        kts = key_tiles(s, qt)
                        pe.wait_ge(pT_evac, u + 1)
                        if u >= 8 and h == 0:
                            pe.wait_ge(ob_evac, u // 4 - 1)
                        for j, kt in enumerate(kts):
                            v = AT0 + s * 512 + VOFF
                            last = mm(ps[:, 6 + (u // 4) % 2, h * P:(h + 1) * P], probT(u)[:, j * P:(j + 1) * P],
                                      PR[:, kt, v:v + P], start=j == 0, stop=j == len(kts) - 1)
                        last.then_inc(pv_done, 1)
                    pe.wait_ge(aq_lo, 2 * TT)
                    scores(0)
                    scores(1)
                    for u in range(len(UNITS)):
                        if u + 2 < len(UNITS):
                            scores(u + 2)
                        transposed(u)
                        if u:
                            weighted(u - 1)
                    weighted(len(UNITS) - 1)
                    for k in range(KD):
                        if k == 0:
                            pe.wait_ge(ob_evac, 2 * TT)
                            pe.wait_ge(oa_done, 1)
                        for t in range(TT):
                            src = O[:, t, k, :] if k < HA else OB[:, t, (k - HA) * P:(k - HA + 1) * P]
                            last = nc.tensor.transpose(ps[:, k, t * P:(t + 1) * P], src, ident[:, :])
                        last.then_inc(mix_T, 1)
                    pe.wait_ge(mix_lo, KD)
                    for m in range(N_OUT):
                        n = N_IN + m
                        pe.wait_ge(lo_done, n + 1)
                        hi, lo = piece_view(whi[n % SPLIT], n), piece_view(wlo[n % SPLIT], n)
                        for b in range(8):
                            t, half = divmod(b, 2)
                            for kk in range(2):
                                for j, (w, h) in enumerate(((hi, MH), (lo, MH), (hi, ML))):
                                    last = mm(ps[:, b, :], h[:, 2 * m + kk, t * P:(t + 1) * P], w[:, kk, half * 512:(half + 1) * 512],
                                              start=m == 0 and kk == 0 and j == 0, stop=m == N_OUT - 1 and kk == 1 and j == 2)
                            last.then_inc(passes, 1)

                    for t in range(TT):
                        pe.wait_ge(h_done, t + 1)
                        pe.wait_ge(x_added, 8)
                        if t >= 2:
                            pe.wait_ge(hT2_evac, 2 * (t - 1))
                        for half in range(2):
                            for j in range(4):
                                k = 4 * half + j
                                last = nc.tensor.transpose(ps[:, 2 * (t % 2) + half, j * P:(j + 1) * P], hw[:, t % 2, k * P:(k + 1) * P], ident[:, :])
                            last.then_inc(hT2_done, 1)
                    pe.wait_ge(e_in, 64)
                    pe.wait_ge(hT2_evac, 2 * TT)
                    for t in range(TT):
                        for k in range(KD):
                            last = mm(ps[:, 4, t * NE:(t + 1) * NE], HT[:, k, t * P:(t + 1) * P], router[:, k, :], start=k == 0, stop=k == KD - 1)
                    last.then_inc(logit_done, 1)
                    pe.wait_ge(aff_done, 1)
                    for t in range(TT):
                        last = nc.tensor.transpose(ps[0:NE, 5, t * P:(t + 1) * P], aff[:, t, :], ident[:, :])
                    last.then_inc(affT_done, 1)
                    pe.wait_ge(chosen, 1)
                    for j in range(2):
                        last = nc.tensor.transpose(ps[:, 6, j * NE:(j + 1) * NE], twice[:, j, :, :].rearrange("p a b -> p (a b)"), ident[0:NE, 0:NE])
                    last.then_inc(chosen_T, 1)
                    pe.wait_ge(spread_done, 1)
                    for j in range(2):
                        last = mm(ps[:, j, :], ones[0:NE, :], spread[:, 8 * j:8 * j + 8, :].rearrange("p a b -> p (a b)"), start=True, stop=True)
                    last.then_inc(rows_done, 1)
                    pe.wait_ge(fold_set, 1)
                    pe.wait_ge(top_ready, 1)
                    pe.sem_inc(m_pass, SPLIT_M)
                    pe.wait_ge(selT_done, 1)
                    pe.wait_ge(ye_done, 1)
                    for half in range(2):
                        mm(ps[:, 6 + half, :], selT[:, 0:P], YE[:, 0:512], start=True, stop=True).then_inc(zeroed, 1)

                    def gather(part):
                        for k in range(4 * part, 4 * part + 4):
                            for z, h in enumerate((EH, EL)):
                                at = 128 * (2 * (k % 2) + z)
                                copies = 2 if at < 384 else 1
                                o = ps[:, k // 2, at:at + copies * P].rearrange("p (c s) -> p c s", c=copies)
                                for t in range(TT):
                                    last = mm(o, h[:, t, k * P:(k + 1) * P], bc(sel[:, t, :], 1, [P, copies, P]), start=t == 0, stop=t == TT - 1)
                        last.then_inc(gathered, 1)
                    def scatter(ns):
                        for n in ns:
                            t, half = divmod(n, 2)
                            mm(ps[:, 4 + n % 4, :], selT[:, t * P:(t + 1) * P], YE[:, half * 512:(half + 1) * 512], start=True, stop=True).then_inc(scattered, 1)
                    pe.wait_ge(sel_done, 1)
                    gather(0)
                    gather(1)
                    with pe.Fori(0, PAIRS) as g:
                        def times(block, js, bank, lhs):
                            for j in js:
                                q = 4 * block + j
                                wait_split(pe, g, q)
                                for kk in range(2):
                                    k = 2 * j + kk
                                    for half in range(2):
                                        for z, w in enumerate((whi, wlo)):
                                            last = mm(ps[:, bank + half, :], lhs(k), two(w[q % SPLIT_M])[:, kk, half * 512:(half + 1) * 512],
                                                      start=k == 0 and z == 0, stop=k == KD - 1 and z == 1)
                                last.then_inc(m_pass, 1)

                        def folds(j):
                            for f in range(DE // P):
                                last = mm(ps[:, 4 + j, f * CAP:(f + 1) * CAP], GU[:, j, f * P:(f + 1) * P], fold[:, :], start=True, stop=True)
                            last.then_inc(folded, 1)

                        def a(k):
                            return XE[:, k, 0, :]

                        def b(k):
                            return XE[:, k, 1, :]

                        def hidden(k):
                            return HP[:, k, :]
                        pe.wait_ge(xe_evac, g * 2 + 1)
                        times(0, range(2), 0, a)
                        pe.wait_ge(xe_evac, g * 2 + 2)
                        times(0, range(2, 3), 0, a)
                        pe.wait_ge(ye_done, g * 2 + 2)
                        pe.wait_ge(selT_done, g + 1)
                        scatter(range(4))
                        times(0, range(3, 4), 0, a)
                        times(1, range(3), 2, a)
                        pe.wait_ge(x_added, g * 8 + 12)
                        scatter(range(4, 8))
                        times(1, range(3, 4), 2, a)
                        pe.wait_ge(gu_evac, g * 4 + 1)
                        times(2, range(2), 0, b)
                        pe.wait_ge(gu_evac, g * 4 + 2)
                        pe.wait_ge(x_added, g * 8 + 16)
                        folds(0)
                        folds(1)
                        times(2, range(2, 4), 0, b)
                        pe.wait_ge(hp_lo, g * 2 + 1)
                        times(3, range(4), 6, hidden)
                        pe.wait_ge(gu_evac, g * 4 + 3)
                        folds(0)
                        times(4, range(4), 2, b)
                        pe.wait_ge(gu_evac, g * 4 + 4)
                        folds(1)
                        pe.wait_ge(sel_done, g + 2)
                        gather(0)
                        pe.wait_ge(hp_lo, g * 2 + 2)
                        pe.wait_ge(ye_done, g * 2 + 3)
                        times(5, range(1), 6, hidden)
                        gather(1)
                        times(5, range(1, 4), 6, hidden)
                    pe.wait_ge(xe_evac, PAIRS * 2 + 1)
                    pe.wait_ge(ye_done, PAIRS * 2 + 2)
                    pe.wait_ge(selT_done, PAIRS + 1)
                    scatter(range(4))
                    pe.wait_ge(x_added, PAIRS * 8 + 12)
                    scatter(range(4, 8))

                @block.scalar
                def _(act):
                    A = nc.scalar.activation

                    for t in range(TT):
                        A(XN[:, t, :], X[:, t, :], ACT.Square, accum_out=ss1[:, t:t + 1]).then_inc(x_sq, 1)
                    rounds(act, 0)
                    rounds(act, 1)
                    act.wait_ge(x_var, 1)
                    A(rs1[:, :], ss1[:, :], ACT.Sqrt).then_inc(x_std, 1)
                    act.wait_ge(par_in, 32)
                    for k in range(KD):
                        act.wait_ge(xT_done, k + 1)
                        A(HH[:, k, :], ps[:, k, :], ACT.Copy, scale=g1[:, k:k + 1]).then_inc(hT_hi, 1)

                    def silu(ct):
                        dst = (QT, KT, VD)[ct // 4][:, ct % 4, :]
                        act.wait_ge(conv_done, ct + 1)
                        A(dst, dst, ACT.Silu).then_inc(silu_done, 1)
                    act.wait_ge(pad_set, 1)
                    for g in range(GROUPS):
                        for n in (2 * g + 2, 2 * g + 3):
                            if n < N_IN:
                                rounds(act, n)
                        if g == 1:
                            act.wait_ge(gate_z, 1)
                            A(eb[:, :, :], tb[:, :, :], ACT.Exp, scale=-1.0).then_inc(gate_e, 1)
                            A(beta[:, :, :], PR[:, :, BA0:BA0 + 8], ACT.Exp, scale=-1.0).then_inc(gate_e, 1)
                            A(ea[:, :], a_log, ACT.Exp).then_inc(gate_e, 1)
                            act.wait_ge(gate_w, 1)
                            A(lb[:, :, :], tb[:, :, :], ACT.Ln).then_inc(gate_ln, 1)
                        if g == FIRST_QKV:
                            act.wait_ge(r_var, 1)
                            A(rsR[:, :, :], ssR[:, :, :], ACT.Sqrt).then_inc(r_std, 1)
                        for t in range(4):
                            act.wait_ge(passes, 8 * g + 4 + t + 1)
                            b = 4 * (g % 2) + t
                            if g in REST_OF:
                                if g == GROUPS - 1 and t == 0:
                                    silu(NQKV - 1)
                                A(PR[:, t, REST_OF[g] * RW:(REST_OF[g] + 1) * RW], ps[:, b, 0:RW], ACT.Copy).then_inc(proj_evac, 1)
                                continue
                            c = g - FIRST_QKV
                            ct = 4 * c + t
                            if ct >= 2:
                                act.wait_ge(conv_done, ct - 1)
                            A(XP[:, ct % 2, 2:SEQ + 2], ps[:, b, :], ACT.Copy).then_inc(proj_evac, 1)
                            act.wait_ge(proj_evac, 4 * g + t + 1)
                            A((QT, KT, VD)[c][:, t, :], XP[:, ct % 2, 0:SEQ], ACT.Copy, scale=cw[:, ct, 0:1]).then_inc(tap0, 1)
                            if ct >= 1:
                                silu(ct - 1)
                    act.wait_ge(proj_evac, 4 * GROUPS)
                    A(PR[:, :, Z0:Z0 + 512], PR[:, :, Z0:Z0 + 512], ACT.Silu).then_inc(z_silu, 1)
                    act.wait_ge(rope_done, TT)
                    for i in range(12):
                        c, t = divmod(i, TT)
                        act.wait_ge(tok_T, i + 1)
                        dst = (O, KN, VN_)[c][:, t, :, :]
                        A(dst, ps[:, i % 8, :].rearrange("p (a b) -> p a b", b=P), ACT.Copy).then_inc(tok_evac, 1)
                        if c < 2:
                            if i >= 2:
                                act.wait_ge(tok_ss, i - 1)
                            A(SQ[:, i % 2, :], ps[:, i % 8, :], ACT.Square).then_inc(tok_sq, 1)
                    act.wait_ge(qk_var, 1)
                    A(rsA[:, :, :, :], ssA[:, :, :, :], ACT.Sqrt).then_inc(qk_std, 1)
                    for i in range(8):
                        c, h = divmod(i, HA)
                        act.wait_ge(back_T, i + 1)
                        A((QT, KT)[c][:, h, :], ps[:, i, :], ACT.Copy).then_inc(back_evac, 1)
                    act.wait_ge(cum_diff, 1)
                    A(egc[:, :, :, :], gcc[:, :, :, :], ACT.Exp)
                    A(egl[:, :, :, :], gll[:, :, :, :], ACT.Exp)
                    A(kdc[:, :, :, :], kdc[:, :, :, :], ACT.Exp).then_inc(cum_exp, 1)
                    for t in range(TT):
                        for d in range(2):
                            i = 2 * t + d
                            B, b0 = delta[d], 4 * d
                            act.wait_ge(row_done, i + 1)
                            if t > 0:
                                act.wait_ge(o_done, i - 1)
                            A(B["QG"][:, :, :], ps[:, b0, :].rearrange("p (a b) -> p a b", b=P), ACT.Exp).then_inc(eg_exp, 1)
                            act.wait_ge(diff_done, i + 1)
                            A(B["DM"][:, :, :], B["DM"][:, :, :], ACT.Exp).then_inc(dm_exp, 1)
                        for d in range(2):
                            i = 2 * t + d
                            B, b0 = delta[d], 4 * d
                            act.wait_ge(t0_T, i + 1)
                            A(B["T"][:, :, :], ps[:, b0 + 3, :].rearrange("p (a b) -> p a b", b=P), ACT.Copy).then_inc(t0_evac, 1)
                        for l in range(1, 7):
                            for d in range(2):
                                c = (6 * t + l - 1) * 2 + d
                                B, b0 = delta[d], 4 * d
                                act.wait_ge(x_done, c + 1)
                                if c >= 2:
                                    act.wait_ge(y_done, c - 1)
                                A(B["XS"][:, :, :], ps[:, b0, :].rearrange("p (a b) -> p a b", b=P), ACT.Copy).then_inc(x_evac, 1)
                        for d in range(2):
                            i = 2 * t + d
                            B, b0 = delta[d], 4 * d
                            act.wait_ge(w_done, i + 1)
                            if t > 0:
                                act.wait_ge(v_done, i - 1)
                            A(B["WT"][:, :, :], ps[:, b0, :].rearrange("p (a b) -> p a b", b=P), ACT.Copy, scale=-1.0).then_inc(w_evac, 1)
                    for i in range(2 * TT):
                        t, half = divmod(i, 2)
                        act.wait_ge(aq_T, i + 1)
                        A(AQH[:, 3 * half:3 * half + 3, t * P:(t + 1) * P],
                          ps[:, 4 + 2 * (t % 2) + half, 0:3 * P].rearrange("p (a b) -> p a b", b=P), ACT.Copy).then_inc(aq_evac, 1)
                    act.wait_ge(oa_var, 1)
                    A(rsO[:, :, :], ssO[:, :, :], ACT.Sqrt).then_inc(oa_std, 1)

                    def weights(u):
                        s, qt, h = UNITS[u]
                        n = P * len(key_tiles(s, qt))
                        act.wait_ge(max_done, u + 1)
                        if u >= 3:
                            act.wait_ge(pT_done, u - 2)
                        if u >= 8 and h == 0:
                            act.wait_ge(ob_evac, u // 4 - 1)
                        src = win(u)[:, 0:n] if s == 0 else ps[:, u % 3, 0:n]
                        A(prob(u)[:, 0:n], src, ACT.Exp, scale=SCALE, bias=nmx[:, (u // 4) % 2, h:h + 1],
                          accum_out=psumS[:, (u // 4) % 2, h:h + 1]).then_inc(prob_done, 1)
                        if s == 0 and h == HB - 1:
                            act.wait_ge(sink_in, qt + 1)
                            A(esk[:, (u // 4) % 2, :], esk[:, (u // 4) % 2, :], ACT.Exp).then_inc(sink_exp, 1)
                    weights(0)
                    for u, (s, qt, h) in enumerate(UNITS):
                        n = P * len(key_tiles(s, qt))
                        if u + 1 < len(UNITS):
                            weights(u + 1)
                        act.wait_ge(pT_done, u + 1)
                        if u >= 3:
                            act.wait_ge(pv_done, u - 2)
                        A(probT(u)[:, 0:n], ps[:, 3 + u % 3, 0:n], ACT.Copy).then_inc(pT_evac, 1)
                    act.wait_ge(pv_done, len(UNITS))
                    for m in range(SPLIT):
                        rounds(act, N_IN + m)
                    for k in range(KD):
                        act.wait_ge(mix_T, k + 1)
                        A(MH[:, k, :], ps[:, k, :], ACT.Copy).then_inc(mix_hi, 1)
                    rounds(act, N_IN + 3)


                    act.wait_ge(x_added, 8)
                    for t in range(TT):
                        A(GU[:, 0, :], X[:, t, :], ACT.Square, accum_out=st2[:, t:t + 1]).then_inc(e_sq, 1)
                        act.wait_ge(e_sq, t + 1)
                    act.wait_ge(e_var, 1)
                    A(st2[:, 4:8], st2[:, 0:4], ACT.Sqrt).then_inc(e_std, 1)
                    for t in range(TT):
                        act.wait_ge(h_done, t + 1)
                        A(EH[:, t, :], hw[:, t % 2, :], ACT.Copy).then_inc(e_hi, 1)
                        for half in range(2):
                            act.wait_ge(hT2_done, 2 * t + half + 1)
                            A(HT[:, 4 * half:4 * half + 4, t * P:(t + 1) * P],
                              ps[:, 2 * (t % 2) + half, :].rearrange("p (a b) -> p a b", b=P), ACT.Copy).then_inc(hT2_evac, 1)
                    act.wait_ge(logit_max, 1)
                    A(aff[:, :, :], aff[:, :, :], ACT.Exp).then_inc(logit_exp, 1)

                    def tokens_in(i, part):
                        act.wait_ge(gathered, i * 2 + (part + 1))
                        for e in range(2):
                            last = A(XE[:, 4 * part:4 * part + 4, e, :].rearrange("p k (z c) -> p k z c", z=2),
                                     ps[:, 2 * part:2 * part + 2, :].rearrange("p b (k z e c) -> p (b k) z e c", k=2, z=2, e=2)[:, :, :, e, :], ACT.Copy)
                        last.then_inc(xe_evac, 1)
                    tokens_in(0, 0)
                    act.wait_ge(zeroed, 2)
                    with act.Fori(0, PAIRS) as g:
                        def rows_out(j, block):
                            act.wait_ge(m_pass, g * TURN + (SPLIT_M + 4 * block + 4))
                            A(GU[:, j, :], ps[:, 2 * j:2 * j + 2, :].rearrange("p a b -> p (a b)"), ACT.Copy).then_inc(gu_evac, 1)

                        def gate(n):
                            act.wait_ge(folded, g * 4 + (2 * n + 1))
                            A(SG[:, :, :], ps[:, 4, :].rearrange("p (a b) -> p a b", b=CAP), ACT.Silu).then_inc(sg_done, 1)

                        def hidden_hi(n):
                            act.wait_ge(hm_done, g * 2 + (n + 1))
                            A(HP[:, :, 0:CAP], HM[:, :, :], ACT.Copy).then_inc(hp_hi, 1)

                        def low_share(n, passed):
                            act.wait_ge(m_pass, g * TURN + (SPLIT_M + passed))
                            A(YT[:, :], ps[CAP:P, 6:8, :].rearrange("p a b -> p (a b)"), ACT.Copy, scale=gate_now[CAP:P, n:n + 1]).then_inc(yt_done, 1)
                        after = {0: [lambda: tokens_in(g, 1)], 1: [lambda: low_share(1, 0)], 6: [lambda: rows_out(0, 0)], 10: [lambda: rows_out(1, 1)],
                                 13: [lambda: gate(0), lambda: hidden_hi(0)], 14: [lambda: rows_out(0, 2)], 18: [lambda: low_share(0, 16)],
                                 22: [lambda: rows_out(1, 4)], 23: [lambda: gate(1), lambda: hidden_hi(1), lambda: tokens_in(g + 1, 0)]}
                        for q in range(TURN):
                            expert_rounds(act, g, q)
                            for work_ in after.get(q, ()):
                                work_()
                    act.wait_ge(m_pass, PAIRS * TURN + SPLIT_M)
                    A(YT[:, :], ps[CAP:P, 6:8, :].rearrange("p a b -> p (a b)"), ACT.Copy, scale=gate_now[CAP:P, 1:2]).then_inc(yt_done, 1)

                @block.vector
                def _(dve):
                    V = nc.vector
                    chained = [0]

                    def step(ins):
                        chained[0] += 1
                        ins.then_inc(v_chain, 1)
                        dve.wait_ge(v_chain, chained[0])
                    dve.wait_ge(x_sq, TT)
                    V.tensor_scalar(ss1[:, :], ss1[:, :], 1.0 / D, EPS, ALU.mult, ALU.add).then_inc(x_var, 1)
                    dve.wait_ge(x_std, 1)
                    step(V.reciprocal(rs1[:, :], rs1[:, :]))
                    for t in range(TT):
                        V.tensor_scalar(XN[:, t, :], X[:, t, :], rs1[:, t:t + 1], None, ALU.mult).then_inc(x_normed, 1)
                    rests(dve, 0)
                    rests(dve, 1)
                    for k in range(KD):
                        dve.wait_ge(hT_hi, k + 1)
                        V.scalar_tensor_tensor(HL[:, k, :], ps[:, k, :], g1[:, k:k + 1], HH[:, k, :],
                                               ALU.mult, ALU.subtract).then_inc(hT_lo, 1)
                    steps = 0
                    for g in range(GROUPS):
                        for n in (2 * g + 2, 2 * g + 3):
                            if n < N_IN:
                                rests(dve, n)
                        if g == 1:
                            dve.wait_ge(proj_evac, 4)
                            dve.wait_ge(par_in, 32)
                            step(V.tensor_tensor(zb[:, :, :], PR[:, :, BA0 + 8:BA0 + 16], bc(dt_b, 1, [P, TT, 8]), ALU.add))
                            V.scalar_tensor_tensor(tb[:, :, :], zb[:, :, :], -1.0, zb[:, :, :], ALU.mult, ALU.max).then_inc(gate_z, 1)
                            dve.wait_ge(gate_e, 3)
                            step(V.tensor_scalar(beta[:, :, :], beta[:, :, :], 1.0, None, ALU.add))
                            V.reciprocal(beta[:, :, :], beta[:, :, :])
                            V.tensor_scalar(tb[:, :, :], eb[:, :, :], 1.0, None, ALU.add).then_inc(gate_w, 1)
                            dve.wait_ge(gate_w, 1)
                            step(V.scalar_tensor_tensor(eb[:, :, :], tb[:, :, :], -1.0, eb[:, :, :], ALU.add, ALU.subtract))
                            dve.wait_ge(gate_ln, 1)
                            step(V.reciprocal(tb[:, :, :], tb[:, :, :]))
                            step(V.tensor_tensor(eb[:, :, :], eb[:, :, :], tb[:, :, :], ALU.mult))
                            step(V.tensor_tensor(lb[:, :, :], lb[:, :, :], eb[:, :, :], ALU.subtract))
                            step(V.scalar_tensor_tensor(zb[:, :, :], zb[:, :, :], 0.0, lb[:, :, :], ALU.max, ALU.add))
                            V.scalar_tensor_tensor(gdec[:, :, :], zb[:, :, :], -1.0, bc(ea[:, :], 1, [P, TT, 8]), ALU.mult, ALU.mult).then_inc(g_ready, 1)
                        if g == FIRST_QKV:
                            for t in range(TT):
                                dve.wait_ge(r_sq, t + 1)
                                V.reduce_sum(ssR[:, t, :], squares(t).rearrange("p (a b) -> p a b", b=HD), axis=AX).then_inc(r_ss, 1)
                            dve.wait_ge(r_ss, TT)
                            V.tensor_scalar(ssR[:, :, :], ssR[:, :, :], 1.0 / HD, EPS, ALU.mult, ALU.add).then_inc(r_var, 1)
                            dve.wait_ge(r_std, 1)
                            V.reciprocal(rsR[:, :, :], rsR[:, :, :]).then_inc(r_scale, 1)
                        if g not in REST_OF:
                            for t in range(4):
                                ct = 4 * (g - FIRST_QKV) + t
                                y = (QT, KT, VD)[g - FIRST_QKV][:, t, :]
                                dve.wait_ge(tap0, ct + 1)
                                for j in range(1, 5):
                                    ins = V.scalar_tensor_tensor(y, XP[:, ct % 2, j:j + SEQ], cw[:, ct, j:j + 1], y, ALU.mult, ALU.add)
                                    if j < 4:
                                        steps += 1
                                        ins.then_inc(conv_step, 1)
                                        dve.wait_ge(conv_step, steps)
                                    else:
                                        ins.then_inc(conv_done, 1)
                    dve.wait_ge(cum_done, 1)
                    four = dict(b=TT, c=HA)
                    V.tensor_copy(gcc[:, :, :, :], ps[:, 7, 0:32].rearrange("p (a b c) -> p a b c", **four))
                    V.tensor_copy(gll[:, :, :, :], ps[:, 7, 32:64].rearrange("p (a b c) -> p a b c", **four)).then_inc(cum_evac, 1)
                    dve.wait_ge(cum_evac, 1)
                    V.tensor_tensor(kdc[:, :, :, :], gll[:, :, :, :], gcc[:, :, :, :], ALU.subtract).then_inc(cum_diff, 1)
                    for i in range(8):
                        c, t = divmod(i, TT)
                        dve.wait_ge(tok_sq, i + 1)
                        V.reduce_sum(ssA[:, c, t, :], SQ[:, i % 2, :].rearrange("p (a b) -> p a b", b=P), axis=AX).then_inc(tok_ss, 1)
                    dve.wait_ge(tok_ss, 8)
                    V.tensor_scalar(ssA[:, :, :, :], ssA[:, :, :, :], EPS, None, ALU.add).then_inc(qk_var, 1)
                    dve.wait_ge(qk_std, 1)
                    step(V.reciprocal(rsA[:, :, :, :], rsA[:, :, :, :]))
                    step(V.tensor_scalar(rsA[:, 0, :, :], rsA[:, 0, :, :], float(P) ** -0.5, None, ALU.mult))
                    dve.wait_ge(tok_evac, 8)
                    for i in range(8):
                        c, t = divmod(i, TT)
                        dst = (O, KN)[c][:, t, :, :]
                        V.tensor_tensor(dst, dst, bc(rsA[:, c, t, :], 2, [P, HA, P]), ALU.mult).then_inc(qk_normed, 1)
                    for t in range(TT):
                        for d in range(2):
                            i = 2 * t + d
                            B, b0 = delta[d], 4 * d
                            dve.wait_ge(eg_exp, i + 1)
                            if t > 0:
                                dve.wait_ge(nt_base, i - 1)
                            for h in range(HA):
                                last = V.tensor_scalar(B["DM"][:, h, :], ps[:, b0, h * P:(h + 1) * P],
                                                       gcc[:, d, tile_of(d, t), h:h + 1], 0.0, ALU.subtract, ALU.min)
                            last.then_inc(diff_done, 1)
                        for d in range(2):
                            i = 2 * t + d
                            B, b0 = delta[d], 4 * d
                            tl = tile_of(d, t)
                            tok = slice(tl * P, (tl + 1) * P)
                            dve.wait_ge(gram_done, i + 1)
                            dve.wait_ge(masked, i + 1)
                            if t > 0:
                                dve.wait_ge(o_done, i - 1)
                            V.tensor_tensor(B["AT"][:, :, :], ps[:, b0 + 1, :].rearrange("p (a b) -> p a b", b=P), B["DM"][:, :, :], ALU.mult).then_inc(at_done, 1)
                            dve.wait_ge(nt_base, i + 1)
                            V.tensor_tensor(B["NT"][:, :, :], ps[:, b0 + 2, :].rearrange("p (a b) -> p a b", b=P), B["NT"][:, :, :], ALU.mult).then_inc(nt_done, 1)
                            dve.wait_ge(eg_exp, i + 1)
                            dve.wait_ge(back_evac, 4)
                            V.tensor_tensor(B["QG"][:, :, :], B["QG"][:, :, :], QT[:, :, tok], ALU.mult).then_inc(qg_done, 1)
                        for d in range(2):
                            i = 2 * t + d
                            B, b0 = delta[d], 4 * d
                            dve.wait_ge(nm_done, 14 * t + d + 1)
                            if t > 0:
                                dve.wait_ge(v_done, i - 1)
                            V.tensor_tensor(B["TTr"][:, :, :], bc(ident[:, :], 1, [P, HA, P]), B["NM"][:, :, :], ALU.subtract).then_inc(t0_done, 1)
                        for l in range(1, 7):
                            for d in range(2):
                                i = 2 * t + d
                                c = (6 * t + l - 1) * 2 + d
                                B, b0 = delta[d], 4 * d
                                dve.wait_ge(y_done, c + 1)
                                if l == 1:
                                    dve.wait_ge(t0_evac, i + 1)
                                if l < 6:
                                    V.tensor_tensor(B["T"][:, :, :], B["T"][:, :, :], ps[:, b0 + 1, :].rearrange("p (a b) -> p a b", b=P), ALU.subtract).then_inc(t_new, 1)
                                V.tensor_tensor(B["TTr"][:, :, :], B["TTr"][:, :, :], ps[:, b0 + 2, :].rearrange("p (a b) -> p a b", b=P), ALU.subtract).then_inc(t_new, 1 if l < 6 else 2)
                        for d in range(2):
                            i = 2 * t + d
                            B, b0 = delta[d], 4 * d
                            tl = tile_of(d, t)
                            dve.wait_ge(v_done, i + 1)
                            if t > 0:
                                dve.wait_ge(s_done, i - 1)
                            V.tensor_tensor(B["VN"][:, :, :], ps[:, b0 + 1, :].rearrange("p (a b) -> p a b", b=P),
                                            bc(beta[:, tl, d * HA:(d + 1) * HA], 2, [P, HA, P]), ALU.mult).then_inc(vn_done, 1)
                        for d in range(2):
                            i = 2 * t + d
                            B, b0 = delta[d], 4 * d
                            tl = tile_of(d, t)
                            dve.wait_ge(o_done, i + 1)
                            o = ps[:, b0 + 2, :].rearrange("p (a b) -> p a b", b=P)
                            if t < TT // 2:
                                if i == 0:
                                    dve.wait_ge(back_T, 4)
                                V.tensor_copy(O[:, tl, :, :], o).then_inc(o_evac, 1)
                            else:
                                dve.wait_ge(o_evac, 4)
                                V.tensor_tensor(O[:, tl, :, :], O[:, tl, :, :], o, ALU.add).then_inc(o_evac, 1)
                            if t < TT - 1:
                                dve.wait_ge(s_done, i + 1)
                                dve.wait_ge(s_dec, i + 1)
                                V.tensor_tensor(S[:, d, :, :], S[:, d, :, :], ps[:, b0 + 3, :].rearrange("p (a b) -> p a b", b=P), ALU.add).then_inc(s_new, 1)
                    dve.wait_ge(o_evac, 8)
                    sq = QT[:, :, :].rearrange("p a b -> p (a b)")
                    flatO = O[:, :, :, :].rearrange("p t h c -> p (t h c)")
                    step(V.tensor_tensor(sq, flatO, flatO, ALU.mult))
                    step(V.reduce_sum(ssO[:, :, :].rearrange("p a b -> p (a b)"), sq.rearrange("p (a b) -> p a b", b=P), axis=AX))
                    V.tensor_scalar(ssO[:, :, :], ssO[:, :, :], 1.0 / P, EPS, ALU.mult, ALU.add).then_inc(oa_var, 1)
                    for i in range(2 * TT):
                        t, half = divmod(i, 2)
                        dve.wait_ge(aq_evac, i + 1)
                        c = (slice(None), slice(3 * half, 3 * half + 3), slice(t * P, (t + 1) * P))
                        V.tensor_tensor(AQL[c], ps[:, 4 + 2 * (t % 2) + half, 0:3 * P].rearrange("p (a b) -> p a b", b=P), AQH[c], ALU.subtract).then_inc(aq_lo, 1)
                    O3 = O[:, :, :, :].rearrange("p t h c -> p (t h) c")

                    def delta_norm(stage):
                        if stage == 0:
                            dve.wait_ge(oa_std, 1)
                            step(V.reciprocal(rsO[:, :, :], rsO[:, :, :]))
                            step(V.tensor_tensor(O3, O3, bc(rsO[:, :, :].rearrange("p a b -> p (a b)"), 2, [P, TT * HA, P]), ALU.mult))
                        elif stage == 1:
                            step(V.tensor_tensor(O3, O3, bc(a_norm, 1, [P, TT * HA, P]), ALU.mult))
                        else:
                            dve.wait_ge(z_silu, 1)
                            V.tensor_tensor(O[:, :, :, :].rearrange("p t h c -> p t (h c)"), O[:, :, :, :].rearrange("p t h c -> p t (h c)"),
                                            PR[:, :, Z0:Z0 + 512], ALU.mult).then_inc(oa_done, 1)
                    step(V.tensor_scalar(nsink[:, :], sink, -1.0, None, ALU.mult))

                    def finish(G):
                        s, qt = divmod(G, TT)
                        r = G % 2
                        dve.wait_ge(pv_done, 4 * G + 4)
                        if s == 0:
                            dve.wait_ge(sink_exp, qt + 1)
                            step(V.tensor_tensor(rinv[:, r, :], psumS[:, r, :], esk[:, r, :], ALU.add))
                            step(V.reciprocal(rinv[:, r, :], rinv[:, r, :]))
                        else:
                            step(V.reciprocal(rinv[:, r, :], psumS[:, r, :]))
                        for a in range(2):
                            c = s * 256 + a * P
                            last = V.tensor_tensor(OB[:, qt, c:c + P].rearrange("p (a b) -> p a b", b=HD),
                                                   ps[:, 6 + G % 2, a * 256:(a + 1) * 256].rearrange("p (a b) -> p a b", b=P)[:, :, a * HD:(a + 1) * HD],
                                                   bc(rinv[:, r, 2 * a:2 * a + 2], 2, [P, 2, HD]), ALU.mult)
                        last.then_inc(ob_evac, 1)
                    for u, (s, qt, h) in enumerate(UNITS):
                        kts = key_tiles(s, qt)
                        n = P * len(kts)
                        r = (u // 4) % 2
                        dve.wait_ge(score_done, u + 1)
                        if u >= 3:
                            dve.wait_ge(prob_done, u - 2)
                        src = ps[:, u % 3, 0:n]
                        if s == 0:
                            off = (kts[0] - qt + 1) * P
                            V.tensor_tensor(win(u)[:, 0:n], src, window[:, off:off + n], ALU.add).then_inc(win_done, 1)
                            dve.wait_ge(win_done, u + 1)
                            src = win(u)[:, 0:n]
                        step(V.reduce_max(rmax[:, u % 3:u % 3 + 1], src, axis=AX))
                        V.tensor_scalar(nmx[:, r, h:h + 1], rmax[:, u % 3:u % 3 + 1], -SCALE, nsink[:, h:h + 1] if s == 0 else None,
                                        ALU.mult, *((ALU.min,) if s == 0 else ())).then_inc(max_done, 1)
                        if s == 0 and h == HB - 1:
                            dve.wait_ge(max_done, u + 1)
                            V.tensor_tensor(esk[:, r, :], nmx[:, r, :], sink, ALU.add).then_inc(sink_in, 1)
                        if u % 4 == 2 and u > 4:
                            finish(u // 4 - 1)
                        if u in (8, 16, 24):
                            delta_norm(u // 8 - 1)
                    finish(2 * TT - 1)
                    for m in range(SPLIT):
                        rests(dve, N_IN + m)
                    for k in range(KD):
                        dve.wait_ge(mix_hi, k + 1)
                        V.tensor_tensor(ML[:, k, :], ps[:, k, :], MH[:, k, :], ALU.subtract).then_inc(mix_lo, 1)
                    rests(dve, N_IN + 3)
                    for b in range(8):
                        t, half = divmod(b, 2)
                        dve.wait_ge(passes, 4 * N_IN + 8 * (N_OUT - 1) + b + 1)
                        xs = X[:, t, half * 512:(half + 1) * 512]
                        V.tensor_tensor(xs, xs, ps[:, b, :], ALU.add).then_inc(x_added, 1)

                    dve.wait_ge(e_sq, TT)
                    V.tensor_scalar(st2[:, 0:4], st2[:, 0:4], 1.0 / D, EPS, ALU.mult, ALU.add).then_inc(e_var, 1)
                    dve.wait_ge(e_in, 64)
                    dve.wait_ge(e_std, 1)
                    step(V.reciprocal(st2[:, 4:8], st2[:, 4:8]))
                    for t in range(TT):
                        if t >= 2:
                            dve.wait_ge(hT2_done, 2 * (t - 1))
                            dve.wait_ge(e_hi, t - 1)
                        V.scalar_tensor_tensor(hw[:, t % 2, :], X[:, t, :], st2[:, 4 + t:5 + t], norm2_row[:, :], ALU.mult, ALU.mult).then_inc(h_done, 1)
                        dve.wait_ge(e_hi, t + 1)
                        V.tensor_tensor(EL[:, t, :], hw[:, t % 2, :], EH[:, t, :], ALU.subtract).then_inc(e_lo, 1)
                    dve.wait_ge(logit_done, 1)
                    lg = ps[:, 4, 0:TT * NE].rearrange("p (a b) -> p a b", b=NE)
                    step(V.reduce_max(st2[:, 8:12], lg, axis=AX))
                    V.tensor_tensor(aff[:, :, :], lg, bc(st2[:, 8:12], 2, [P, TT, NE]), ALU.subtract).then_inc(logit_max, 1)
                    dve.wait_ge(logit_exp, 1)
                    step(V.reduce_sum(st2[:, 12:16], aff[:, :, :], axis=AX))
                    step(V.reciprocal(st2[:, 12:16], st2[:, 12:16]))
                    V.tensor_tensor(aff[:, :, :], aff[:, :, :], bc(st2[:, 12:16], 2, [P, TT, NE]), ALU.mult).then_inc(aff_done, 1)
                    dve.wait_ge(affT_done, 1)
                    step(V.tensor_copy(work[:, :], ps[0:NE, 5, :]))
                    for r in range(CAP // 8):
                        b = slice(8 * r, 8 * r + 8)
                        step(V.max(best[:, b], work[:, :]))
                        step(V.max_index(best_at[:, b], best[:, b], work[:, :]))
                        if r < CAP // 8 - 1:
                            step(V.match_replace(work[:, :], best[:, b], work[:, :], -1.0))
                    step(V.tensor_copy(twice[:, 0, 0, :], best_at[:, :]))
                    V.tensor_copy(twice[:, 0, 1, :], twice[:, 0, 0, :])
                    V.tensor_copy(twice[:, 1, :, :], bc(best[:, :], 1, [NE, 2, CAP])).then_inc(chosen, 1)
                    V.tensor_tensor(spread[:, :, :], bc(twice[:, 0, 0, :], 1, [NE, NE, CAP]), bc(ident[0:NE, 0:NE], 2, [NE, NE, CAP]), ALU.mult).then_inc(spread_done, 1)
                    dve.wait_ge(chosen_T, 1)
                    pair = ps[:, 6, 0:NE].rearrange("p (g e) -> p g e", e=2)
                    V.tensor_copy(slot_tok[0:CAP, :], pair[0:CAP, :, 0])
                    V.tensor_copy(slot_tok[CAP:P, :], pair[CAP:P, :, 1])
                    V.tensor_copy(slot_gate[:, :], ps[:, 6, NE:2 * NE])
                    dve.wait_ge(rows_done, 1)
                    V.tensor_copy(idx_rows[:, NE * CAP:], ps[:, 0, 0:2 * CAP])
                    V.tensor_copy(idx_rows[:, 0:NE * CAP], ps[:, 0:2, :].rearrange("p a b -> p (a b)")).then_inc(top_ready, 1)
                    dve.wait_ge(top_ready, 1)

                    def choose(columns):
                        for t in range(TT):
                            last = V.tensor_scalar(sel[:, t, :], idx_rows[:, columns], tokid[:, t:t + 1], None, ALU.is_equal)
                        last.then_inc(sel_done, 1)
                    choose(slice(0, 2 * CAP))
                    V.tensor_copy(gate_now[:, :], slot_gate[:, 0:2])
                    V.tensor_scalar(selT[:, :], iota[:, :], -1.0, None, ALU.is_equal).then_inc(selT_done, 1)
                    for half in range(2):
                        last = V.tensor_scalar(YE[:, half * 512:(half + 1) * 512], iota[:, :], -1.0, None, ALU.is_equal)
                    last.then_inc(ye_done, 1)

                    def to_tokens(g, ns):
                        for n in ns:
                            t, half = divmod(n, 2)
                            dve.wait_ge(scattered, g * 8 + (n + 1))
                            xs = X[:, t, half * 512:(half + 1) * 512]
                            V.tensor_tensor(xs, xs, ps[:, 4 + n % 4, :], ALU.add).then_inc(x_added, 1)
                    with dve.Fori(0, PAIRS) as g:
                        def hidden(n):
                            dve.wait_ge(sg_done, g * 2 + (n + 1))
                            dve.wait_ge(folded, g * 4 + (2 * n + 2))
                            V.tensor_tensor(HM[:, :, :], SG[:, :, :], ps[:, 5, :].rearrange("p (a b) -> p a b", b=CAP), ALU.mult).then_inc(hm_done, 1)

                        def hidden_lo(n):
                            dve.wait_ge(hp_hi, g * 2 + (n + 1))
                            V.tensor_tensor(HP[:, :, CAP:P], HM[:, :, :], HP[:, :, 0:CAP], ALU.subtract).then_inc(hp_lo, 1)

                        def output(n):
                            dve.wait_ge(yt_done, g * 2 + (2 - n))
                            V.scalar_tensor_tensor(YE[n * CAP:(n + 1) * CAP, :], ps[0:CAP, 6:8, :].rearrange("p a b -> p (a b)"),
                                                   gate_now[0:CAP, n:n + 1], YT[:, :], ALU.mult, ALU.add).then_inc(ye_done, 1)

                        def next_choice():
                            dve.wait_ge(gathered, g * 2 + 2)
                            choose(bass.ds(g * P + P, P))

                        def tokens_of_slots():
                            V.tensor_scalar(selT[:, :], iota[:, :], slot_tok[:, bass.ds(g, 1)], None, ALU.is_equal).then_inc(selT_done, 1)
                        def last_pair():
                            output(1)
                            dve.wait_ge(ye_done, g * 2 + 2)
                            V.tensor_copy(gate_now[:, :], slot_gate[:, bass.ds(g * 2, 2)])
                        after = {1: [last_pair], 5: [lambda: to_tokens(g, (0, 1))], 6: [lambda: to_tokens(g, (2, 3))],
                                 9: [lambda: to_tokens(g, (4, 5))], 10: [lambda: to_tokens(g, (6, 7)), tokens_of_slots],
                                 13: [lambda: hidden(0), lambda: hidden_lo(0)], 15: [next_choice], 18: [lambda: output(0)],
                                 22: [lambda: hidden(1), lambda: hidden_lo(1)]}
                        for q in range(TURN):
                            if not by_pool(q):
                                expert_rests(dve, g, q)
                            for work_ in after.get(q, ()):
                                work_()
                    dve.wait_ge(yt_done, PAIRS * 2 + 1)
                    V.scalar_tensor_tensor(YE[CAP:P, :], ps[0:CAP, 6:8, :].rearrange("p a b -> p (a b)"),
                                           gate_now[0:CAP, 1:2], YT[:, :], ALU.mult, ALU.add).then_inc(ye_done, 1)
                    to_tokens(PAIRS, range(8))

                @block.gpsimd
                def _(pool):
                    G = nc.gpsimd
                    chained = [0]

                    def step(ins):
                        chained[0] += 1
                        ins.then_inc(p_chain, 1)
                        pool.wait_ge(p_chain, chained[0])
                    G.memset(XP[:, :, 0:2], 0.0)
                    G.memset(XP[:, :, SEQ + 2:SEQ + 4], 0.0).then_inc(pad_set, 1)
                    pool.wait_ge(par_in, 32)
                    at = 0
                    for j, heads in enumerate((4, 2, 4, 2)):
                        last = G.tensor_copy(GN[:, at:at + heads, :], bc(gains[:, j, :], 1, [P, heads, HD]))
                        at += heads
                    last.then_inc(gain_set, 1)
                    pool.wait_ge(proj_evac, 3 * TT)
                    for t in range(TT):
                        if t >= 2:
                            pool.wait_ge(r_ss, t - 1)
                        G.tensor_tensor(squares(t).rearrange("p (s a b) -> p s a b", s=2, b=HD), qk(t), qk(t), ALU.mult).then_inc(r_sq, 1)
                    pool.wait_ge(r_scale, 1)
                    pool.wait_ge(gain_set, 1)
                    pool.wait_ge(const_in, 5 * 16)
                    for t in range(TT):
                        step(G.tensor_tensor(qk(t), qk(t), bc(rsR[:, t, :].rearrange("p (s a) -> p s a", s=2), 3, [P, 2, 6, HD]), ALU.mult))
                        step(G.tensor_tensor(qk(t), qk(t), GN[:, :, :].rearrange("p (s a) b -> p s a b", s=2), ALU.mult))
                        if t > 0:
                            pool.wait_ge(rope_done, t)
                        q = PR[:, t, AT0:AT0 + 1024].rearrange("p (s c) -> p s c", s=2)
                        for s in range(2):
                            src = q[:, s, 0:VOFF].rearrange("p (a b) -> p a b", b=HD)
                            c_ = rotary(0, s).rearrange("p (a b) -> p a b", b=HD)
                            G.tensor_tensor(c_, src, bc(cosT[:, s, t, :], 1, [P, 6, HD]), ALU.mult)
                            w = HD // 2 if s == 0 else HD // 4
                            m = HD // (2 * w)
                            srcv = q[:, s, 0:VOFF].rearrange("p (a m z w) -> p a m z w", m=m, z=2, w=w)
                            dstv = rotary(1, s).rearrange("p (a m z w) -> p a m z w", m=m, z=2, w=w)
                            sinv = sinT[:, s, t, :].rearrange("p (m z w) -> p m z w", z=2, w=w)
                            for z in range(2):
                                a, b, c = dstv[:, :, :, z, :], srcv[:, :, :, 1 - z, :], sinv[:, :, z, :]
                                last = G.tensor_tensor(a, b, bc(c, 1, [P, 6, m, w]), ALU.mult)
                        step(last)
                        for s in range(2):
                            c_, r_, o_ = (v.rearrange("p (a b) -> p a b", b=HD) for v in (rotary(0, s), rotary(1, s), q[:, s, 0:VOFF]))
                            G.tensor_tensor(o_[:, 0:4, :].rearrange("p (j i) b -> p i j b", j=2),
                                            c_[:, 0:4, :].rearrange("p (i j) b -> p i j b", i=2),
                                            r_[:, 0:4, :].rearrange("p (i j) b -> p i j b", i=2), ALU.add)
                            last = G.tensor_tensor(o_[:, 4:6, :], c_[:, 4:6, :], r_[:, 4:6, :], ALU.add)
                        last.then_inc(rope_done, 1)
                    pool.wait_ge(tok_T, 12)
                    G.memset(S[:, :, :, :], 0.0).then_inc(s_zero, 1)
                    pool.wait_ge(s_zero, 1)
                    pool.wait_ge(const_in, 5 * 16)
                    pool.wait_ge(g_ready, 1)
                    pool.wait_ge(proj_evac, 4 * GROUPS)
                    for t in range(TT):
                        for d in range(2):
                            i = 2 * t + d
                            B = delta[d]
                            if t > 0:
                                pool.wait_ge(x_done, 12 * t + d - 1)
                            G.tensor_tensor(B["NM"][:, :, :], bc(cum[:, d, :], 1, [P, HA, P]),
                                            bc(gdec[:, tile_of(d, t), d * HA:(d + 1) * HA], 2, [P, HA, P]), ALU.mult).then_inc(gu_ready, 1)
                        for d in range(2):
                            i = 2 * t + d
                            tl = tile_of(d, t)
                            B = delta[d]
                            pool.wait_ge(dm_exp, i + 1)
                            G.tensor_tensor(B["DM"][:, :, :], B["DM"][:, :, :], bc(cum[:, d, :], 1, [P, HA, P]), ALU.mult).then_inc(masked, 1)
                            pool.wait_ge(masked, i + 1)
                            G.tensor_tensor(B["NT"][:, :, :], B["DM"][:, :, :], bc(beta[:, tl, d * HA:(d + 1) * HA], 2, [P, HA, P]), ALU.mult).then_inc(nt_base, 1)
                        for l in range(7):
                            for d in range(2):
                                i = 2 * t + d
                                B = delta[d]
                                if l == 0:
                                    pool.wait_ge(nt_done, i + 1)
                                    pool.wait_ge(row_done, i + 1)
                                elif l == 1:
                                    pool.wait_ge(t0_done, i + 1)
                                else:
                                    pool.wait_ge(x_done, (6 * t + l - 2) * 2 + d + 1)
                                G.tensor_tensor(B["NM"][:, :, :], B["NT"][:, :, :], bc(level[:, l, :], 1, [P, HA, P]), ALU.mult).then_inc(nm_done, 1)
                            if l == 1:
                                for d in range(2):
                                    i = 2 * t + d
                                    tl = tile_of(d, t)
                                    B = delta[d]
                                    pool.wait_ge(cum_exp, 1)
                                    pool.wait_ge(qk_normed, 8)
                                    if t > 0:
                                        pool.wait_ge(w_done, i - 1)
                                        pool.wait_ge(s_done, i - 1)
                                    G.tensor_tensor(B["KG"][:, :, :], KN[:, tl, :, :], bc(egc[:, d, tl, :], 2, [P, HA, P]), ALU.mult).then_inc(kgd_done, 1)
                                    G.tensor_tensor(B["KD"][:, :, :], KN[:, tl, :, :], bc(kdc[:, d, tl, :], 2, [P, HA, P]), ALU.mult).then_inc(kgd_done, 1)
                        if t < TT - 1:
                            for d in range(2):
                                i = 2 * t + d
                                pool.wait_ge(o_done, i + 1)
                                if t > 0:
                                    pool.wait_ge(s_new, i - 1)
                                G.tensor_tensor(S[:, d, :, :], S[:, d, :, :], bc(egl[:, d, tile_of(d, t), :], 2, [P, HA, P]), ALU.mult).then_inc(s_dec, 1)
                    pool.wait_ge(x_added, 8)
                    G.tensor_tensor(fold[:, :], ident[:, 0:CAP], ident[:, CAP:P], ALU.add).then_inc(fold_set, 1)
                    with pool.Fori(0, PAIRS) as g:
                        for q in range(TURN):
                            if by_pool(q):
                                expert_rests(pool, g, q)
            nc.all_engine_barrier(sems_to_clear=range(raw_full[0].num, slot_free.num + 1))
        with nc.Block() as block:
            @block.sync
            def _(sp):
                sp.dma_start(out.rearrange("o (t p) d -> p (o t) d", p=P), X[:, :, :]).then_inc(s_out, 16)
                sp.wait_ge(s_out, 16)


_INS = ["x", "rows", "cols", "norm2", "w_in", "w_out", "w_router", "w_gate", "w_up", "w_down", "consts"]
_OUTS = [((1, SEQ, D), "float32")]


def kernel(**inputs):
    import numpy as _np
    import concourse.bacc as _bacc
    from concourse import mybir as _mybir
    from concourse.bass_utils import run_bass_kernel_spmd as _run

    i = {k: _np.asarray(v) for k, v in inputs.items()}
    laid = {k: i[k] for k in ("x", "w_in", "w_out", "w_router", "w_gate", "w_up", "w_down")}
    laid["rows"] = _np.concatenate([i["a_log"].reshape(LAYERS, -1), i["dt_bias"].reshape(LAYERS, -1), i["a_norm_g"],
                                    i["b_qnorm_g"], i["b_knorm_g"], i["c_qnorm_g"], i["c_knorm_g"], i["b_sink"]], 1)
    laid["cols"] = _np.concatenate([i["norm1_g"].reshape(LAYERS, KD, P).transpose(0, 2, 1),
                                    i["conv_w"].reshape(LAYERS, 5, NQKV, P).transpose(0, 3, 2, 1).reshape(LAYERS, P, -1)], 2)
    laid["norm2"] = i["norm2_g"]
    laid["consts"] = constants()
    nc = _bacc.Bacc("TRN2", target_bir_lowering=False, num_devices=1)
    arrays, args = {}, []
    for name in _INS:
        a = _np.ascontiguousarray(laid[name])
        arrays[f"in_{name}_dram"] = a
        args.append(nc.dram_tensor(f"in_{name}_dram", a.shape, _mybir.dt.from_np(a.dtype), kind="ExternalInput").ap())
    for n, (shape, dtype) in enumerate(_OUTS):
        args.append(nc.dram_tensor(f"out_{n}_dram", shape, _mybir.dt.from_np(_np.dtype(dtype)), kind="ExternalOutput").ap())
    bass_hybrid_encoder(nc, *args)
    r = _run(nc, [arrays], core_ids=[0])
    return r.results[0]["out_0_dram"]
```

```python
from contextlib import ExitStack

import numpy as np

import concourse.bass as bass
from concourse import mybir

ALU = mybir.AluOpType
ACT = mybir.ActivationFunctionType
F32 = mybir.dt.float32
F32R = mybir.dt.float32r
U32 = mybir.dt.uint32
AX = mybir.AxisListType.X

P = 128
EPS = 1e-6

LAYERS = 2
SEQ = 512
D = 1024
TT = SEQ // P
KD = D // P
HA = 4
NQKV = 3 * HA
PROJ = 3088
REST = PROJ - NQKV * P
HD = 64
HB = 4
NSLOT = 12
NE = 16
CAP = 2 * SEQ // NE
DE = 1024
Z0, BA0, AT0 = 0, 512, 528
VOFF = 384

GROUPS = 7
FIRST_QKV = 3
REST_OF = {0: 1, 1: 2, 2: 3, 6: 0}
RW = REST // 4
PIECE = 2048
RAW_A = 3
SPLIT = 3
N_IN = 2 * GROUPS
N_OUT = 4
SCALE = HD ** -0.5
RAW_M = 6
SPLIT_M = 4
PAIRS = NE // 2
PER = 12
TURN = 2 * PER
GATE, UP, DOWN = range(3)
STREAM = [(GATE, 0), (UP, 0), (GATE, 1), (DOWN, 0), (UP, 1), (DOWN, 1)]
BY_POOL = (5, 10, 20)
LOADS_A = (N_IN + N_OUT) // RAW_A

CONST_COLS = dict(ident=P, cum=2 * P, level=7 * P, window=3 * P, cos=2 * TT * HD, sin=2 * TT * HD,
                  iota=SEQ, tokid=TT)


def constants():
    p = np.arange(P)
    c = {"ident": np.eye(P)}
    c["cum"] = np.stack([p[:, None] <= p[None, :], p[:, None] >= p[None, :]], 1).reshape(P, -1)
    c["level"] = np.stack([(p[:, None] >> (l + 1) == p[None, :] >> (l + 1))
                           & (p[:, None] >> l != p[None, :] >> l) for l in range(7)], 1).reshape(P, -1)
    w = np.zeros((P, 3, P))
    w[:, 0] = np.where(p[None, :] >= p[:, None], 0.0, -1e30)
    w[:, 2] = np.where(p[None, :] <= p[:, None], 0.0, -1e30)
    c["window"] = w.reshape(P, -1)
    f = np.float32

    def table(pos, dim):
        inv = f(10000.0) ** (-np.arange(0, dim, 2, dtype=f) / f(dim))
        ang = pos.astype(f)[:, None] * inv[None, :]
        sign = np.concatenate([-np.ones(dim // 2), np.ones(dim // 2)])
        ang = np.concatenate([ang, ang], -1)
        return np.cos(ang), np.sin(ang) * sign
    pos = np.arange(SEQ)
    one, row, col = table(pos, HD), table(pos // 64, HD // 2), table(pos % 64, HD // 2)
    for n, key in enumerate(("cos", "sin")):
        t = np.stack([one[n], np.concatenate([row[n], col[n]], -1)], 1)
        c[key] = t.reshape(TT, P, 2, HD).transpose(1, 2, 0, 3).reshape(P, -1)
    c["iota"] = np.broadcast_to(np.arange(SEQ), (P, SEQ))
    c["tokid"] = p[:, None] + P * np.arange(TT)[None, :]
    return np.concatenate([c[k].astype(f) for k in CONST_COLS], 1)


def const_at(name):
    at = 0
    for k, n in CONST_COLS.items():
        if k == name:
            return at, n
        at += n


ROW_COLS = dict(a_log=8, dt_bias=8, a_norm=P, gains=4 * HD, sink=HB)
ROWS = sum(ROW_COLS.values())
COLS = KD + NQKV * 5


def bc(ap, axis, shape):
    return ap.unsqueeze(axis).to_broadcast(shape)


def bass_hybrid_encoder(nc, x, rows, cols, norm2, w_in, w_out, w_router, w_gate, w_up, w_down, consts, out):
    ctx = ExitStack()
    with ctx:
        def sem(name):
            return ctx.enter_context(nc.semaphore(name))

        def sb(name, shape, dt=F32, at=None):
            return (at or ctx).enter_context(nc.sbuf_tensor(name, shape, dt))

        X = sb("X", [P, TT, D])
        ident = sb("ident", [P, P])
        ones = sb("ones", [P, P])
        ssX = sb("ssX", [P, TT])
        row = sb("row", [P, ROWS])
        col = sb("col", [P, COLS])
        raw = [sb(f"raw{i}", [P, PIECE]) for i in range(RAW_A)]
        one = ExitStack()
        delta = [{n: sb(f"{n}{d}", [P, HA, P], at=one)
                  for n in ("DM", "NT", "NM", "T", "TTr", "XS", "AT", "WT", "QG", "KD", "KG", "VN")}
                 for d in range(2)]
        one.close()
        whi = [sb(f"whi{i}", [P, PIECE], F32R) for i in range(SPLIT)]
        wlo = [sb(f"wlo{i}", [P, PIECE], F32R) for i in range(SPLIT)]
        mixer = ExitStack()
        one = ExitStack()
        QT, KT = (sb(n, [P, HA, SEQ], at=one) for n in ("QT", "KT"))
        KN, VN_ = (sb(n, [P, TT, HA, P], at=one) for n in ("KN", "VA"))
        one.close()
        MH, ML = (sb(n, [P, KD, SEQ], F32R, at=mixer) for n in ("MH", "ML"))
        one = ExitStack()
        HH, HL = (sb(n, [P, KD, SEQ], F32R, at=one) for n in ("HH", "HL"))
        one.close()
        one = ExitStack()
        spare = [{n: sb(f"{n}{d}b", [P, HA, P], at=one) for n in ("NT", "AT", "QG", "GU")} for d in range(2)]
        one.close()
        AQH, AQL = (sb(n, [P, 6, SEQ], F32R, at=mixer) for n in ("AQH", "AQL"))
        O = sb("O", [P, TT, HA, P], at=mixer)
        one = ExitStack()
        XN = sb("XN", [P, TT, D], at=one)
        one.close()
        PR = sb("PR", [P, TT, REST], at=mixer)
        one = ExitStack()
        XP = sb("XP", [P, 2, SEQ + 4], at=one)
        VD = sb("VD", [P, HA, SEQ], at=one)
        one.close()
        OB = sb("OB", [P, TT, 2 * HB * HD], at=mixer)
        S = sb("S", [P, 2, HA, P], at=mixer)
        sb("conv_rest", [P, 8], at=mixer)
        cum = sb("cum", [P, 2, P], at=mixer)
        level = sb("level", [P, 7, P], at=mixer)
        window = sb("window", [P, 3 * P], at=mixer)
        cosT = sb("cosT", [P, 2, TT, HD], at=mixer)
        sinT = sb("sinT", [P, 2, TT, HD], at=mixer)
        GN = sb("GN", [P, NSLOT, HD], at=mixer)
        st = sb("st", [P, 640], at=mixer)
        mixer.close()
        raw += [sb(f"raw{i}", [P, PIECE]) for i in range(RAW_A, RAW_M)]
        whi += [sb(f"whi{i}", [P, PIECE], F32R) for i in range(SPLIT, SPLIT_M)]
        wlo += [sb(f"wlo{i}", [P, PIECE], F32R) for i in range(SPLIT, SPLIT_M)]
        EH, EL = (sb(n, [P, TT, D], F32R) for n in ("EH", "EL"))
        idx_rows = sb("idx_rows", [P, (NE + 2) * CAP])
        sel = sb("sel", [P, TT, 2 * CAP], F32R)
        one = ExitStack()
        norm2_row = sb("norm2_row", [P, D], at=one)
        router = sb("router", [P, KD, NE], at=one)
        one.close()
        XE = sb("XE", [P, KD, 2, P], F32R)
        selT = sb("selT", [P, SEQ])
        one = ExitStack()
        HT = sb("HT", [P, KD, SEQ], at=one)
        one.close()
        one = ExitStack()
        aff = sb("aff", [P, TT, NE], at=one)
        work = sb("work", [NE, SEQ], at=one)
        best = sb("best", [NE, CAP], at=one)
        best_at = sb("best_at", [NE, CAP], U32, at=one)
        twice = sb("twice", [NE, 2, 2, CAP], at=one)
        spread = sb("spread", [NE, NE, CAP], at=one)
        one.close()
        GU = sb("GU", [P, 2, DE])
        YT = sb("YT", [CAP, D])
        YE = sb("YE", [P, D])
        one = ExitStack()
        hw = sb("hw", [P, 2, D], at=one)
        one.close()
        SG = sb("SG", [P, DE // P, CAP])
        HM = sb("HM", [P, DE // P, CAP])
        HP = sb("HP", [P, DE // P, P], F32R)
        iota = sb("iota", [P, SEQ])
        tokid = sb("tokid", [P, TT])
        fold = sb("fold", [P, CAP])
        slot_tok = sb("slot_tok", [P, PAIRS])
        slot_gate = sb("slot_gate", [P, NE])
        gate_now = sb("gate_now", [P, 2])
        st2 = sb("st2", [P, 32])
        ps = ctx.enter_context(nc.psum_tensor("ps", [P, 8, 512], F32))

        used = [0]

        def small(*shape):
            n = int(np.prod(shape))
            v = st[:, used[0]:used[0] + n]
            used[0] += n
            if len(shape) == 2:
                return v.rearrange("p (a b) -> p a b", b=shape[1])
            if len(shape) == 3:
                return v.rearrange("p (a b c) -> p a b c", b=shape[1], c=shape[2])
            return v
        ss1, rs1 = small(TT), small(TT)
        ssA, rsA = small(2, TT, HA), small(2, TT, HA)
        zb, tb, eb, lb = (small(TT, 8) for _ in range(4))
        beta, gdec = small(TT, 8), small(TT, 8)
        gcc, gll = small(2, TT, HA), small(2, TT, HA)
        egc, egl, kdc = small(2, TT, HA), small(2, TT, HA), small(2, TT, HA)
        ea = small(8)
        ssR, rsR = small(TT, NSLOT), small(TT, NSLOT)
        ssO, rsO = small(TT, HA), small(TT, HA)
        nsink = small(HB)
        rmax, nmx = small(3), small(2, HB)
        psumS, rinv, esk = small(2, HB), small(2, HB), small(2, HB)

        a_log, dt_b = row[:, 0:8], row[:, 8:16]
        a_norm = row[:, 16:16 + P]
        gains = row[:, 16 + P:16 + P + 4 * HD].rearrange("p (a b) -> p a b", b=HD)
        sink = row[:, 16 + P + 4 * HD:ROWS]
        g1 = col[:, 0:KD]
        cw = col[:, KD:COLS].rearrange("p (c j) -> p c j", j=5)

        s_init, ones_set, s_out = sem("s_init"), sem("ones_set"), sem("s_out")
        raw_full = [sem(f"raw_full{i}") for i in range(RAW_M)]
        par_in, const_in = sem("par_in"), sem("const_in")
        hi_done, lo_done, passes = sem("hi_done"), sem("lo_done"), sem("passes")
        x_sq, x_var, x_std, x_normed = (sem(n) for n in ("x_sq", "x_var", "x_std", "x_normed"))
        xT_done, hT_hi, hT_lo = sem("xT_done"), sem("hT_hi"), sem("hT_lo")
        pad_set, proj_evac, tap0, conv_done, silu_done = (sem(n) for n in ("pad_set", "proj_evac", "tap0", "conv_done", "silu_done"))
        conv_step = sem("conv_step")
        tok_T, tok_evac, tok_sq, tok_ss = (sem(n) for n in ("tok_T", "tok_evac", "tok_sq", "tok_ss"))
        v_chain, p_chain = sem("v_chain"), sem("p_chain")
        qk_var, qk_std, qk_normed, back_T, back_evac = (sem(n) for n in ("qk_var", "qk_std", "qk_normed", "back_T", "back_evac"))
        gate_z, gate_e, gate_w, gate_ln, g_ready = (sem(n) for n in ("gate_z", "gate_e", "gate_w", "gate_ln", "g_ready"))
        cum_done, cum_evac, cum_diff, cum_exp = (sem(n) for n in ("cum_done", "cum_evac", "cum_diff", "cum_exp"))
        gu_ready, row_done, diff_done, dm_exp, eg_exp, masked, nt_base = (sem(n) for n in ("gu_ready", "row_done", "diff_done", "dm_exp", "eg_exp", "masked", "nt_base"))
        qk_done, kk_done, at_done, nt_done, qg_done, kgd_done = (sem(n) for n in ("qk_done", "kk_done", "at_done", "nt_done", "qg_done", "kgd_done"))
        nm_done, t0_done, t0_T, t0_evac = (sem(n) for n in ("nm_done", "t0_done", "t0_T", "t0_evac"))
        x_done, x_evac, yt_sum, y_done, t_new = (sem(n) for n in ("x_done", "x_evac", "yt_sum", "y_done", "t_new"))
        w_done, w_evac, v_done, vn_done, o_done, o_evac = (sem(n) for n in ("w_done", "w_evac", "v_done", "vn_done", "o_done", "o_evac"))
        s_done, s_dec, s_new, s_zero = (sem(n) for n in ("s_done", "s_dec", "s_new", "s_zero"))
        r_sq, r_ss, r_std, rope_done, aq_T, aq_evac, aq_lo, gain_set = (sem(n) for n in ("r_sq", "r_ss", "r_std", "rope_done", "aq_T", "aq_evac", "aq_lo", "gain_set"))
        score_done, win_done, max_done, prob_done, pT_done, pT_evac, pv_done, ob_evac = (sem(n) for n in ("score_done", "win_done", "max_done", "prob_done", "pT_done", "pT_evac", "pv_done", "ob_evac"))
        sink_in, sink_exp = sem("sink_in"), sem("sink_exp")
        oa_var, oa_std, o_sums, z_silu, oa_done, r_var, r_scale = (sem(n) for n in ("oa_var", "oa_std", "o_sums", "z_silu", "oa_done", "r_var", "r_scale"))
        mix_T, mix_hi, mix_lo, x_added = (sem(n) for n in ("mix_T", "mix_hi", "mix_lo", "x_added"))
        e_in, fold_set, e_sq, e_var, e_std, h_done, e_hi, e_lo, hT2_done, hT2_evac = (sem(n) for n in (
            "e_in", "fold_set", "e_sq", "e_var", "e_std", "h_done", "e_hi", "e_lo", "hT2_done", "hT2_evac"))
        logit_done, logit_rows, logit_T, logit_max, logit_exp, aff_done, affT_done, chosen, chosen_T, spread_done, rows_done, top_ready = (sem(n) for n in (
            "logit_done", "logit_rows", "logit_T", "logit_max", "logit_exp", "aff_done", "affT_done", "chosen", "chosen_T", "spread_done", "rows_done", "top_ready"))
        m_hi, m_lo, m_lo_pool, m_pass = (sem(n) for n in ("m_hi", "m_lo", "m_lo_pool", "m_pass"))
        sel_done, selT_done, gathered, xe_evac = (sem(n) for n in ("sel_done", "selT_done", "gathered", "xe_evac"))
        gu_evac, folded, sg_done, hm_done, hp_hi, hp_lo = (sem(n) for n in ("gu_evac", "folded", "sg_done", "hm_done", "hp_hi", "hp_lo"))
        yt_done, ye_done, zeroed, scattered = (sem(n) for n in ("yt_done", "ye_done", "zeroed", "scattered"))
        slot_free = sem("slot_free")

        def piece_view(t, n):
            if n >= N_IN:
                return t[:, :].rearrange("p (k c) -> p k c", k=2)
            w = RW if n // 2 in REST_OF else 512
            return t[:, 0:4 * w].rearrange("p (k c) -> p k c", k=4)

        def piece_dram(L, n):
            if n >= N_IN:
                m = n - N_IN
                return w_out[bass.ds(L, 1), m * 2 * P:(m + 1) * 2 * P, :].rearrange("l (k p) c -> p (l k) c", p=P)
            g, half = divmod(n, 2)
            c0, w = (NQKV * P + REST_OF[g] * RW, RW) if g in REST_OF else ((g - FIRST_QKV) * 512, 512)
            return w_in[bass.ds(L, 1), half * 4 * P:(half + 1) * 4 * P, c0:c0 + w].rearrange("l (k p) c -> p (l k) c", p=P)

        def qk(t):
            return PR[:, t, AT0:AT0 + 1024].rearrange("p (s c) -> p s c", s=2)[:, :, 0:VOFF].rearrange("p s (a b) -> p s a b", b=HD)

        def squares(t):
            a = t % 2 * 2 * VOFF
            return VN_[:, :, :, :].rearrange("p a b c -> p (a b c)")[:, a:a + 2 * VOFF]

        def rotary(z, s):
            a = (2 * z + s) * VOFF
            return KN[:, :, :, :].rearrange("p a b c -> p (a b c)")[:, a:a + VOFF]

        TOK = [(c, t) for c in (1, 0, 2) for t in range(TT)]

        def tok_bank(i):
            return 4 + i % 4 if i < 8 else i - 8

        def sq_rows(i):
            return VN_[:, i % 2, :, :]

        UNITS = [(s, qt, h) for s in range(2) for qt in range(TT) for h in range(HB)]

        ROUND_AT = (5, 7, 13, 15, 21, 23)
        REST_AT = (11, 13, 19, 21, 27, 29)

        def out_half(ring, m, half):
            n = N_IN + m
            t = ring[n % (RAW_A if ring is raw else SPLIT)]
            return t[:, half * (PIECE // 2):(half + 1) * (PIECE // 2)]

        def key_tiles(s, qt):
            return range(max(0, qt - 1), min(TT, qt + 2)) if s == 0 else range(TT)

        def tile_of(d, t):
            return t if d == 0 else TT - 1 - t

        def buf(name, d, t):
            return (delta, spare)[t % 2][d][name][:, :, :]

        def bank_heads(bank):
            return ps[:, bank, :].rearrange("p (a b) -> p a b", b=P)

        flight = [[KT[:, u, :], KN[:, u, :, :].rearrange("p a b -> p (a b)"), VN_[:, u, :, :].rearrange("p a b -> p (a b)")] for u in range(3)]

        def win(u):
            return flight[u % 3][0]

        def prob(u):
            return flight[u % 3][1]

        def probT(u):
            return flight[u % 3][2]

        def rounds(eng, n):
            eng.wait_ge(raw_full[n % RAW_A], 16 * (n // RAW_A + 1))
            if n >= SPLIT:
                m = n - SPLIT
                eng.wait_ge(passes, 4 * (m + 1) if m < N_IN else 4 * N_IN + 8 * (m - N_IN + 1))
            nc.scalar.activation(piece_view(whi[n % SPLIT], n), piece_view(raw[n % RAW_A], n), ACT.Copy).then_inc(hi_done, 1)

        def rests(eng, n):
            eng.wait_ge(hi_done, n + 1)
            nc.vector.tensor_tensor(piece_view(wlo[n % SPLIT], n), piece_view(raw[n % RAW_A], n),
                                    piece_view(whi[n % SPLIT], n), ALU.subtract).then_inc(lo_done, 1)

        def expert_dram(L, g, q):
            (m, e), j = STREAM[q // 4], q % 4
            w = (w_gate, w_up, w_down)[m]
            return w[bass.ds(L, 1), bass.ds(g * 2 + e, 1), j * 2 * P:(j + 1) * 2 * P, :].rearrange("l e (k p) c -> p (l e k) c", p=P)

        def two(t):
            return t[:, :].rearrange("p (k c) -> p k c", k=2)

        def by_pool(q):
            return q in BY_POOL

        def dve_split(q):
            return sum(not by_pool(p) for p in range(q + 1))
        DVE_TURN, POOL_TURN = dve_split(TURN - 1), TURN - dve_split(TURN - 1)

        def wait_split(eng, g, q):
            if by_pool(q):
                eng.wait_ge(m_lo_pool, g * POOL_TURN + (q + 1 - dve_split(q)))
            else:
                eng.wait_ge(m_lo, g * DVE_TURN + dve_split(q))

        def expert_rounds(eng, g, q):
            slot = q % RAW_M
            eng.wait_ge(raw_full[slot], (g * (TURN // RAW_M) + (q // RAW_M + 1 + (LOADS_A if slot < RAW_A else 0))) * 16)
            eng.wait_ge(m_pass, g * TURN + (q + 1))
            nc.scalar.activation(whi[q % SPLIT_M][:, :], raw[slot][:, :], ACT.Copy).then_inc(m_hi, 1)

        def expert_rests(eng, g, q):
            eng.wait_ge(m_hi, g * TURN + (q + 1))
            o, a, b = wlo[q % SPLIT_M][:, :], raw[q % RAW_M][:, :], whi[q % SPLIT_M][:, :]
            if by_pool(q):
                nc.gpsimd.tensor_tensor(o, a, b, ALU.subtract).then_inc(m_lo_pool, 1)
            else:
                nc.vector.tensor_tensor(o, a, b, ALU.subtract).then_inc(m_lo, 1)

        with nc.Block() as block:
            @block.sync
            def _(sp):
                sp.dma_start(X[:, :, :], x.rearrange("o (t p) d -> p (o t) d", p=P)).then_inc(s_init, 16)
                a, n = const_at("ident")
                sp.dma_start(ident[:, :], consts[:, a:a + n]).then_inc(s_init, 16)
                sp.wait_ge(s_init, 32)
                sp.wait_ge(ones_set, 1)

            @block.gpsimd
            def _(pool):
                nc.gpsimd.memset(ones[:, :], 1.0).then_inc(ones_set, 1)

        with nc.Fori(0, LAYERS) as L:
            with nc.Block() as block:
                @block.sync
                def _(sp):
                    for n in range(2):
                        sp.dma_start(piece_view(raw[n], n), piece_dram(L, n)).then_inc(raw_full[n % RAW_A], 16)
                    sp.dma_start(row[:, :], rows[bass.ds(L, 1), :].to_broadcast([P, ROWS])).then_inc(par_in, 16)
                    sp.dma_start(col[:, :], cols[bass.ds(L, 1), :, :].rearrange("l p c -> p (l c)")).then_inc(par_in, 16)
                    for name, dst in (("cum", cum[:, :, :]), ("level", level[:, :, :]), ("window", window[:, :]),
                                      ("cos", cosT[:, :, :, :]), ("sin", sinT[:, :, :, :])):
                        a, n = const_at(name)
                        src = consts[:, a:a + n]
                        if name in ("cum", "level"):
                            src = src.rearrange("p (a b) -> p a b", b=P)
                        elif name != "window":
                            src = src.rearrange("p (a b c) -> p a b c", b=TT, c=HD)
                        sp.dma_start(dst, src).then_inc(const_in, 16)
                    for n in range(2, N_IN + N_OUT):
                        if n >= RAW_A:
                            sp.wait_ge(lo_done, n - RAW_A + 1)
                        sp.dma_start(piece_view(raw[n % RAW_A], n), piece_dram(L, n)).then_inc(raw_full[n % RAW_A], 16)

                    sp.wait_ge(mix_T, KD)
                    sp.dma_start(norm2_row[:, :], norm2[bass.ds(L, 1), :].to_broadcast([P, D])).then_inc(e_in, 16)
                    sp.dma_start(router[:, :, :], w_router[bass.ds(L, 1), :, :].rearrange("l (k p) e -> p (l k) e", p=P)).then_inc(e_in, 16)
                    for name, dst in (("iota", iota[:, :]), ("tokid", tokid[:, :])):
                        a, n = const_at(name)
                        sp.dma_start(dst, consts[:, a:a + n]).then_inc(e_in, 16)
                    for i in range(RAW_A):
                        sp.wait_ge(lo_done, N_IN + N_OUT - RAW_A + i + 1)
                        sp.dma_start(two(raw[i]), expert_dram(L, 0, i)).then_inc(raw_full[i], 16)
                    sp.wait_ge(x_added, 8)
                    for i in range(RAW_A, RAW_M):
                        sp.dma_start(two(raw[i]), expert_dram(L, 0, i)).then_inc(raw_full[i], 16)

                    def refill(g, q):
                        n = q + RAW_M
                        src = expert_dram(L, g + n // TURN, n % TURN)
                        wait_split(sp, g, q)
                        sp.sem_inc(slot_free, 1)
                        sp.dma_start(two(raw[q % RAW_M]), src).then_inc(raw_full[q % RAW_M], 16)
                    with sp.Fori(0, PAIRS - 1) as g:
                        for q in range(TURN):
                            refill(g, q)
                    for q in range(TURN - RAW_M):
                        refill(PAIRS - 1, q)

                @block.tensor
                def _(pe):
                    mm = nc.tensor.matmul
                    pe.wait_ge(x_normed, TT)
                    for k in range(KD):
                        for t in range(TT):
                            last = nc.tensor.transpose(ps[:, k, t * P:(t + 1) * P], XN[:, t, k * P:(k + 1) * P], ident[:, :])
                        last.then_inc(xT_done, 1)
                    def to_rows(part):
                        pe.wait_ge(silu_done, (8, 8, NQKV)[part])
                        for i in range(4 * part, 4 * part + 4):
                            c, t = TOK[i]
                            if i < 4:
                                pe.wait_ge(proj_evac, 24)
                            elif i < 8:
                                pe.wait_ge(tok_sq, i - 3)
                            elif i == 11:
                                pe.wait_ge(cum_evac, 1)
                            for h in range(HA):
                                src = (QT, KT, VD)[c][:, h, t * P:(t + 1) * P]
                                last = nc.tensor.transpose(ps[:, tok_bank(i), h * P:(h + 1) * P], src, ident[:, :])
                            last.then_inc(tok_T, 1)
                    for g in range(GROUPS):
                        for half in range(2):
                            n = 2 * g + half
                            pe.wait_ge(lo_done, n + 1)
                            if g == 0:
                                pe.wait_ge(hT_lo, 4 * (half + 1))
                            if g == 1:
                                pe.wait_ge(hT_lo, KD)
                            if n == N_IN - 1:
                                to_rows(0)
                            hi, lo = piece_view(whi[n % SPLIT], n), piece_view(wlo[n % SPLIT], n)
                            for t in range(4):
                                if g >= 2 and half == 0:
                                    pe.wait_ge(proj_evac, 4 * (g - 2) + t + 1)
                                b = 4 * (g % 2) + t
                                for kk in range(4):
                                    k = 4 * half + kk
                                    for j, (w, h) in enumerate(((hi, HH), (lo, HH), (hi, HL))):
                                        flags = dict(start=half == 0 and kk == 0 and j == 0, stop=half == 1 and kk == 3 and j == 2)
                                        if g not in REST_OF:
                                            last = mm(ps[:, b, :], w[:, kk, t * P:(t + 1) * P], h[:, k, :], **flags)
                                        else:
                                            last = mm(ps[:, b, 0:RW], h[:, k, t * P:(t + 1) * P], w[:, kk, :], **flags)
                                last.then_inc(passes, 1)
                    to_rows(1)
                    pe.wait_ge(g_ready, 1)
                    pe.wait_ge(const_in, 5 * 16)
                    pe.wait_ge(proj_evac, 4 * GROUPS)
                    for d in range(2):
                        g = gdec[:, :, d * HA:(d + 1) * HA]
                        mm(ps[:, 3, d * 16:(d + 1) * 16], cum[:, d, :], g, start=True, stop=True)
                        last = mm(ps[:, 3, 32 + d * 16:48 + d * 16], ones[:, :], g, start=True, stop=True)
                    last.then_inc(cum_done, 1)
                    to_rows(2)
                    for i, (c, h) in enumerate((c, h) for c in (1, 0) for h in range(HA)):
                        if h == 0:
                            pe.wait_ge(qk_normed, i + 4)
                        if i < 4:
                            pe.wait_ge(tok_sq, 8)
                            pe.wait_ge(tok_evac, 9 + i)
                        for t in range(TT):
                            src = (O, KN)[c][:, t, h, :]
                            last = nc.tensor.transpose(ps[:, i, t * P:(t + 1) * P], src, ident[:, :])
                        last.then_inc(back_T, 1)
                    pe.wait_ge(back_evac, 8)

                    def row_sums(t, d):
                        i = 2 * t + d
                        pe.wait_ge(gu_ready, i + 1)
                        if t > 0:
                            pe.wait_ge(nt_done, i - 1)
                        if t > 1:
                            pe.wait_ge(s_new, i - 3)
                        mm(ps[:, 4 * d + 3, :], ones[:, :], spare[d]["GU"][:, :, :].rearrange("p a b -> p (a b)"), start=True, stop=True).then_inc(row_done, 1)

                    def gram(t, d, rows_, read, done):
                        i = 2 * t + d
                        tok = slice(tile_of(d, t) * P, (tile_of(d, t) + 1) * P)
                        pe.wait_ge(read, i + 1)
                        for h in range(HA):
                            last = mm(ps[:, 4 * d + 3, h * P:(h + 1) * P], KT[:, h, tok], rows_[:, h, tok], start=True, stop=True)
                        last.then_inc(done, 1)

                    def transposed_start(t, d):
                        i = 2 * t + d
                        pe.wait_ge(t0_done, i + 1)
                        if t > 0:
                            pe.wait_ge(w_evac, i - 1)
                        for h in range(HA):
                            last = nc.tensor.transpose(ps[:, 4 * d, h * P:(h + 1) * P], delta[d]["TTr"][:, h, :], ident[:, :])
                        last.then_inc(t0_T, 1)
                    for d in range(2):
                        row_sums(0, d)
                    for d in range(2):
                        gram(0, d, QT, diff_done, qk_done)
                    for d in range(2):
                        gram(0, d, KT, at_done, kk_done)
                    for d in range(2):
                        transposed_start(0, d)
                    for t in range(TT):
                        for l in range(1, 7):
                            for d in range(2):
                                i = 2 * t + d
                                c = (6 * t + l - 1) * 2 + d
                                B, b0 = delta[d], 4 * d
                                pe.wait_ge(nm_done, (7 * t + l) * 2 + d + 1)
                                if l == 1:
                                    pe.wait_ge(t0_evac, i + 1)
                                else:
                                    pe.wait_ge(t_new, 2 * (c - 1) - 1)
                                for h in range(HA):
                                    last = mm(ps[:, b0, h * P:(h + 1) * P], B["NM"][:, h, :], B["T"][:, h, :], start=True, stop=True)
                                last.then_inc(x_done, 1)
                            if t < TT - 1:
                                for d in range(2):
                                    if l == 2:
                                        row_sums(t + 1, d)
                                    elif l == 3:
                                        gram(t + 1, d, QT, diff_done, qk_done)
                                    elif l == 5 + d:
                                        gram(t + 1, d, KT, at_done, kk_done)
                            for d in range(2):
                                i = 2 * t + d
                                c = (6 * t + l - 1) * 2 + d
                                B, b0 = delta[d], 4 * d
                                pe.wait_ge(x_evac, c + 1)
                                if l > 1:
                                    pe.wait_ge(t_new, 2 * (c - 1))
                                if l == 1 and t > 0:
                                    pe.wait_ge(vn_done, i - 1)
                                    pe.wait_ge(o_evac, i - 1)
                                if l < 6:
                                    for h in range(HA):
                                        last = mm(ps[:, b0 + 1, h * P:(h + 1) * P], B["TTr"][:, h, :], B["XS"][:, h, :], start=True, stop=True)
                                    last.then_inc(yt_sum, 1)
                                for h in range(HA):
                                    last = mm(ps[:, b0 + 2, h * P:(h + 1) * P], B["XS"][:, h, :], B["TTr"][:, h, :], start=True, stop=True)
                                last.then_inc(y_done, 1)
                        for d in range(2):
                            i = 2 * t + d
                            B, b0 = delta[d], 4 * d
                            tl = tile_of(d, t)
                            pe.wait_ge(t_new, 2 * ((6 * t + 5) * 2 + d + 1))
                            pe.wait_ge(kgd_done, 2 * (i + 1))
                            for h in range(HA):
                                last = mm(ps[:, b0, h * P:(h + 1) * P], B["KG"][:, h, :], B["TTr"][:, h, :], start=True, stop=True)
                            last.then_inc(w_done, 1)
                        for d in range(2):
                            i = 2 * t + d
                            B, b0 = delta[d], 4 * d
                            tl = tile_of(d, t)
                            pe.wait_ge(w_evac, i + 1)
                            if t == 0:
                                pe.wait_ge(s_zero, 1)
                            else:
                                pe.wait_ge(s_new, i - 1)
                            pe.wait_ge(t0_evac, i + 1)
                            for h in range(HA):
                                mm(ps[:, b0 + 1, h * P:(h + 1) * P], B["TTr"][:, h, :], VN_[:, tl, h, :], start=True, stop=False)
                                last = mm(ps[:, b0 + 1, h * P:(h + 1) * P], B["WT"][:, h, :], S[:, d, h, :], start=False, stop=True)
                            last.then_inc(v_done, 1)
                        for d in range(2):
                            i = 2 * t + d
                            B, b0 = delta[d], 4 * d
                            pe.wait_ge(vn_done, i + 1)
                            pe.wait_ge(qg_done, i + 1)
                            for h in range(HA):
                                mm(ps[:, b0 + 2, h * P:(h + 1) * P], buf("QG", d, t)[:, h, :], S[:, d, h, :], start=True, stop=False)
                                last = mm(ps[:, b0 + 2, h * P:(h + 1) * P], buf("AT", d, t)[:, h, :], B["VN"][:, h, :], start=False, stop=True)
                            last.then_inc(o_done, 1)
                            if t < TT - 1:
                                pe.wait_ge(nt_done, i + 3)
                                for h in range(HA):
                                    last = mm(ps[:, b0 + 3, h * P:(h + 1) * P], B["KD"][:, h, :], B["VN"][:, h, :], start=True, stop=True)
                                last.then_inc(s_done, 1)
                        if t < TT - 1:
                            for d in range(2):
                                transposed_start(t + 1, d)
                    for t in range(TT):
                        if t == 0:
                            pe.wait_ge(rope_done, TT)
                            pe.wait_ge(o_evac, 8)
                            pe.wait_ge(t0_evac, 8)
                        if t >= 2:
                            pe.wait_ge(aq_lo, 2 * (t - 1))
                        for half in range(2):
                            for j in range(3):
                                c = AT0 + half * 512 + j * P
                                last = nc.tensor.transpose(ps[:, 4 + 2 * (t % 2) + half, j * P:(j + 1) * P], PR[:, t, c:c + P], ident[:, :])
                            last.then_inc(aq_T, 1)

                    def scores(u):
                        s, qt, h = UNITS[u]
                        kts = key_tiles(s, qt)
                        if u >= 3:
                            if UNITS[u - 3][0] == 0:
                                pe.wait_ge(win_done, u - 2)
                            else:
                                pe.wait_ge(prob_done, u - 2)
                        base = HD * (h // 2)
                        for j, (a, b) in enumerate(((AQH, AQH), (AQL, AQH), (AQH, AQL))):
                            last = mm(ps[:, u % 3, 0:P * len(kts)], a[base:base + HD, 3 * s + h % 2, qt * P:(qt + 1) * P],
                                      b[base:base + HD, 3 * s + 2, kts[0] * P:(kts[-1] + 1) * P], start=j == 0, stop=j == 2)
                        last.then_inc(score_done, 1)

                    def transposed(u):
                        s, qt, h = UNITS[u]
                        pe.wait_ge(prob_done, u + 1)
                        if u >= 3:
                            pe.wait_ge(pT_evac, u - 2)
                        for j in range(len(key_tiles(s, qt))):
                            last = nc.tensor.transpose(ps[:, 3 + u % 3, j * P:(j + 1) * P], prob(u)[:, j * P:(j + 1) * P], ident[:, :])
                        last.then_inc(pT_done, 1)

                    def weighted(u):
                        s, qt, h = UNITS[u]
                        kts = key_tiles(s, qt)
                        pe.wait_ge(pT_evac, u + 1)
                        if u >= 8 and h == 0:
                            pe.wait_ge(ob_evac, u // 4 - 1)
                        for j, kt in enumerate(kts):
                            v = AT0 + s * 512 + VOFF
                            last = mm(ps[:, 6 + (u // 4) % 2, h * P:(h + 1) * P], probT(u)[:, j * P:(j + 1) * P],
                                      PR[:, kt, v:v + P], start=j == 0, stop=j == len(kts) - 1)
                        last.then_inc(pv_done, 1)
                    pe.wait_ge(aq_lo, 2 * TT)
                    scores(0)
                    scores(1)
                    for u in range(len(UNITS)):
                        if u + 2 < len(UNITS):
                            scores(u + 2)
                        transposed(u)
                        if u:
                            weighted(u - 1)
                    weighted(len(UNITS) - 1)
                    for k in range(KD):
                        if k == 0:
                            pe.wait_ge(ob_evac, 2 * TT)
                            pe.wait_ge(oa_done, 1)
                        for t in range(TT):
                            src = O[:, t, k, :] if k < HA else OB[:, t, (k - HA) * P:(k - HA + 1) * P]
                            last = nc.tensor.transpose(ps[:, k, t * P:(t + 1) * P], src, ident[:, :])
                        last.then_inc(mix_T, 1)
                    pe.wait_ge(mix_lo, KD)
                    for m in range(N_OUT):
                        n = N_IN + m
                        pe.wait_ge(lo_done, n + 1)
                        hi, lo = piece_view(whi[n % SPLIT], n), piece_view(wlo[n % SPLIT], n)
                        for b in range(8):
                            t, half = divmod(b, 2)
                            for kk in range(2):
                                for j, (w, h) in enumerate(((hi, MH), (lo, MH), (hi, ML))):
                                    last = mm(ps[:, b, :], h[:, 2 * m + kk, t * P:(t + 1) * P], w[:, kk, half * 512:(half + 1) * 512],
                                              start=m == 0 and kk == 0 and j == 0, stop=m == N_OUT - 1 and kk == 1 and j == 2)
                            last.then_inc(passes, 1)

                    def logits(t):
                        pe.wait_ge(hT2_evac, 2 * (t + 1))
                        for k in range(KD):
                            last = mm(ps[0:NE, 4, t * P:(t + 1) * P], router[:, k, :], HT[:, k, t * P:(t + 1) * P], start=k == 0, stop=k == KD - 1)
                        return last
                    pe.wait_ge(x_added, 8)
                    pe.sem_inc(m_pass, SPLIT_M)
                    pe.wait_ge(e_in, 64)
                    for t in range(TT):
                        pe.wait_ge(h_done, t + 1)
                        if t >= 2:
                            pe.wait_ge(hT2_evac, 2 * (t - 1))
                        for half in range(2):
                            for j in range(4):
                                k = 4 * half + j
                                last = nc.tensor.transpose(ps[:, 2 * (t % 2) + half, j * P:(j + 1) * P], hw[:, t % 2, k * P:(k + 1) * P], ident[:, :])
                            last.then_inc(hT2_done, 1)
                        if t:
                            logits(t - 1)
                    logits(TT - 1).then_inc(logit_done, 1)
                    pe.wait_ge(logit_rows, 1)
                    for t in range(TT):
                        last = nc.tensor.transpose(ps[:, 7, t * NE:(t + 1) * NE], work[:, t * P:(t + 1) * P], ident[0:NE, 0:NE])
                    last.then_inc(logit_T, 1)
                    pe.wait_ge(aff_done, 1)
                    for t in range(TT):
                        last = nc.tensor.transpose(ps[0:NE, 5, t * P:(t + 1) * P], aff[:, t, :], ident[:, :])
                    last.then_inc(affT_done, 1)
                    pe.wait_ge(chosen, 1)
                    for j in range(2):
                        last = nc.tensor.transpose(ps[:, 6, j * NE:(j + 1) * NE], twice[:, j, :, :].rearrange("p a b -> p (a b)"), ident[0:NE, 0:NE])
                    last.then_inc(chosen_T, 1)
                    pe.wait_ge(spread_done, 1)
                    for j in range(2):
                        mm(ps[:, 4 + j, :], ones[0:NE, :], spread[:, 8 * j:8 * j + 8, :].rearrange("p a b -> p (a b)"), start=True, stop=True).then_inc(rows_done, 1)
                    pe.wait_ge(fold_set, 1)

                    def gather(part):
                        for k in range(4 * part, 4 * part + 4):
                            for z, h in enumerate((EH, EL)):
                                at = 128 * (2 * (k % 2) + z)
                                copies = 2 if at < 384 else 1
                                o = ps[:, k // 2, at:at + copies * P].rearrange("p (c s) -> p c s", c=copies)
                                for t in range(TT):
                                    last = mm(o, h[:, t, k * P:(k + 1) * P], bc(sel[:, t, :], 1, [P, copies, P]), start=t == 0, stop=t == TT - 1)
                        last.then_inc(gathered, 1)
                    def scatter(ns):
                        for n in ns:
                            t, half = divmod(n, 2)
                            mm(ps[:, 4 + n % 4, :], selT[:, t * P:(t + 1) * P], YE[:, half * 512:(half + 1) * 512], start=True, stop=True).then_inc(scattered, 1)
                    pe.wait_ge(sel_done, 1)
                    gather(0)
                    gather(1)
                    pe.wait_ge(selT_done, 1)
                    pe.wait_ge(ye_done, 1)
                    pe.wait_ge(top_ready, 2)
                    for half in range(2):
                        mm(ps[:, 6 + half, :], selT[:, 0:P], YE[:, 0:512], start=True, stop=True).then_inc(zeroed, 1)
                    with pe.Fori(0, PAIRS) as g:
                        def times(block, js, bank, lhs):
                            for j in js:
                                q = 4 * block + j
                                wait_split(pe, g, q)
                                for kk in range(2):
                                    k = 2 * j + kk
                                    for half in range(2):
                                        for z, w in enumerate((whi, wlo)):
                                            last = mm(ps[:, bank + half, :], lhs(k), two(w[q % SPLIT_M])[:, kk, half * 512:(half + 1) * 512],
                                                      start=k == 0 and z == 0, stop=k == KD - 1 and z == 1)
                                last.then_inc(m_pass, 1)

                        def folds(j):
                            for f in range(DE // P):
                                last = mm(ps[:, 4 + j, f * CAP:(f + 1) * CAP], GU[:, j, f * P:(f + 1) * P], fold[:, :], start=True, stop=True)
                            last.then_inc(folded, 1)

                        def a(k):
                            return XE[:, k, 0, :]

                        def b(k):
                            return XE[:, k, 1, :]

                        def hidden(k):
                            return HP[:, k, :]
                        pe.wait_ge(xe_evac, g * 2 + 1)
                        times(0, range(2), 0, a)
                        pe.wait_ge(xe_evac, g * 2 + 2)
                        times(0, range(2, 3), 0, a)
                        pe.wait_ge(ye_done, g * 2 + 2)
                        pe.wait_ge(selT_done, g + 1)
                        scatter(range(4))
                        times(0, range(3, 4), 0, a)
                        times(1, range(3), 2, a)
                        pe.wait_ge(x_added, g * 8 + 12)
                        scatter(range(4, 8))
                        times(1, range(3, 4), 2, a)
                        pe.wait_ge(gu_evac, g * 4 + 1)
                        times(2, range(2), 0, b)
                        pe.wait_ge(gu_evac, g * 4 + 2)
                        pe.wait_ge(x_added, g * 8 + 16)
                        folds(0)
                        folds(1)
                        times(2, range(2, 4), 0, b)
                        pe.wait_ge(hp_lo, g * 2 + 1)
                        times(3, range(4), 6, hidden)
                        pe.wait_ge(gu_evac, g * 4 + 3)
                        folds(0)
                        pe.wait_ge(sel_done, g + 2)
                        gather(0)
                        times(4, range(4), 2, b)
                        pe.wait_ge(gu_evac, g * 4 + 4)
                        folds(1)
                        gather(1)
                        pe.wait_ge(hp_lo, g * 2 + 2)
                        pe.wait_ge(ye_done, g * 2 + 3)
                        times(5, range(4), 6, hidden)
                    pe.wait_ge(ye_done, PAIRS * 2 + 2)
                    pe.wait_ge(selT_done, PAIRS + 1)
                    scatter(range(4))
                    pe.wait_ge(x_added, PAIRS * 8 + 12)
                    scatter(range(4, 8))

                @block.scalar
                def _(act):
                    A = nc.scalar.activation

                    for t in range(TT):
                        A(XN[:, t, :], X[:, t, :], ACT.Square, accum_out=ss1[:, t:t + 1]).then_inc(x_sq, 1)
                    act.wait_ge(x_var, 1)
                    A(rs1[:, :], ss1[:, :], ACT.Sqrt).then_inc(x_std, 1)
                    rounds(act, 0)
                    rounds(act, 1)
                    act.wait_ge(par_in, 32)
                    for k in range(KD):
                        act.wait_ge(xT_done, k + 1)
                        A(HH[:, k, :], ps[:, k, :], ACT.Copy, scale=g1[:, k:k + 1]).then_inc(hT_hi, 1)

                    def silu(ct):
                        dst = (QT, KT, VD)[ct // 4][:, ct % 4, :]
                        act.wait_ge(conv_done, ct + 1)
                        A(dst, dst, ACT.Silu).then_inc(silu_done, 1)

                    def rows_in(i):
                        c, t = TOK[i]
                        act.wait_ge(tok_T, i + 1)
                        A((O, KN, VN_)[c][:, t, :, :], ps[:, tok_bank(i), :].rearrange("p (a b) -> p a b", b=P), ACT.Copy).then_inc(tok_evac, 1)
                        if i < 8:
                            if i >= 2:
                                act.wait_ge(tok_ss, i - 1)
                            A(sq_rows(i), ps[:, tok_bank(i), :].rearrange("p (a b) -> p a b", b=P), ACT.Square).then_inc(tok_sq, 1)
                    act.wait_ge(pad_set, 1)
                    for g in range(GROUPS):
                        for n in (2 * g + 2, 2 * g + 3):
                            if n < N_IN:
                                rounds(act, n)
                        if g == 1:
                            act.wait_ge(gate_z, 1)
                            A(eb[:, :, :], tb[:, :, :], ACT.Exp, scale=-1.0).then_inc(gate_e, 1)
                            A(beta[:, :, :], PR[:, :, BA0:BA0 + 8], ACT.Exp, scale=-1.0).then_inc(gate_e, 1)
                            A(ea[:, :], a_log, ACT.Exp).then_inc(gate_e, 1)
                            act.wait_ge(gate_w, 1)
                            A(lb[:, :, :], tb[:, :, :], ACT.Ln).then_inc(gate_ln, 1)
                        if g == FIRST_QKV:
                            act.wait_ge(r_var, 1)
                            A(rsR[:, :, :], ssR[:, :, :], ACT.Sqrt).then_inc(r_std, 1)
                        if g == GROUPS - 1:
                            silu(NQKV - 1)
                            act.wait_ge(rope_done, TT)
                            for i in range(4):
                                rows_in(i)
                        for t in range(4):
                            act.wait_ge(passes, 8 * g + 4 + t + 1)
                            b = 4 * (g % 2) + t
                            if g in REST_OF:
                                A(PR[:, t, REST_OF[g] * RW:(REST_OF[g] + 1) * RW], ps[:, b, 0:RW], ACT.Copy).then_inc(proj_evac, 1)
                                continue
                            c = g - FIRST_QKV
                            ct = 4 * c + t
                            if ct >= 2:
                                act.wait_ge(conv_done, ct - 1)
                            A(XP[:, ct % 2, 2:SEQ + 2], ps[:, b, :], ACT.Copy).then_inc(proj_evac, 1)
                            act.wait_ge(proj_evac, 4 * g + t + 1)
                            A((QT, KT, VD)[c][:, t, :], XP[:, ct % 2, 0:SEQ], ACT.Copy, scale=cw[:, ct, 0:1]).then_inc(tap0, 1)
                            if ct >= 1:
                                silu(ct - 1)
                    act.wait_ge(proj_evac, 4 * GROUPS)
                    A(PR[:, :, Z0:Z0 + 512], PR[:, :, Z0:Z0 + 512], ACT.Silu).then_inc(z_silu, 1)
                    for i in range(4, 8):
                        rows_in(i)
                    act.wait_ge(qk_var, 1)
                    A(rsA[:, :, :, :], ssA[:, :, :, :], ACT.Sqrt).then_inc(qk_std, 1)
                    act.wait_ge(tok_ss, 8)
                    for i in range(8, 12):
                        rows_in(i)
                    for i in range(8):
                        c, h = 1 - i // HA, i % HA
                        act.wait_ge(back_T, i + 1)
                        A((QT, KT)[c][:, h, :], ps[:, i, :], ACT.Copy).then_inc(back_evac, 1)
                    act.wait_ge(cum_diff, 1)
                    A(egc[:, :, :, :], gcc[:, :, :, :], ACT.Exp)
                    A(egl[:, :, :, :], gll[:, :, :, :], ACT.Exp)
                    A(kdc[:, :, :, :], kdc[:, :, :, :], ACT.Exp).then_inc(cum_exp, 1)

                    def exp_rows(t, d):
                        i = 2 * t + d
                        act.wait_ge(row_done, i + 1)
                        if t > 1:
                            act.wait_ge(o_done, i - 3)
                        A(buf("QG", d, t), bank_heads(4 * d + 3), ACT.Exp).then_inc(eg_exp, 1)

                    def exp_diff(t, d):
                        act.wait_ge(diff_done, 2 * t + d + 1)
                        A(delta[d]["DM"][:, :, :], delta[d]["DM"][:, :, :], ACT.Exp).then_inc(dm_exp, 1)

                    def start_out(t, d):
                        act.wait_ge(t0_T, 2 * t + d + 1)
                        A(delta[d]["T"][:, :, :], bank_heads(4 * d), ACT.Copy).then_inc(t0_evac, 1)
                    for d in range(2):
                        exp_rows(0, d)
                    for d in range(2):
                        exp_diff(0, d)
                    for d in range(2):
                        start_out(0, d)
                    for t in range(TT):
                        for l in range(1, 7):
                            if t < TT - 1 and l == 3:
                                for d in range(2):
                                    exp_diff(t + 1, d)
                            for d in range(2):
                                c = (6 * t + l - 1) * 2 + d
                                B, b0 = delta[d], 4 * d
                                act.wait_ge(x_done, c + 1)
                                if c >= 2:
                                    act.wait_ge(y_done, c - 1)
                                A(B["XS"][:, :, :], ps[:, b0, :].rearrange("p (a b) -> p a b", b=P), ACT.Copy).then_inc(x_evac, 1)
                            if t < TT - 1 and l == 2:
                                for d in range(2):
                                    exp_rows(t + 1, d)
                        for d in range(2):
                            i = 2 * t + d
                            B, b0 = delta[d], 4 * d
                            act.wait_ge(w_done, i + 1)
                            if t > 0:
                                act.wait_ge(v_done, i - 1)
                            A(B["WT"][:, :, :], ps[:, b0, :].rearrange("p (a b) -> p a b", b=P), ACT.Copy, scale=-1.0).then_inc(w_evac, 1)
                        if t < TT - 1:
                            for d in range(2):
                                start_out(t + 1, d)
                    for i in range(2 * TT):
                        t, half = divmod(i, 2)
                        act.wait_ge(aq_T, i + 1)
                        A(AQH[:, 3 * half:3 * half + 3, t * P:(t + 1) * P],
                          ps[:, 4 + 2 * (t % 2) + half, 0:3 * P].rearrange("p (a b) -> p a b", b=P), ACT.Copy).then_inc(aq_evac, 1)
                    act.wait_ge(oa_var, 1)
                    A(rsO[:, :, :], ssO[:, :, :], ACT.Sqrt).then_inc(oa_std, 1)

                    def weights(u):
                        s, qt, h = UNITS[u]
                        n = P * len(key_tiles(s, qt))
                        act.wait_ge(max_done, u + 1)
                        if u >= 3:
                            act.wait_ge(pT_done, u - 2)
                        if u >= 8 and h == 0:
                            act.wait_ge(ob_evac, u // 4 - 1)
                        src = win(u)[:, 0:n] if s == 0 else ps[:, u % 3, 0:n]
                        A(prob(u)[:, 0:n], src, ACT.Exp, scale=SCALE, bias=nmx[:, (u // 4) % 2, h:h + 1],
                          accum_out=psumS[:, (u // 4) % 2, h:h + 1]).then_inc(prob_done, 1)
                        if s == 0 and h == HB - 1:
                            act.wait_ge(sink_in, qt + 1)
                            A(esk[:, (u // 4) % 2, :], esk[:, (u // 4) % 2, :], ACT.Exp).then_inc(sink_exp, 1)
                    weights(0)
                    for u, (s, qt, h) in enumerate(UNITS):
                        n = P * len(key_tiles(s, qt))
                        if u + 1 < len(UNITS):
                            weights(u + 1)
                        act.wait_ge(pT_done, u + 1)
                        if u >= 3:
                            act.wait_ge(pv_done, u - 2)
                        A(probT(u)[:, 0:n], ps[:, 3 + u % 3, 0:n], ACT.Copy).then_inc(pT_evac, 1)
                        if u in ROUND_AT:
                            m, half = divmod(ROUND_AT.index(u), 2)
                            act.wait_ge(raw_full[(N_IN + m) % RAW_A], 16 * ((N_IN + m) // RAW_A + 1))
                            last = A(out_half(whi, m, half), out_half(raw, m, half), ACT.Copy)
                            if half:
                                last.then_inc(hi_done, 1)
                    act.wait_ge(pv_done, len(UNITS))
                    for k in range(KD):
                        act.wait_ge(mix_T, k + 1)
                        A(MH[:, k, :], ps[:, k, :], ACT.Copy).then_inc(mix_hi, 1)
                    rounds(act, N_IN + 3)

                    for t in range(TT):
                        act.wait_ge(x_added, 2 * t + 2)
                        A(ps[:, 2 * t:2 * t + 2, :].rearrange("p a b -> p (a b)"), X[:, t, :], ACT.Square, accum_out=ssX[:, t:t + 1]).then_inc(e_sq, 1)
                    act.wait_ge(e_var, 1)
                    A(st2[:, 4:8], st2[:, 0:4], ACT.Sqrt).then_inc(e_std, 1)
                    for t in range(TT):
                        act.wait_ge(h_done, t + 1)
                        A(EH[:, t, :], hw[:, t % 2, :], ACT.Copy).then_inc(e_hi, 1)
                        for half in range(2):
                            act.wait_ge(hT2_done, 2 * t + half + 1)
                            A(HT[:, 4 * half:4 * half + 4, t * P:(t + 1) * P],
                              ps[:, 2 * (t % 2) + half, :].rearrange("p (a b) -> p a b", b=P), ACT.Copy).then_inc(hT2_evac, 1)
                    act.wait_ge(logit_max, 1)
                    A(aff[:, :, :], aff[:, :, :], ACT.Exp).then_inc(logit_exp, 1)

                    def tokens_in(i, part):
                        act.wait_ge(gathered, i * 2 + (part + 1))
                        for e in range(2):
                            last = A(XE[:, 4 * part:4 * part + 4, e, :].rearrange("p k (z c) -> p k z c", z=2),
                                     ps[:, 2 * part:2 * part + 2, :].rearrange("p b (k z e c) -> p (b k) z e c", k=2, z=2, e=2)[:, :, :, e, :], ACT.Copy)
                        last.then_inc(xe_evac, 1)
                    with act.Fori(0, PAIRS) as g:
                        def rows_out(j, block):
                            act.wait_ge(m_pass, g * TURN + (SPLIT_M + 4 * block + 4))
                            A(GU[:, j, :], ps[:, 2 * j:2 * j + 2, :].rearrange("p a b -> p (a b)"), ACT.Copy).then_inc(gu_evac, 1)

                        def gate(n):
                            act.wait_ge(folded, g * 4 + (2 * n + 1))
                            A(SG[:, :, :], ps[:, 4, :].rearrange("p (a b) -> p a b", b=CAP), ACT.Silu).then_inc(sg_done, 1)

                        def hidden_hi(n):
                            act.wait_ge(hm_done, g * 2 + (n + 1))
                            A(HP[:, :, 0:CAP], HM[:, :, :], ACT.Copy).then_inc(hp_hi, 1)

                        def low_share(n, passed):
                            act.wait_ge(m_pass, g * TURN + (SPLIT_M + passed))
                            A(YT[:, :], ps[CAP:P, 6:8, :].rearrange("p a b -> p (a b)"), ACT.Copy, scale=gate_now[CAP:P, n:n + 1]).then_inc(yt_done, 1)
                        for q in range(TURN):
                            expert_rounds(act, g, q)
                            if q == 1:
                                tokens_in(g, 0)
                                tokens_in(g, 1)
                                act.wait_ge(zeroed, 2)
                                low_share(1, 0)
                            elif q == 6:
                                rows_out(0, 0)
                            elif q == 10:
                                rows_out(1, 1)
                            elif q == 13:
                                gate(0)
                                hidden_hi(0)
                            elif q == 14:
                                rows_out(0, 2)
                            elif q == 18:
                                low_share(0, 16)
                            elif q == 22:
                                rows_out(1, 4)
                            elif q == 23:
                                gate(1)
                                hidden_hi(1)
                    act.wait_ge(m_pass, PAIRS * TURN + SPLIT_M)
                    A(YT[:, :], ps[CAP:P, 6:8, :].rearrange("p a b -> p (a b)"), ACT.Copy, scale=gate_now[CAP:P, 1:2]).then_inc(yt_done, 1)

                @block.vector
                def _(dve):
                    V = nc.vector
                    chained = [0]

                    def step(ins):
                        chained[0] += 1
                        ins.then_inc(v_chain, 1)
                        dve.wait_ge(v_chain, chained[0])
                    dve.wait_ge(x_sq, TT)
                    V.tensor_scalar(ss1[:, :], ss1[:, :], 1.0 / D, EPS, ALU.mult, ALU.add).then_inc(x_var, 1)
                    dve.wait_ge(x_std, 1)
                    step(V.reciprocal(rs1[:, :], rs1[:, :]))
                    for t in range(TT):
                        V.tensor_scalar(XN[:, t, :], X[:, t, :], rs1[:, t:t + 1], None, ALU.mult).then_inc(x_normed, 1)
                    rests(dve, 0)
                    rests(dve, 1)
                    for k in range(KD):
                        dve.wait_ge(hT_hi, k + 1)
                        V.scalar_tensor_tensor(HL[:, k, :], ps[:, k, :], g1[:, k:k + 1], HH[:, k, :],
                                               ALU.mult, ALU.subtract).then_inc(hT_lo, 1)

                    def head_sums(i):
                        c, t = TOK[i]
                        dve.wait_ge(tok_sq, i + 1)
                        V.reduce_sum(ssA[:, c, t, :], sq_rows(i), axis=AX).then_inc(tok_ss, 1)
                    steps = 0
                    for g in range(GROUPS):
                        for n in (2 * g + 2, 2 * g + 3):
                            if n < N_IN:
                                rests(dve, n)
                        if g == GROUPS - 1:
                            for i in range(4):
                                head_sums(i)
                        if g == 1:
                            dve.wait_ge(proj_evac, 4)
                            dve.wait_ge(par_in, 32)
                            step(V.tensor_tensor(zb[:, :, :], PR[:, :, BA0 + 8:BA0 + 16], bc(dt_b, 1, [P, TT, 8]), ALU.add))
                            V.scalar_tensor_tensor(tb[:, :, :], zb[:, :, :], -1.0, zb[:, :, :], ALU.mult, ALU.max).then_inc(gate_z, 1)
                            dve.wait_ge(gate_e, 3)
                            step(V.tensor_scalar(beta[:, :, :], beta[:, :, :], 1.0, None, ALU.add))
                            V.reciprocal(beta[:, :, :], beta[:, :, :])
                            V.tensor_scalar(tb[:, :, :], eb[:, :, :], 1.0, None, ALU.add).then_inc(gate_w, 1)
                            dve.wait_ge(gate_w, 1)
                            step(V.scalar_tensor_tensor(eb[:, :, :], tb[:, :, :], -1.0, eb[:, :, :], ALU.add, ALU.subtract))
                            dve.wait_ge(gate_ln, 1)
                            step(V.reciprocal(tb[:, :, :], tb[:, :, :]))
                            step(V.tensor_tensor(eb[:, :, :], eb[:, :, :], tb[:, :, :], ALU.mult))
                            step(V.tensor_tensor(lb[:, :, :], lb[:, :, :], eb[:, :, :], ALU.subtract))
                            step(V.scalar_tensor_tensor(zb[:, :, :], zb[:, :, :], 0.0, lb[:, :, :], ALU.max, ALU.add))
                            V.scalar_tensor_tensor(gdec[:, :, :], zb[:, :, :], -1.0, bc(ea[:, :], 1, [P, TT, 8]), ALU.mult, ALU.mult).then_inc(g_ready, 1)
                        if g == FIRST_QKV:
                            for t in range(TT):
                                dve.wait_ge(r_sq, t + 1)
                                V.reduce_sum(ssR[:, t, :], squares(t).rearrange("p (a b) -> p a b", b=HD), axis=AX).then_inc(r_ss, 1)
                            dve.wait_ge(r_ss, TT)
                            V.tensor_scalar(ssR[:, :, :], ssR[:, :, :], 1.0 / HD, EPS, ALU.mult, ALU.add).then_inc(r_var, 1)
                            dve.wait_ge(r_std, 1)
                            V.reciprocal(rsR[:, :, :], rsR[:, :, :]).then_inc(r_scale, 1)
                        if g not in REST_OF:
                            for t in range(4):
                                ct = 4 * (g - FIRST_QKV) + t
                                y = (QT, KT, VD)[g - FIRST_QKV][:, t, :]
                                dve.wait_ge(tap0, ct + 1)
                                for j in range(1, 5):
                                    ins = V.scalar_tensor_tensor(y, XP[:, ct % 2, j:j + SEQ], cw[:, ct, j:j + 1], y, ALU.mult, ALU.add)
                                    if j < 4:
                                        steps += 1
                                        ins.then_inc(conv_step, 1)
                                        dve.wait_ge(conv_step, steps)
                                    else:
                                        ins.then_inc(conv_done, 1)
                    head_sums(4)
                    dve.wait_ge(cum_done, 1)
                    four = dict(b=TT, c=HA)
                    V.tensor_copy(gcc[:, :, :, :], ps[:, 3, 0:32].rearrange("p (a b c) -> p a b c", **four))
                    V.tensor_copy(gll[:, :, :, :], ps[:, 3, 32:64].rearrange("p (a b c) -> p a b c", **four)).then_inc(cum_evac, 1)
                    dve.wait_ge(cum_evac, 1)
                    V.tensor_tensor(kdc[:, :, :, :], gll[:, :, :, :], gcc[:, :, :, :], ALU.subtract).then_inc(cum_diff, 1)
                    for i in range(5, 8):
                        head_sums(i)
                    dve.wait_ge(tok_ss, 8)
                    V.tensor_scalar(ssA[:, :, :, :], ssA[:, :, :, :], EPS, None, ALU.add).then_inc(qk_var, 1)
                    dve.wait_ge(qk_std, 1)
                    step(V.reciprocal(rsA[:, :, :, :], rsA[:, :, :, :]))
                    step(V.tensor_scalar(rsA[:, 0, :, :], rsA[:, 0, :, :], float(P) ** -0.5, None, ALU.mult))
                    dve.wait_ge(tok_evac, 8)
                    for c, t in TOK[0:8]:
                        dst = (O, KN)[c][:, t, :, :]
                        V.tensor_tensor(dst, dst, bc(rsA[:, c, t, :], 2, [P, HA, P]), ALU.mult).then_inc(qk_normed, 1)

                    def differences(t, d):
                        i = 2 * t + d
                        dve.wait_ge(eg_exp, i + 1)
                        if t > 0:
                            dve.wait_ge(nt_base, i - 1)
                        for h in range(HA):
                            last = V.tensor_scalar(delta[d]["DM"][:, h, :], ps[:, 4 * d + 3, h * P:(h + 1) * P],
                                                   gcc[:, d, tile_of(d, t), h:h + 1], 0.0, ALU.subtract, ALU.min)
                        last.then_inc(diff_done, 1)

                    def inner(t, d):
                        i = 2 * t + d
                        dve.wait_ge(qk_done, i + 1)
                        dve.wait_ge(masked, i + 1)
                        if t > 1:
                            dve.wait_ge(o_done, i - 3)
                        V.tensor_tensor(buf("AT", d, t), bank_heads(4 * d + 3), delta[d]["DM"][:, :, :], ALU.mult).then_inc(at_done, 1)

                    def strict(t, d):
                        i = 2 * t + d
                        dve.wait_ge(kk_done, i + 1)
                        dve.wait_ge(nt_base, i + 1)
                        V.tensor_tensor(buf("NT", d, t), bank_heads(4 * d + 3), buf("NT", d, t), ALU.mult).then_inc(nt_done, 1)

                    def q_decayed(t, d):
                        tok = slice(tile_of(d, t) * P, (tile_of(d, t) + 1) * P)
                        dve.wait_ge(eg_exp, 2 * t + d + 1)
                        dve.wait_ge(back_evac, 8)
                        V.tensor_tensor(buf("QG", d, t), buf("QG", d, t), QT[:, :, tok], ALU.mult).then_inc(qg_done, 1)

                    def start(t, d):
                        i = 2 * t + d
                        dve.wait_ge(nm_done, 14 * t + d + 1)
                        if t > 0:
                            dve.wait_ge(v_done, i - 1)
                        V.tensor_tensor(delta[d]["TTr"][:, :, :], bc(ident[:, :], 1, [P, HA, P]), delta[d]["NM"][:, :, :], ALU.subtract).then_inc(t0_done, 1)

                    def state(t, d):
                        i = 2 * t + d
                        dve.wait_ge(s_done, i + 1)
                        dve.wait_ge(s_dec, i + 1)
                        V.tensor_tensor(S[:, d, :, :], S[:, d, :, :], bank_heads(4 * d + 3), ALU.add).then_inc(s_new, 1)

                    def out_squares(tiles):
                        dve.wait_ge(o_evac, 8 if 0 in tiles else 6)
                        for tl in tiles:
                            last = V.tensor_tensor(QT[:, tl, :].rearrange("p (a b) -> p a b", b=P), O[:, tl, :, :], O[:, tl, :, :], ALU.mult)
                        step(last)
                        for tl in tiles:
                            last = V.reduce_sum(ssO[:, tl, :], QT[:, tl, :].rearrange("p (a b) -> p a b", b=P), axis=AX)
                        last.then_inc(o_sums, 1)
                    for stage in (differences, inner, strict, start, q_decayed):
                        for d in range(2):
                            stage(0, d)
                    for t in range(TT):
                        for l in range(1, 7):
                            if l == 1 and t > 0:
                                for d in range(2):
                                    state(t - 1, d)
                            if t == TT - 1 and l == 3:
                                out_squares((1, 2))
                            if t < TT - 1:
                                if l == 2:
                                    differences(t + 1, 0)
                                    differences(t + 1, 1)
                                elif l == 3:
                                    q_decayed(t + 1, 0)
                                    q_decayed(t + 1, 1)
                                elif l == 4:
                                    inner(t + 1, 0)
                                elif l == 5:
                                    inner(t + 1, 1)
                                    strict(t + 1, 0)
                                elif l == 6:
                                    strict(t + 1, 1)
                            for d in range(2):
                                i = 2 * t + d
                                c = (6 * t + l - 1) * 2 + d
                                B, b0 = delta[d], 4 * d
                                if l == 1:
                                    dve.wait_ge(t0_evac, i + 1)
                                if l < 6:
                                    dve.wait_ge(yt_sum, (5 * t + l - 1) * 2 + d + 1)
                                    V.tensor_tensor(B["T"][:, :, :], B["T"][:, :, :], ps[:, b0 + 1, :].rearrange("p (a b) -> p a b", b=P), ALU.subtract).then_inc(t_new, 1)
                                dve.wait_ge(y_done, c + 1)
                                V.tensor_tensor(B["TTr"][:, :, :], B["TTr"][:, :, :], ps[:, b0 + 2, :].rearrange("p (a b) -> p a b", b=P), ALU.subtract).then_inc(t_new, 1 if l < 6 else 2)
                        for d in range(2):
                            i = 2 * t + d
                            B, b0 = delta[d], 4 * d
                            tl = tile_of(d, t)
                            dve.wait_ge(v_done, i + 1)
                            if t > 0:
                                dve.wait_ge(s_done, i - 1)
                            V.tensor_tensor(B["VN"][:, :, :], ps[:, b0 + 1, :].rearrange("p (a b) -> p a b", b=P),
                                            bc(beta[:, tl, d * HA:(d + 1) * HA], 2, [P, HA, P]), ALU.mult).then_inc(vn_done, 1)
                        if t < TT - 1:
                            start(t + 1, 0)
                            start(t + 1, 1)
                        for d in range(2):
                            i = 2 * t + d
                            B, b0 = delta[d], 4 * d
                            tl = tile_of(d, t)
                            dve.wait_ge(o_done, i + 1)
                            o = ps[:, b0 + 2, :].rearrange("p (a b) -> p a b", b=P)
                            if t < TT // 2:
                                if i == 0:
                                    dve.wait_ge(back_T, 8)
                                V.tensor_copy(O[:, tl, :, :], o).then_inc(o_evac, 1)
                            else:
                                dve.wait_ge(o_evac, 4)
                                V.tensor_tensor(O[:, tl, :, :], O[:, tl, :, :], o, ALU.add).then_inc(o_evac, 1)
                    out_squares((0, 3))
                    dve.wait_ge(o_sums, 2)
                    V.tensor_scalar(ssO[:, :, :], ssO[:, :, :], 1.0 / P, EPS, ALU.mult, ALU.add).then_inc(oa_var, 1)
                    for i in range(2 * TT):
                        t, half = divmod(i, 2)
                        dve.wait_ge(aq_evac, i + 1)
                        c = (slice(None), slice(3 * half, 3 * half + 3), slice(t * P, (t + 1) * P))
                        V.tensor_tensor(AQL[c], ps[:, 4 + 2 * (t % 2) + half, 0:3 * P].rearrange("p (a b) -> p a b", b=P), AQH[c], ALU.subtract).then_inc(aq_lo, 1)
                    O3 = O[:, :, :, :].rearrange("p t h c -> p (t h) c")

                    def delta_norm(stage):
                        if stage == 0:
                            dve.wait_ge(oa_std, 1)
                            step(V.reciprocal(rsO[:, :, :], rsO[:, :, :]))
                            step(V.tensor_tensor(O3, O3, bc(rsO[:, :, :].rearrange("p a b -> p (a b)"), 2, [P, TT * HA, P]), ALU.mult))
                        elif stage == 1:
                            step(V.tensor_tensor(O3, O3, bc(a_norm, 1, [P, TT * HA, P]), ALU.mult))
                        else:
                            dve.wait_ge(z_silu, 1)
                            V.tensor_tensor(O[:, :, :, :].rearrange("p t h c -> p t (h c)"), O[:, :, :, :].rearrange("p t h c -> p t (h c)"),
                                            PR[:, :, Z0:Z0 + 512], ALU.mult).then_inc(oa_done, 1)
                    step(V.tensor_scalar(nsink[:, :], sink, -1.0, None, ALU.mult))

                    def finish(G):
                        s, qt = divmod(G, TT)
                        r = G % 2
                        dve.wait_ge(pv_done, 4 * G + 4)
                        if s == 0:
                            dve.wait_ge(sink_exp, qt + 1)
                            step(V.tensor_tensor(rinv[:, r, :], psumS[:, r, :], esk[:, r, :], ALU.add))
                            step(V.reciprocal(rinv[:, r, :], rinv[:, r, :]))
                        else:
                            step(V.reciprocal(rinv[:, r, :], psumS[:, r, :]))
                        for a in range(2):
                            c = s * 256 + a * P
                            last = V.tensor_tensor(OB[:, qt, c:c + P].rearrange("p (a b) -> p a b", b=HD),
                                                   ps[:, 6 + G % 2, a * 256:(a + 1) * 256].rearrange("p (a b) -> p a b", b=P)[:, :, a * HD:(a + 1) * HD],
                                                   bc(rinv[:, r, 2 * a:2 * a + 2], 2, [P, 2, HD]), ALU.mult)
                        last.then_inc(ob_evac, 1)
                    for u, (s, qt, h) in enumerate(UNITS):
                        kts = key_tiles(s, qt)
                        n = P * len(kts)
                        r = (u // 4) % 2
                        dve.wait_ge(score_done, u + 1)
                        if u >= 3:
                            dve.wait_ge(prob_done, u - 2)
                        src = ps[:, u % 3, 0:n]
                        if s == 0:
                            off = (kts[0] - qt + 1) * P
                            V.tensor_tensor(win(u)[:, 0:n], src, window[:, off:off + n], ALU.add).then_inc(win_done, 1)
                            dve.wait_ge(win_done, u + 1)
                            src = win(u)[:, 0:n]
                        step(V.reduce_max(rmax[:, u % 3:u % 3 + 1], src, axis=AX))
                        V.tensor_scalar(nmx[:, r, h:h + 1], rmax[:, u % 3:u % 3 + 1], -SCALE, nsink[:, h:h + 1] if s == 0 else None,
                                        ALU.mult, *((ALU.min,) if s == 0 else ())).then_inc(max_done, 1)
                        if s == 0 and h == HB - 1:
                            dve.wait_ge(max_done, u + 1)
                            V.tensor_tensor(esk[:, r, :], nmx[:, r, :], sink, ALU.add).then_inc(sink_in, 1)
                        if u % 4 == 2 and u > 4:
                            finish(u // 4 - 1)
                        if u in (8, 16, 24):
                            delta_norm(u // 8 - 1)
                        if u in REST_AT:
                            m, half = divmod(REST_AT.index(u), 2)
                            dve.wait_ge(hi_done, N_IN + m + 1)
                            last = V.tensor_tensor(out_half(wlo, m, half), out_half(raw, m, half), out_half(whi, m, half), ALU.subtract)
                            if half:
                                last.then_inc(lo_done, 1)
                    finish(2 * TT - 1)
                    for k in range(KD):
                        dve.wait_ge(mix_hi, k + 1)
                        V.tensor_tensor(ML[:, k, :], ps[:, k, :], MH[:, k, :], ALU.subtract).then_inc(mix_lo, 1)
                    rests(dve, N_IN + 3)
                    for b in range(8):
                        t, half = divmod(b, 2)
                        dve.wait_ge(passes, 4 * N_IN + 8 * (N_OUT - 1) + b + 1)
                        xs = X[:, t, half * 512:(half + 1) * 512]
                        V.tensor_tensor(xs, xs, ps[:, b, :], ALU.add).then_inc(x_added, 1)

                    dve.wait_ge(e_sq, TT)
                    V.tensor_scalar(st2[:, 0:4], ssX[:, :], 1.0 / D, EPS, ALU.mult, ALU.add).then_inc(e_var, 1)
                    dve.wait_ge(e_in, 64)
                    dve.wait_ge(e_std, 1)
                    step(V.reciprocal(st2[:, 4:8], st2[:, 4:8]))

                    def low_part(t):
                        dve.wait_ge(e_hi, t + 1)
                        V.tensor_tensor(EL[:, t, :], hw[:, t % 2, :], EH[:, t, :], ALU.subtract).then_inc(e_lo, 1)
                    for t in range(TT):
                        if t >= 2:
                            dve.wait_ge(hT2_done, 2 * (t - 1))
                            dve.wait_ge(e_lo, t - 1)
                        V.scalar_tensor_tensor(hw[:, t % 2, :], X[:, t, :], st2[:, 4 + t:5 + t], norm2_row[:, :], ALU.mult, ALU.mult).then_inc(h_done, 1)
                        if t:
                            low_part(t - 1)
                    low_part(TT - 1)
                    dve.wait_ge(logit_done, 1)
                    V.tensor_copy(work[:, :], ps[0:NE, 4, :]).then_inc(logit_rows, 1)
                    dve.wait_ge(logit_T, 1)
                    lg = ps[:, 7, 0:TT * NE].rearrange("p (a b) -> p a b", b=NE)
                    step(V.reduce_max(st2[:, 8:12], lg, axis=AX))
                    V.tensor_tensor(aff[:, :, :], lg, bc(st2[:, 8:12], 2, [P, TT, NE]), ALU.subtract).then_inc(logit_max, 1)
                    V.tensor_scalar(selT[:, :], iota[:, :], -1.0, None, ALU.is_equal).then_inc(selT_done, 1)
                    for half in range(2):
                        last = V.tensor_scalar(YE[:, half * 512:(half + 1) * 512], iota[:, :], -1.0, None, ALU.is_equal)
                    last.then_inc(ye_done, 1)
                    dve.wait_ge(logit_exp, 1)
                    step(V.reduce_sum(st2[:, 12:16], aff[:, :, :], axis=AX))
                    step(V.reciprocal(st2[:, 12:16], st2[:, 12:16]))
                    V.tensor_tensor(aff[:, :, :], aff[:, :, :], bc(st2[:, 12:16], 2, [P, TT, NE]), ALU.mult).then_inc(aff_done, 1)
                    dve.wait_ge(affT_done, 1)
                    step(V.tensor_copy(work[:, :], ps[0:NE, 5, :]))
                    for r in range(CAP // 8):
                        b = slice(8 * r, 8 * r + 8)
                        step(V.max(best[:, b], work[:, :]))
                        step(V.max_index(best_at[:, b], best[:, b], work[:, :]))
                        if r < CAP // 8 - 1:
                            step(V.match_replace(work[:, :], best[:, b], work[:, :], -1.0))
                    step(V.tensor_copy(twice[:, 0, 0, :], best_at[:, :]))
                    V.tensor_copy(twice[:, 0, 1, :], twice[:, 0, 0, :])
                    V.tensor_copy(twice[:, 1, :, :], bc(best[:, :], 1, [NE, 2, CAP])).then_inc(chosen, 1)
                    V.tensor_tensor(spread[:, :, :], bc(twice[:, 0, 0, :], 1, [NE, NE, CAP]), bc(ident[0:NE, 0:NE], 2, [NE, NE, CAP]), ALU.mult).then_inc(spread_done, 1)
                    dve.wait_ge(chosen_T, 1)
                    pair = ps[:, 6, 0:NE].rearrange("p (g e) -> p g e", e=2)
                    V.tensor_copy(slot_tok[0:CAP, :], pair[0:CAP, :, 0])
                    V.tensor_copy(slot_tok[CAP:P, :], pair[CAP:P, :, 1])
                    V.tensor_copy(slot_gate[:, :], ps[:, 6, NE:2 * NE])
                    dve.wait_ge(rows_done, 1)
                    V.tensor_copy(gate_now[:, :], ps[:, 6, NE:NE + 2])
                    V.tensor_copy(idx_rows[:, 0:512], ps[:, 4, :]).then_inc(top_ready, 1)
                    dve.wait_ge(top_ready, 1)

                    def choose(columns):
                        for t in range(TT):
                            last = V.tensor_scalar(sel[:, t, :], idx_rows[:, columns], tokid[:, t:t + 1], None, ALU.is_equal)
                        last.then_inc(sel_done, 1)
                    choose(slice(0, 2 * CAP))
                    dve.wait_ge(rows_done, 2)
                    V.tensor_copy(idx_rows[:, NE * CAP:], ps[:, 4, 0:2 * CAP])
                    V.tensor_copy(idx_rows[:, 512:NE * CAP], ps[:, 5, :]).then_inc(top_ready, 1)

                    def to_tokens(g, ns):
                        for n in ns:
                            t, half = divmod(n, 2)
                            dve.wait_ge(scattered, g * 8 + (n + 1))
                            xs = X[:, t, half * 512:(half + 1) * 512]
                            V.tensor_tensor(xs, xs, ps[:, 4 + n % 4, :], ALU.add).then_inc(x_added, 1)
                    with dve.Fori(0, PAIRS) as g:
                        def hidden(n):
                            dve.wait_ge(sg_done, g * 2 + (n + 1))
                            dve.wait_ge(folded, g * 4 + (2 * n + 2))
                            V.tensor_tensor(HM[:, :, :], SG[:, :, :], ps[:, 5, :].rearrange("p (a b) -> p a b", b=CAP), ALU.mult).then_inc(hm_done, 1)

                        def hidden_lo(n):
                            dve.wait_ge(hp_hi, g * 2 + (n + 1))
                            V.tensor_tensor(HP[:, :, CAP:P], HM[:, :, :], HP[:, :, 0:CAP], ALU.subtract).then_inc(hp_lo, 1)

                        def output(n):
                            dve.wait_ge(yt_done, g * 2 + (2 - n))
                            V.scalar_tensor_tensor(YE[n * CAP:(n + 1) * CAP, :], ps[0:CAP, 6:8, :].rearrange("p a b -> p (a b)"),
                                                   gate_now[0:CAP, n:n + 1], YT[:, :], ALU.mult, ALU.add).then_inc(ye_done, 1)

                        def next_choice():
                            dve.wait_ge(top_ready, 2)
                            dve.wait_ge(gathered, g * 2 + 2)
                            choose(bass.ds(g * P + P, P))

                        def tokens_of_slots():
                            V.tensor_scalar(selT[:, :], iota[:, :], slot_tok[:, bass.ds(g, 1)], None, ALU.is_equal).then_inc(selT_done, 1)
                        def last_pair():
                            output(1)
                            dve.wait_ge(ye_done, g * 2 + 2)
                            V.tensor_copy(gate_now[:, :], slot_gate[:, bass.ds(g * 2, 2)])
                        for q in range(TURN):
                            if not by_pool(q):
                                expert_rests(dve, g, q)
                            if q == 1:
                                last_pair()
                            elif q == 5:
                                to_tokens(g, (0, 1))
                            elif q == 6:
                                to_tokens(g, (2, 3))
                            elif q == 7:
                                next_choice()
                            elif q == 9:
                                to_tokens(g, (4, 5))
                            elif q == 10:
                                to_tokens(g, (6, 7))
                                tokens_of_slots()
                            elif q == 13:
                                hidden(0)
                                hidden_lo(0)
                            elif q == 18:
                                output(0)
                            elif q == 22:
                                hidden(1)
                                hidden_lo(1)
                    dve.wait_ge(yt_done, PAIRS * 2 + 1)
                    V.scalar_tensor_tensor(YE[CAP:P, :], ps[0:CAP, 6:8, :].rearrange("p a b -> p (a b)"),
                                           gate_now[0:CAP, 1:2], YT[:, :], ALU.mult, ALU.add).then_inc(ye_done, 1)
                    to_tokens(PAIRS, range(8))

                @block.gpsimd
                def _(pool):
                    G = nc.gpsimd
                    chained = [0]

                    def step(ins):
                        chained[0] += 1
                        ins.then_inc(p_chain, 1)
                        pool.wait_ge(p_chain, chained[0])
                    G.memset(XP[:, :, 0:2], 0.0)
                    G.memset(XP[:, :, SEQ + 2:SEQ + 4], 0.0).then_inc(pad_set, 1)
                    pool.wait_ge(par_in, 32)
                    at = 0
                    for j, heads in enumerate((4, 2, 4, 2)):
                        last = G.tensor_copy(GN[:, at:at + heads, :], bc(gains[:, j, :], 1, [P, heads, HD]))
                        at += heads
                    last.then_inc(gain_set, 1)
                    pool.wait_ge(proj_evac, 3 * TT)
                    for t in range(TT):
                        if t >= 2:
                            pool.wait_ge(r_ss, t - 1)
                        G.tensor_tensor(squares(t).rearrange("p (s a b) -> p s a b", s=2, b=HD), qk(t), qk(t), ALU.mult).then_inc(r_sq, 1)
                    pool.wait_ge(r_scale, 1)
                    pool.wait_ge(gain_set, 1)
                    pool.wait_ge(const_in, 5 * 16)
                    for t in range(TT):
                        step(G.tensor_tensor(qk(t), qk(t), bc(rsR[:, t, :].rearrange("p (s a) -> p s a", s=2), 3, [P, 2, 6, HD]), ALU.mult))
                        step(G.tensor_tensor(qk(t), qk(t), GN[:, :, :].rearrange("p (s a) b -> p s a b", s=2), ALU.mult))
                        if t > 0:
                            pool.wait_ge(rope_done, t)
                        q = PR[:, t, AT0:AT0 + 1024].rearrange("p (s c) -> p s c", s=2)
                        for s in range(2):
                            src = q[:, s, 0:VOFF].rearrange("p (a b) -> p a b", b=HD)
                            c_ = rotary(0, s).rearrange("p (a b) -> p a b", b=HD)
                            G.tensor_tensor(c_, src, bc(cosT[:, s, t, :], 1, [P, 6, HD]), ALU.mult)
                            w = HD // 2 if s == 0 else HD // 4
                            m = HD // (2 * w)
                            srcv = q[:, s, 0:VOFF].rearrange("p (a m z w) -> p a m z w", m=m, z=2, w=w)
                            dstv = rotary(1, s).rearrange("p (a m z w) -> p a m z w", m=m, z=2, w=w)
                            sinv = sinT[:, s, t, :].rearrange("p (m z w) -> p m z w", z=2, w=w)
                            for z in range(2):
                                a, b, c = dstv[:, :, :, z, :], srcv[:, :, :, 1 - z, :], sinv[:, :, z, :]
                                last = G.tensor_tensor(a, b, bc(c, 1, [P, 6, m, w]), ALU.mult)
                        step(last)
                        for s in range(2):
                            c_, r_, o_ = (v.rearrange("p (a b) -> p a b", b=HD) for v in (rotary(0, s), rotary(1, s), q[:, s, 0:VOFF]))
                            G.tensor_tensor(o_[:, 0:4, :].rearrange("p (j i) b -> p i j b", j=2),
                                            c_[:, 0:4, :].rearrange("p (i j) b -> p i j b", i=2),
                                            r_[:, 0:4, :].rearrange("p (i j) b -> p i j b", i=2), ALU.add)
                            last = G.tensor_tensor(o_[:, 4:6, :], c_[:, 4:6, :], r_[:, 4:6, :], ALU.add)
                        last.then_inc(rope_done, 1)
                    pool.wait_ge(tok_T, 12)
                    G.memset(S[:, :, :, :], 0.0).then_inc(s_zero, 1)
                    pool.wait_ge(s_zero, 1)
                    pool.wait_ge(const_in, 5 * 16)
                    pool.wait_ge(g_ready, 1)
                    pool.wait_ge(proj_evac, 4 * GROUPS)

                    def decays(t, d):
                        if t > 0:
                            pool.wait_ge(row_done, 2 * t + d - 1)
                        G.tensor_tensor(spare[d]["GU"][:, :, :], bc(cum[:, d, :], 1, [P, HA, P]),
                                        bc(gdec[:, tile_of(d, t), d * HA:(d + 1) * HA], 2, [P, HA, P]), ALU.mult).then_inc(gu_ready, 1)

                    def masks(t, d):
                        i = 2 * t + d
                        DM = delta[d]["DM"][:, :, :]
                        pool.wait_ge(dm_exp, i + 1)
                        G.tensor_tensor(DM, DM, bc(cum[:, d, :], 1, [P, HA, P]), ALU.mult).then_inc(masked, 1)
                        pool.wait_ge(masked, i + 1)
                        if t > 1:
                            pool.wait_ge(nm_done, (7 * (t - 2) + 6) * 2 + d + 1)
                        G.tensor_tensor(buf("NT", d, t), DM, bc(beta[:, tile_of(d, t), d * HA:(d + 1) * HA], 2, [P, HA, P]), ALU.mult).then_inc(nt_base, 1)

                    def level_part(t, l, d):
                        i = 2 * t + d
                        if l == 0:
                            pool.wait_ge(nt_done, i + 1)
                            if t > 0:
                                pool.wait_ge(x_done, 12 * t + d - 1)
                        elif l == 1:
                            pool.wait_ge(t0_done, i + 1)
                        else:
                            pool.wait_ge(x_done, (6 * t + l - 2) * 2 + d + 1)
                        G.tensor_tensor(delta[d]["NM"][:, :, :], buf("NT", d, t), bc(level[:, l, :], 1, [P, HA, P]), ALU.mult).then_inc(nm_done, 1)

                    def state_decayed(t, d):
                        i = 2 * t + d
                        pool.wait_ge(o_done, i + 1)
                        if t > 0:
                            pool.wait_ge(s_new, i - 1)
                        G.tensor_tensor(S[:, d, :, :], S[:, d, :, :], bc(egl[:, d, tile_of(d, t), :], 2, [P, HA, P]), ALU.mult).then_inc(s_dec, 1)

                    def k_decayed(t, d):
                        i = 2 * t + d
                        tl = tile_of(d, t)
                        B = delta[d]
                        pool.wait_ge(cum_exp, 1)
                        pool.wait_ge(qk_normed, 8)
                        if t > 0:
                            pool.wait_ge(w_done, i - 1)
                            pool.wait_ge(s_done, i - 1)
                        G.tensor_tensor(B["KG"][:, :, :], KN[:, tl, :, :], bc(egc[:, d, tl, :], 2, [P, HA, P]), ALU.mult).then_inc(kgd_done, 1)
                        G.tensor_tensor(B["KD"][:, :, :], KN[:, tl, :, :], bc(kdc[:, d, tl, :], 2, [P, HA, P]), ALU.mult).then_inc(kgd_done, 1)
                    for stage in (decays, masks):
                        for d in range(2):
                            stage(0, d)
                    for d in range(2):
                        level_part(0, 0, d)
                    for t in range(TT):
                        for l in range(1, 7):
                            if t < TT - 1 and l in (4, 5):
                                masks(t + 1, l - 4)
                            for d in range(2):
                                level_part(t, l, d)
                            if l == 1:
                                for d in range(2):
                                    if t > 0:
                                        state_decayed(t - 1, d)
                                for d in range(2):
                                    if t < TT - 1:
                                        decays(t + 1, d)
                                for d in range(2):
                                    k_decayed(t, d)
                        if t < TT - 1:
                            for d in range(2):
                                level_part(t + 1, 0, d)
                    pool.wait_ge(x_added, 8)
                    G.tensor_tensor(fold[:, :], ident[:, 0:CAP], ident[:, CAP:P], ALU.add).then_inc(fold_set, 1)
                    with pool.Fori(0, PAIRS) as g:
                        for q in range(TURN):
                            if by_pool(q):
                                expert_rests(pool, g, q)
            nc.all_engine_barrier(sems_to_clear=range(raw_full[0].num, slot_free.num + 1))
        with nc.Block() as block:
            @block.sync
            def _(sp):
                sp.dma_start(out.rearrange("o (t p) d -> p (o t) d", p=P), X[:, :, :]).then_inc(s_out, 16)
                sp.wait_ge(s_out, 16)


_INS = ["x", "rows", "cols", "norm2", "w_in", "w_out", "w_router", "w_gate", "w_up", "w_down", "consts"]
_OUTS = [((1, SEQ, D), "float32")]


def kernel(**inputs):
    import numpy as _np
    import concourse.bacc as _bacc
    from concourse import mybir as _mybir
    from concourse.bass_utils import run_bass_kernel_spmd as _run

    i = {k: _np.asarray(v) for k, v in inputs.items()}
    laid = {k: i[k] for k in ("x", "w_in", "w_out", "w_router", "w_gate", "w_up", "w_down")}
    laid["rows"] = _np.concatenate([i["a_log"].reshape(LAYERS, -1), i["dt_bias"].reshape(LAYERS, -1), i["a_norm_g"],
                                    i["b_qnorm_g"], i["b_knorm_g"], i["c_qnorm_g"], i["c_knorm_g"], i["b_sink"]], 1)
    laid["cols"] = _np.concatenate([i["norm1_g"].reshape(LAYERS, KD, P).transpose(0, 2, 1),
                                    i["conv_w"].reshape(LAYERS, 5, NQKV, P).transpose(0, 3, 2, 1).reshape(LAYERS, P, -1)], 2)
    laid["norm2"] = i["norm2_g"]
    laid["consts"] = constants()
    nc = _bacc.Bacc("TRN2", target_bir_lowering=False, num_devices=1)
    arrays, args = {}, []
    for name in _INS:
        a = _np.ascontiguousarray(laid[name])
        arrays[f"in_{name}_dram"] = a
        args.append(nc.dram_tensor(f"in_{name}_dram", a.shape, _mybir.dt.from_np(a.dtype), kind="ExternalInput").ap())
    for n, (shape, dtype) in enumerate(_OUTS):
        args.append(nc.dram_tensor(f"out_{n}_dram", shape, _mybir.dt.from_np(_np.dtype(dtype)), kind="ExternalOutput").ap())
    bass_hybrid_encoder(nc, *args)
    r = _run(nc, [arrays], core_ids=[0])
    return r.results[0]["out_0_dram"]
```
